# Optimizing a Trainium2 kernel written in Bass

```python
import jax
import jax.numpy as jnp
from jax import lax
import numpy as np

D_MODEL = 1024
BATCH = 1
SEQ = 512
DEPTH = 1
DEC_BATCH = 8
DEC_SEQ = 8
PAST_LEN = 4096
PAGE_SIZE = 128

H_M = 4
DH_M = D_MODEL // (2 * H_M)
W_M = H_M * DH_M
H_F = 8
DH_F = D_MODEL // (2 * H_F)
W_F = H_F * DH_F
D_MIX = W_M + W_F
N_IN = 4 * W_M + 2 * H_M + 3 * W_F + H_F
D_FF = -(-8 * D_MODEL // (3 * 256)) * 256
CHUNK = 128
Q_BLOCK = 128
FOX_F_BIAS = 4.0
EPS = 1e-6

kernel_name = 'hymba_mlstm_fox_decode_step'

def _rmsnorm(x, g):
    x32 = x.astype(jnp.float32)
    y = x32 * lax.rsqrt(jnp.mean(x32 * x32, axis=-1, keepdims=True) + EPS)
    return (y * g.astype(jnp.float32)).astype(x.dtype)

def _project(x, g, w_in, b_mi, b_mf, b_ff):
    B, L = x.shape[0], x.shape[1]
    h = _rmsnorm(x, g)
    proj = jnp.matmul(h, w_in).astype(jnp.float32)
    sizes = (W_M, W_M, W_M, W_M, H_M, H_M, W_F, W_F, W_F, H_F)
    cuts = [int(c) for c in np.cumsum(sizes)[:-1]]
    q_m, k_m, v_m, o_m, i_m, f_m, q_f, k_f, v_f, f_f = jnp.split(proj, cuts, axis=-1)
    mh = lambda a: a.reshape(B, L, H_M, DH_M)
    fh = lambda a: a.reshape(B, L, H_F, DH_F)
    mlstm = (mh(q_m), mh(k_m) * (DH_M ** -0.5), mh(v_m),
             i_m + b_mi.astype(jnp.float32),
             jax.nn.log_sigmoid(f_m + b_mf.astype(jnp.float32)))
    fox = (fh(q_f) * (DH_F ** -0.5), fh(k_f), fh(v_f),
           jax.nn.log_sigmoid(f_f + b_ff.astype(jnp.float32)))
    return mlstm, o_m, fox

def _mlstm_chunk(state, inp):
    C, n, m = state
    q, k, v, logi, logf = inp
    L = q.shape[1]
    b = jnp.swapaxes(jnp.cumsum(logf, axis=1), 1, 2)
    li = jnp.swapaxes(logi, 1, 2)
    causal = jnp.tril(jnp.ones((L, L), dtype=bool))
    D = jnp.where(causal, b[..., :, None] - b[..., None, :] + li[..., None, :], -jnp.inf)
    inter = m[..., None] + b
    m_t = jnp.maximum(inter, jnp.max(D, axis=-1))
    S = jnp.einsum('bthd,bshd->bhts', q, k) * jnp.exp(D - m_t[..., None])
    w_inter = jnp.exp(inter - m_t)
    num = w_inter[..., None] * jnp.einsum('bhvk,bthk->bhtv', C, q) + jnp.einsum('bhts,bshv->bhtv', S, v)
    den = w_inter * jnp.einsum('bhk,bthk->bht', n, q) + jnp.sum(S, axis=-1)
    h = num / jnp.maximum(jnp.abs(den), jnp.exp(-m_t))[..., None]
    b_last = b[..., -1]
    m_new = m_t[..., -1]
    decay = jnp.exp(m + b_last - m_new)
    w_s = jnp.swapaxes(jnp.exp(li + b_last[..., None] - b - m_new[..., None]), 1, 2)
    C_new = decay[..., None, None] * C + jnp.einsum('bshv,bshk->bhvk', v * w_s[..., None], k)
    n_new = decay[..., None] * n + jnp.einsum('bsh,bshk->bhk', w_s, k)
    return (C_new, n_new, m_new), jnp.transpose(h, (0, 2, 1, 3))

def _mlstm_prompt(q, k, v, logi, logf):
    B, S = q.shape[0], q.shape[1]
    n_chunks = S // CHUNK
    to_chunks = lambda a: jnp.swapaxes(a.reshape((B, n_chunks, CHUNK) + a.shape[2:]), 0, 1)
    state0 = (jnp.zeros((B, H_M, DH_M, DH_M), jnp.float32),
              jnp.zeros((B, H_M, DH_M), jnp.float32),
              jnp.zeros((B, H_M), jnp.float32))
    state, h = lax.scan(_mlstm_chunk, state0,
                        (to_chunks(q), to_chunks(k), to_chunks(v), to_chunks(logi), to_chunks(logf)))
    return jnp.swapaxes(h, 0, 1).reshape(B, S, H_M, DH_M), state

def _fox_logits(q, cq, qpos, k, ck, kpos):
    s = jnp.einsum('bqhd,bkhd->bhqk', q, k)
    bias = jnp.swapaxes(cq, 1, 2)[..., :, None] - jnp.swapaxes(ck, 1, 2)[..., None, :]
    mask = kpos[None, :] <= qpos[:, None]
    return jnp.where(mask, s + bias, -jnp.inf)

def _fox_prompt(q, k, v, logf):
    B, S = q.shape[0], q.shape[1]
    nb = S // Q_BLOCK
    c = jnp.cumsum(logf, axis=1)
    pos = jnp.arange(S)
    qb = jnp.swapaxes(q.reshape(B, nb, Q_BLOCK, H_F, DH_F), 0, 1)
    cb = jnp.swapaxes(c.reshape(B, nb, Q_BLOCK, H_F), 0, 1)
    pb = pos.reshape(nb, Q_BLOCK)

    def block(args):
        q_i, c_i, p_i = args
        p = jax.nn.softmax(_fox_logits(q_i, c_i, p_i, k, c, pos), axis=-1)
        return jnp.einsum('bhqk,bkhd->bqhd', p, v)

    o = lax.map(block, (qb, cb, pb))
    return jnp.swapaxes(o, 0, 1).reshape(B, S, H_F, DH_F)

def _fox_sample(q, k, v, logf, k_pool, v_pool, logf_pool, page_table):
    B, T = q.shape[0], q.shape[1]
    P = page_table.shape[1] * PAGE_SIZE
    k_past = k_pool[page_table].reshape(B, P, H_F, DH_F).astype(jnp.float32)
    v_past = v_pool[page_table].reshape(B, P, H_F, DH_F).astype(jnp.float32)
    lf_past = logf_pool[page_table].reshape(B, P, H_F).astype(jnp.float32)
    c_past = lf_past - lax.cumsum(lf_past, axis=1, reverse=True)
    c_new = jnp.cumsum(logf, axis=1)
    pos_past = jnp.arange(P)
    pos_new = P + jnp.arange(T)
    s = jnp.concatenate([_fox_logits(q, c_new, pos_new, k_past, c_past, pos_past),
                         _fox_logits(q, c_new, pos_new, k, c_new, pos_new)], axis=-1)
    p = jax.nn.softmax(s, axis=-1)
    return (jnp.einsum('bhqk,bkhd->bqhd', p[..., :P], v_past)
            + jnp.einsum('bhqk,bkhd->bqhd', p[..., P:], v))

def _merge_ffn(x, h_m, o_m, h_f, head_g, w_out, g_ffn, w_gate, w_up, w_down):
    B, L = x.shape[0], x.shape[1]
    hm = h_m * lax.rsqrt(jnp.mean(h_m * h_m, axis=-1, keepdims=True) + EPS)
    hm = hm * head_g.astype(jnp.float32).reshape(H_M, DH_M)
    hm = hm.reshape(B, L, W_M) * jax.nn.sigmoid(o_m)
    mix = jnp.concatenate([hm, h_f.reshape(B, L, W_F)], axis=-1).astype(x.dtype)
    x = x + jnp.matmul(mix, w_out)
    h = _rmsnorm(x, g_ffn)
    return x + jnp.matmul(jax.nn.silu(jnp.matmul(h, w_gate)) * jnp.matmul(h, w_up), w_down)

def setup_inputs(seed: int = 0) -> dict:
    key = jax.random.key(seed)
    ks = jax.random.split(key, 24)
    n_pages = PAST_LEN // PAGE_SIZE
    n_pool = (DEC_BATCH * n_pages * 5) // 4
    nrm = lambda kk, shape, s=1.0: s * jax.random.normal(kk, shape, jnp.float32)
    return {
        'x_prompt': nrm(ks[0], (BATCH, SEQ, D_MODEL)),
        'x_sample': nrm(ks[1], (DEC_BATCH, DEC_SEQ, D_MODEL)),
        'cache_fox_k': nrm(ks[2], (DEPTH, n_pool, PAGE_SIZE, H_F, DH_F)),
        'cache_fox_v': nrm(ks[3], (DEPTH, n_pool, PAGE_SIZE, H_F, DH_F)),
        'cache_fox_logf': jax.nn.log_sigmoid(nrm(ks[4], (DEPTH, n_pool, PAGE_SIZE, H_F)) + FOX_F_BIAS),
        'page_table': jax.random.permutation(ks[5], n_pool)[: DEC_BATCH * n_pages].reshape(DEC_BATCH, n_pages).astype(jnp.int32),
        'state_mlstm_C': nrm(ks[6], (DEPTH, DEC_BATCH, H_M, DH_M, DH_M), 0.5),
        'state_mlstm_n': nrm(ks[7], (DEPTH, DEC_BATCH, H_M, DH_M), 0.5),
        'state_mlstm_m': nrm(ks[8], (DEPTH, DEC_BATCH, H_M)),
        'norm_mix_g': 1.0 + nrm(ks[9], (DEPTH, D_MODEL), 0.01),
        'w_in': nrm(ks[10], (DEPTH, D_MODEL, N_IN), D_MODEL ** -0.5),
        'b_m_igate': nrm(ks[11], (DEPTH, H_M), 0.1),
        'b_m_fgate': jnp.linspace(3.0, 6.0, H_M)[None, :] + nrm(ks[12], (DEPTH, H_M), 0.1),
        'b_f_fgate': FOX_F_BIAS + nrm(ks[13], (DEPTH, H_F), 0.1),
        'mlstm_head_g': 1.0 + nrm(ks[14], (DEPTH, W_M), 0.01),
        'w_out': nrm(ks[15], (DEPTH, D_MIX, D_MODEL), D_MIX ** -0.5),
        'norm_ffn_g': 1.0 + nrm(ks[16], (DEPTH, D_MODEL), 0.01),
        'w_gate': nrm(ks[17], (DEPTH, D_MODEL, D_FF), D_MODEL ** -0.5),
        'w_up': nrm(ks[18], (DEPTH, D_MODEL, D_FF), D_MODEL ** -0.5),
        'w_down': nrm(ks[19], (DEPTH, D_FF, D_MODEL), D_FF ** -0.5),
        'norm_final_g': 1.0 + nrm(ks[20], (D_MODEL,), 0.01),
    }

def reference(x_prompt, x_sample, cache_fox_k, cache_fox_v, cache_fox_logf, page_table,
              state_mlstm_C, state_mlstm_n, state_mlstm_m, norm_mix_g, w_in, b_m_igate, b_m_fgate,
              b_f_fgate, mlstm_head_g, w_out, norm_ffn_g, w_gate, w_up, w_down, norm_final_g):
    xp, xs = x_prompt, x_sample
    pk, pv, plf, pC, pn, pm = [], [], [], [], [], []
    sk, sv, slf, sC, sn, sm = [], [], [], [], [], []
    for l in range(DEPTH):
        (q, k, v, li, lf), o_m, (qf, kf, vf, lff) = _project(
            xp, norm_mix_g[l], w_in[l], b_m_igate[l], b_m_fgate[l], b_f_fgate[l])
        h_m, (C, n, m) = _mlstm_prompt(q, k, v, li, lf)
        h_f = _fox_prompt(qf, kf, vf, lff)
        xp = _merge_ffn(xp, h_m, o_m, h_f, mlstm_head_g[l], w_out[l], norm_ffn_g[l],
                        w_gate[l], w_up[l], w_down[l])
        pk.append(kf); pv.append(vf); plf.append(lff); pC.append(C); pn.append(n); pm.append(m)
        (q, k, v, li, lf), o_m, (qf, kf, vf, lff) = _project(
            xs, norm_mix_g[l], w_in[l], b_m_igate[l], b_m_fgate[l], b_f_fgate[l])
        state = (state_mlstm_C[l].astype(jnp.float32), state_mlstm_n[l].astype(jnp.float32),
                 state_mlstm_m[l].astype(jnp.float32))
        (C, n, m), h_m = _mlstm_chunk(state, (q, k, v, li, lf))
        h_f = _fox_sample(qf, kf, vf, lff, cache_fox_k[l], cache_fox_v[l], cache_fox_logf[l], page_table)
        xs = _merge_ffn(xs, h_m, o_m, h_f, mlstm_head_g[l], w_out[l], norm_ffn_g[l],
                        w_gate[l], w_up[l], w_down[l])
        sk.append(kf); sv.append(vf); slf.append(lff); sC.append(C); sn.append(n); sm.append(m)
    y_prompt = _rmsnorm(xp, norm_final_g)
    y_sample = _rmsnorm(xs, norm_final_g)
    st = lambda a, ref: jnp.stack(a, axis=0).astype(ref.dtype)
    return (y_prompt, y_sample,
            st(pk, cache_fox_k), st(pv, cache_fox_v), st(plf, cache_fox_logf),
            st(pC, state_mlstm_C), st(pn, state_mlstm_n), st(pm, state_mlstm_m),
            st(sk, cache_fox_k), st(sv, cache_fox_v), st(slf, cache_fox_logf),
            st(sC, state_mlstm_C), st(sn, state_mlstm_n), st(sm, state_mlstm_m))


_drawn_inputs = setup_inputs


def setup_inputs(seed=0):
    import zlib

    import numpy as np

    out = dict(_drawn_inputs(seed))
    spreads = {}
    factors = {'cache_fox_logf': 3.644,
     'norm_mix_g': 2.931,
     'mlstm_head_g': 8.0,
     'norm_ffn_g': 8.0,
     'norm_final_g': 5.872}
    for name, (base, spread) in spreads.items():
        noise = np.random.default_rng([zlib.crc32(name.encode()), seed]).standard_normal(out[name].shape)
        drawn = base * np.exp(spread * noise) if base else spread * noise
        out[name] = jnp.asarray(drawn.astype(out[name].dtype))
    for name, factor in factors.items():
        out[name] = (out[name] * factor).astype(out[name].dtype)
    return out
```

```python
from contextlib import ExitStack

import numpy as np

import concourse.bass as bass
from concourse import mybir

F32 = mybir.dt.float32
I32 = mybir.dt.int32
ALU = mybir.AluOpType
ACT = mybir.ActivationFunctionType
AX = mybir.AxisListType

P = 128
D = 1024
KT = D // P
SEQ, DB, DS = 512, 8, 8
NS = DB * DS
T = SEQ + NS
TH = T // 2
ST = SEQ // P
HM, DM = 4, 128
HF, DF = 8, 64
NJ = HF // 2
DFF = 2816
FT = DFF // P
PAGES, PAGE = 32, 128
PC = 4
NCH = PAGES // PC
CH = NCH + 1
PAST = PAGES * PAGE
EPS = 1e-6
NEG = -1e30
ROWS_F, ROWS_FF = 32, 64
GR = ROWS_FF + HF

QM, KM, VM, OM, QF, KF, VF = 0, 4, 8, 12, 16, 20, 24
NT_IN = 28
UNIT_W = 2 * P
WSLOT = FT * P
U_IN, U_OUT, U_GU, U_DN = NT_IN // 2, KT // 2, FT, KT
U0_OUT, U0_GU, U0_DN = U_IN, U_IN + U_OUT, U_IN + U_OUT + U_GU
T0_OUT, T0_GU, T0_DN = NT_IN, NT_IN + KT, NT_IN + KT + 2 * FT
WIN = KT * UNIT_W
PT_AT = 8192
ARENA = PT_AT + NT_IN * T + 3 * (ST + 1) * 512 + HM * DB * DM
OUT_EARLY = 7


def constants():
    s, t = np.arange(P)[:, None], np.arange(P)[None, :]
    causal_t = np.where(s <= t, 0.0, NEG)
    causal_n = np.where(t <= s, 0.0, NEG)
    s6, t6 = np.arange(NS)[:, None], np.arange(NS)[None, :]
    causal_s = np.full((P, NS), NEG)
    causal_s[:NS] = np.where((s6 <= t6) & (s6 // DS == t6 // DS), 0.0, NEG)
    block = np.zeros((P, DB))
    block[:NS] = s6 // DS == np.arange(DB)[None, :]
    new_mask = np.full((P, DB, NS), NEG)
    for b in range(DB):
        for q in range(DS):
            for h in range(HF):
                new_mask[h * DS + q, b, b * DS:b * DS + q + 1] = 0.0
    suffix = (s >= t) & (s // PAGES == t // PAGES)
    wide = np.concatenate([np.eye(P), causal_t, causal_n, causal_s, block, new_mask.reshape(P, -1),
                           suffix, np.ones((P, P))], axis=1).astype(np.float32)
    sel4 = np.zeros((HM, HM, P))
    sel4[np.arange(HM), np.arange(HM)] = 1.0
    sel8 = np.zeros((HF, HF, P))
    sel8[np.arange(HF), np.arange(HF)] = 1.0
    selq = np.repeat(np.eye(HF), DS, axis=1)
    reset = np.ones(T)
    reset[0] = 0.0
    reset[SEQ::DS] = 0.0
    rows = np.zeros((HF, HM * P + HF * P + NS + 2 * T))
    rows[:HM, :HM * P] = sel4.reshape(HM, -1)
    rows[:, HM * P:HM * P + HF * P] = sel8.reshape(HF, -1)
    rows[:, HM * P + HF * P:HM * P + HF * P + NS] = selq
    rows[:, HM * P + HF * P + NS:HM * P + HF * P + NS + T] = reset
    rows[:, HM * P + HF * P + NS + T:] = (1.0 - reset) * NEG
    return wide, rows.astype(np.float32)


WIDE_COLS = 3 * P + NS + DB + DB * NS + 2 * P
ROW_COLS = HM * P + HF * P + NS + 2 * T


def build(nc, A):
    ctx = ExitStack()
    with ctx:
        def sb(name, shape, dt=F32):
            return ctx.enter_context(nc.sbuf_tensor(name, shape, dt))

        def sem(name):
            return ctx.enter_context(nc.semaphore(name))

        PS = ctx.enter_context(nc.psum_tensor("PS", [P, 8, 512], F32))

        hT = sb("hT", [P, KT, T])
        wide = sb("wide", [P, WIDE_COLS])
        rowc = sb("rowc", [HF, ROW_COLS])
        gains = sb("gains", [P, 3 * KT + HM])
        epsc = sb("epsc", [P, 1])
        o = 0
        ident = wide[:, o:o + P]; o += P
        causal_t = wide[:, o:o + P]; o += P
        causal_n = wide[:, o:o + P]; o += P
        causal_s = wide[:, o:o + NS]; o += NS
        block_of = wide[:, o:o + DB]; o += DB
        new_mask = wide[:, o:o + DB * NS].rearrange("p (b k) -> p b k", b=DB); o += DB * NS
        suffix = wide[:, o:o + P]; o += P
        ones = wide[:, o:o + P]
        o = 0
        sel4 = rowc[0:HM, o:o + HM * P]; o += HM * P
        sel8 = rowc[:, o:o + HF * P]; o += HF * P
        selq = rowc[:, o:o + NS]; o += NS
        keep = rowc[:, o:o + T]; o += T
        drop = rowc[:, o:o + T]

        qbd = sb("qbd", [P, NJ, NS])
        kf_new = sb("kf_new", [P, NJ, NS])
        qf_new = sb("qf_new", [P, NJ, NS])
        vf_new = sb("vf_new", [NS, HF * DF])
        bias_new = sb("bias_new", [NS, DB, NS])
        ptab = sb("ptab", [1, DB * PAGES], I32)
        pidx = sb("pidx", [P, 2], I32)
        pgs = sb("pgs", [P, 2, HF])
        gbias = sb("gbias", [GR, 1])
        wg = sb("wg", [P, KT, GR])
        m_top = sb("m_top", [HM, T])
        emt = sb("emt", [HM, T])
        winter = sb("winter", [HM, NS])
        ca = sb("ca", [ROWS_F + HM, T])
        cat = sb("cat", [P, ST + 1, ROWS_F + HM])
        lff = sb("lff", [HF, T])
        ncf = sb("ncf", [HF, T])
        mst = sb("mst", [HM, DB])
        dec = sb("dec", [HM, DB])
        nml = sb("nml", [HM, 1])
        mout = sb("mout", [HM, 1 + DB])
        decb = sb("decb", [P, HM, DB])
        nst = sb("nst", [P, HM, DB])
        nnew = sb("nnew", [P, HM, DB])
        ctp = sb("ctp", [P, HM, DM + 1])
        smx = sb("smx", [NS, CH])
        snm = sb("snm", [NS, 2])
        ssum = sb("ssum", [NS, CH])
        sri = sb("sri", [NS, 2])
        ptile = sb("ptile", [P, 3, PC * NS])
        osb = sb("osb", [NS, HF * DF])
        fmx = sb("fmx", [P, 5, ST])

        arena = sb("arena", [P, ARENA])
        at = [0]

        def take(words):
            at[0] += words
            assert at[0] <= ARENA, at[0]
            return arena[:, at[0] - words:at[0]]

        wring_in = [take(WIN) for _ in range(2)]
        scr_a = at[0]
        at[0] = PT_AT
        PT = take(NT_IN * T).rearrange("p (n t) -> p n t", n=NT_IN)
        nat_at = at[0]
        knat, vnat, fnat = (take((ST + 1) * 512).rearrange("p (i c) -> p i c", i=ST + 1) for _ in range(3))
        ctm = take(HM * DB * DM).rearrange("p (h b v) -> p h b v", h=HM, b=DB)
        at[0] = PT_AT
        xT = take(KT * T).rearrange("p (k t) -> p k t", k=KT)
        sq = take(2 * T).rearrange("p (a t) -> p a t", a=2)
        rb = take(T)
        at[0] = scr_a
        lg = take(2 * HF * PAGE).rearrange("p (a h k) -> p a h k", a=2, h=HF)
        at[0] = nat_at
        gx, ge, gu, gd = (take(T)[0:GR] for _ in range(4))
        li, lfm, bm, mt, mprev, a0 = (take(T)[0:HM] for _ in range(6))
        at[0] = scr_a
        me = take(2 * 512).rearrange("p (i t) -> p i t", i=2)
        mstt = take(2 * 512).rearrange("p (i t) -> p i t", i=2)
        da = take(T); dr = take(T); hh = take(T)
        gm = take(2 * P).rearrange("p (i t) -> p i t", i=2)
        assert at[0] <= PT_AT
        at[0] = PT_AT + VM * T
        nmb = take(T); emb = take(T); hs = take(T)
        vw = take(ST * (P + 1)).rearrange("p (i c) -> p i c", i=ST)
        assert at[0] <= PT_AT + OM * T
        at[0] = PT_AT + VF * T
        wib = take(NS); nq = take(NS); ts1 = take(NS); ts2 = take(NS); hn = take(NS)
        wm = take(DB)
        vmk = take(DB * P).rearrange("p (b v) -> p b v", b=DB)
        assert at[0] <= nat_at
        at[0] = scr_a
        ncb = take(512)
        ncm = take(512).rearrange("p (i s) -> p i s", i=ST)
        pts = take(2 * 512).rearrange("p (i s) -> p i s", i=2)
        at[0] = nat_at
        scp = take(ST * 512).rearrange("p (i s) -> p i s", i=ST)
        pp = take(ST * 512).rearrange("p (i s) -> p i s", i=ST)
        at[0] = 0
        kring = [take(PC * NJ * P).rearrange("p (g j k) -> p g j k", g=PC, j=NJ) for _ in range(4)]
        vring = [take(PC * 512).rearrange("p (g c) -> p g c", g=PC) for _ in range(4)]
        scores = take(PAST + NS)
        probs = take(PAST + NS)
        bias = [take(PAST) for _ in range(2)]
        at[0] = 0
        wring = [take(WSLOT) for _ in range(2)]
        at[0] = PT_AT + KT * T
        act_ff = take(FT * T).rearrange("p (n t) -> p n t", n=FT)

        bscr = nc.dram_tensor("bias_scratch", [DB, HF, PAST], F32, kind="Internal").ap()

        names = """const_in x_in x_again small_in state_in idx_in lg_in w_in0 w_in1
            k_in0 k_in1 k_in2 k_in3 v_in0 v_in1 v_in2 v_in3 bias_in0 bias_in1 bias_out out_dma zeroed
            sq_ready sq_used root_done rinv_done h_ready
            gate_done gate_evac gate_step gate_act rows_ready rows_act page_step page_sum page_done
            tile_done tile_evac silu_done sig_ready qk_scaled new_copied
            nat_done nat_out_v nat_out_s cat_done cat_evac newb_ready
            mb_done mb_evac vw_ready mg_ready me_ready ms_done mst_ready mnd_done mint_done mden_ready
            mda_ready mdv hs_ready mss_done mroot mmix ct_done ct_out
            fb_done fb_evac fs_done f_dve f_max f_exp f_pn ft_done ft_evac fo_done fo_evac
            q_ready sc_done sc_evac s_step mx_ready p_ready pt_done pt_evac pv_done o_ready ot_done ot_evac
            y_ready y_out passed""".split()
        S = {n: sem(n) for n in names}
        w_in = [S["w_in0"], S["w_in1"]]
        k_in = [S[f"k_in{i}"] for i in range(4)]
        v_in = [S[f"v_in{i}"] for i in range(4)]
        bias_in = [S["bias_in0"], S["bias_in1"]]

        def pair(b):
            return PS[:, b:b + 2, 0:TH]

        def halves(ap):
            return ap.rearrange("p (a t) -> p a t", a=2)

        def stepped(ap, offset, dims):
            return bass.AP(ap.tensor, ap.offset + offset, [ap.ap[0], *dims])

        def hold_here(eng):
            eng.sem_inc(S["passed"], 1)

        blk = ctx.enter_context(nc.Block())

        @blk.sync
        def _(sp):
            sp.dma_start(xT[:, :, :], A["x"]).then_inc(S["x_in"], 16)
            sp.dma_start(wide[:, :], A["wide"]).then_inc(S["const_in"], 16)
            sp.dma_start(rowc[:, :], A["rows"]).then_inc(S["const_in"], 16)
            sp.dma_start(gains[:, :], A["gains"]).then_inc(S["const_in"], 16)
            sp.dma_start(wg[:, :, :], A["wgate"]).then_inc(S["small_in"], 16)
            sp.dma_start(gbias[:, :], A["gbias"]).then_inc(S["small_in"], 16)
            sp.dma_start(ptab[:, :], A["ptab"]).then_inc(S["small_in"], 16)
            sp.dma_start(mst[:, :], A["m"]).then_inc(S["small_in"], 16)
            sp.dma_start(nst[:, :, :], A["n"]).then_inc(S["small_in"], 16)

            for s in range(2):
                sp.dma_start(wring_in[s], A["win"][s]).then_inc(w_in[s], 16)
            sp.dma_start(ctm[:, :, :, :], A["C"]).then_inc(S["state_in"], 16)
            with sp.Fori(1, U_IN // 2) as i:
                for s in range(2):
                    sp.wait_ge(S["tile_done"], 4 * i + (2 * s - 2))
                    sp.dma_start(wring_in[s], A["win"][bass.ds(2 * i + s, 1), :, :]
                                 .rearrange("a p n -> p (a n)")).then_inc(w_in[s], 16)

            def pages(ring, sems, pool, b, c):
                hold_here(sp)
                slot = c % 4
                for g in range(PC):
                    pg = sp.value_load(ptab[0:1, bass.ds(b * PAGES + c * PC + g, 1)], min_val=0,
                                       max_val=A["npool"] - 1)
                    dst = ring[slot][:, g]
                    if pool is A["K"]:
                        dst = dst.rearrange("p j k -> p (j k)")
                    sp.dma_start(dst, pool[bass.ds(pg, 1), :, :].rearrange("a p n -> p (a n)"))\
                      .then_inc(sems[slot], 16)

            def load_keys(b, c):
                if c >= 4:
                    sp.wait_ge(S["sc_done"], b * CH + c - 3)
                elif not (isinstance(b, int) and b == 0):
                    sp.wait_ge(S["sc_done"], (b - 1) * CH + c + 5)
                pages(kring, k_in, A["K"], b, c)

            def load_values(b, c):
                if c >= 4:
                    sp.wait_ge(S["pv_done"], b * CH + c - 3)
                elif not (isinstance(b, int) and b == 0):
                    sp.wait_ge(S["pv_done"], (b - 1) * CH + c + 5)
                pages(vring, v_in, A["V"], b, c)

            def load_bias(b, par, wait):
                if wait:
                    sp.wait_ge(S["sc_evac"], (b - 1) * CH)
                for h in range(HF):
                    src = bass.AP(bscr.tensor, b * (HF * PAST) + h * PAST, [[0, DS], [1, PAST]])
                    sp.dma_start(bias[par][h * DS:(h + 1) * DS, :], src).then_inc(bias_in[par], 16)

            sp.wait_ge(S["small_in"], 5 * 16)
            sp.wait_ge(S["bias_out"], 8 * 16)
            sp.wait_ge(S["fo_done"], HF * ST)
            sp.wait_ge(S["fo_evac"], HF)
            sp.wait_ge(S["new_copied"], 3)
            sp.wait_ge(S["out_dma"], 16 * OUT_EARLY)
            load_keys(0, 0)
            load_bias(0, 0, False)
            load_bias(1, 1, False)
            for c in range(1, NCH):
                load_keys(0, c)

            def batch(b, next_par):
                for c in range(NCH):
                    load_keys(b, c)
                    load_values(b - 1, c)
                    if c == 3 and next_par is not None:
                        load_bias(b + 1, next_par, True)

            batch(1, 0)
            with sp.Fori(1, DB // 2 - 1) as i:
                batch(2 * i, 1)
                batch(2 * i + 1, 0)
            batch(DB - 2, 1)
            batch(DB - 1, None)
            for c in range(NCH):
                load_values(DB - 1, c)

            sp.wait_ge(S["pv_done"], DB * CH)
            sp.wait_ge(S["p_ready"], DB * CH)
            sp.wait_ge(S["pt_evac"], DB * CH)
            sp.dma_start(xT[:, :, :], A["x"]).then_inc(S["x_again"], 16)

            def stream(name, units, words, t0, per, before):
                for s in range(2):
                    sp.wait_ge(S["tile_done"], before[s])
                    sp.dma_start(wring[s][:, 0:words], A[name][s]).then_inc(w_in[s], 16)
                with sp.Fori(1, units // 2) as i:
                    for s in range(2):
                        sp.wait_ge(S["tile_done"], i * (2 * per) + (t0 + (s - 1) * per))
                        sp.dma_start(wring[s][:, 0:words], A[name][bass.ds(2 * i + s, 1), :, :]
                                     .rearrange("a p n -> p (a n)")).then_inc(w_in[s], 16)

            stream("wout", U_OUT, KT * UNIT_W, T0_OUT, 2, (T0_OUT, T0_OUT))
            stream("wgu", U_GU, 2 * KT * P, T0_GU, 2, (T0_GU - 2, T0_GU))
            stream("wdown", U_DN, FT * P, T0_DN, 1, (T0_DN - 2, T0_DN))
            sp.wait_ge(S["y_ready"], KT)
            sp.dma_start(A["o_y"], hT[:, :, :]).then_inc(S["y_out"], 16)
            sp.wait_ge(S["y_out"], 16)

        @blk.gpsimd
        def _(pool):
            nc.gpsimd.memset(epsc[:, :], EPS).then_inc(S["zeroed"], 1)
            nc.gpsimd.memset(ca[:, :], 0.0).then_inc(S["zeroed"], 1)
            nc.gpsimd.memset(qbd[:, :, :], 0.0).then_inc(S["zeroed"], 1)
            pool.dma_start(pidx[:, :], A["pidx"]).then_inc(S["idx_in"], 16)
            pool.wait_ge(S["idx_in"], 16)
            for half in range(2):
                nc.gpsimd.indirect_dma_start(
                    lg[:, half, :, :].rearrange("p h k -> p (h k)"), None, A["logf"],
                    bass.IndirectOffsetOnAxis(ap=pidx[:, half:half + 1], axis=0)).then_inc(S["lg_in"], 16)
            pool.wait_ge(S["page_done"], 1)
            for b in range(DB):
                pool.dma_start(bscr[b].rearrange("h (g k) -> g h k", g=PAGES),
                               lg[(b % 4) * PAGES:(b % 4 + 1) * PAGES, b // 4, :, :]).then_inc(S["bias_out"], 16)
            pool.wait_ge(S["rows_ready"], 1)
            pool.dma_start(A["o_logf"], lff[:, :]).then_inc(S["out_dma"], 16)
            pool.dma_start(A["o_m"], mout[:, :]).then_inc(S["out_dma"], 16)
            pool.wait_ge(S["tile_evac"], NT_IN)
            pool.dma_start(A["o_kf"], PT[:, KF:KF + NJ, :]).then_inc(S["out_dma"], 16)
            pool.dma_start(A["o_vf"], PT[:, VF:VF + NJ, :]).then_inc(S["out_dma"], 16)
            pool.wait_ge(S["ct_out"], HM)
            pool.dma_start(A["o_C"], ctm[:, :, :, :]).then_inc(S["out_dma"], 16)
            pool.dma_start(A["o_n"], nnew[:, :, :]).then_inc(S["out_dma"], 16)
            pool.dma_start(A["o_Cp"], ctp[:, :, :]).then_inc(S["out_dma"], 16)

            pool.wait_ge(S["new_copied"], 2)
            pool.wait_ge(S["zeroed"], 3)

            def queries(b):
                if not (isinstance(b, int) and b == 0):
                    pool.wait_ge(S["sc_done"], b * CH)
                for par in range(2):
                    rows = slice(par * DF, par * DF + DF)
                    dst = stepped(qbd[rows, :, :], par * DS, [[NS + 2 * DS, NJ], [1, DS]])
                    nc.gpsimd.tensor_copy(dst, qf_new[rows, :, bass.ds(b * DS, DS)]).then_inc(S["q_ready"], 1)

            queries(0)
            with pool.Fori(1, DB) as b:
                queries(b)

        @blk.scalar
        def _(act):
            a = nc.scalar

            def root(n):
                act.wait_ge(S["sq_used"], KT * (n + 1))
                if n:
                    act.wait_ge(S["h_ready"], KT * n)
                a.activation(halves(rb[:, :]), pair(0), ACT.Sqrt, bias=epsc[:, 0:1], scale=1.0 / D)\
                    .then_inc(S["root_done"], 1)

            act.wait_ge(S["zeroed"], 2)
            root(0)
            act.wait_ge(S["gate_step"], 1)
            a.activation(ge, gu, ACT.Exp).then_inc(S["gate_act"], 1)
            act.wait_ge(S["gate_step"], 3)
            a.activation(gu, gu, ACT.Ln).then_inc(S["gate_act"], 1)

            with act.Fori(0, NT_IN // 4) as i:
                for t in range(4):
                    act.wait_ge(S["tile_done"], 4 * i + t + 1)
                    dst = PT[:, bass.ds(4 * i + t, 1), :].rearrange("p a (g t) -> p (a g) t", g=2)
                    a.copy(dst, pair(2 * t)).then_inc(S["tile_evac"], 1)

            act.wait_ge(S["tile_evac"], NT_IN)
            act.wait_ge(S["rows_ready"], 1)
            a.activation(emt[:, :], mt, ACT.Exp, scale=-1.0)
            a.activation(winter[:, :], mprev[:, SEQ:T], ACT.Exp)
            a.activation(dec[:, :], dec[:, :], ACT.Exp)
            a.activation(ca[0:HM, 0:SEQ], a0[:, 0:SEQ], ACT.Exp, bias=nml[:, 0:1])
            a.activation(ca[0:HM, SEQ:T], a0[:, SEQ:T], ACT.Exp).then_inc(S["rows_act"], 1)
            act.wait_ge(S["rows_act"], 1)
            for n in range(1, 3 * (ST + 1), 2):
                rows = P if n % (ST + 1) < ST else NS
                dst = (knat, vnat, fnat)[n // (ST + 1)]
                act.wait_ge(S["nat_done"], n + 1)
                a.copy(dst[0:rows, n % (ST + 1), :], PS[0:rows, n % 4, :]).then_inc(S["nat_out_s"], 1)
            a.activation(PT[:, OM:OM + HM, :], PT[:, OM:OM + HM, :], ACT.Sigmoid).then_inc(S["sig_ready"], 1)
            act.wait_ge(S["cat_evac"], 2)
            act.wait_ge(S["nat_out_v"], 8)
            act.wait_ge(S["nat_out_s"], 7)
            act.wait_ge(S["out_dma"], 16 * 4)

            for h in range(HM):
                act.wait_ge(S["mb_done"], h + 1)
                if h:
                    act.wait_ge(S["mmix"], h)
                a.activation(halves(nmb), pair(0), ACT.Copy, scale=-1.0).then_inc(S["mb_evac"], 1)
                a.copy(halves(emb), pair(2)).then_inc(S["mb_evac"], 1)
                a.copy(wib, PS[:, 3, TH:TH + NS]).then_inc(S["mb_evac"], 1)
                act.wait_ge(S["mb_evac"], 3 * h + 3)
                for i in range(ST + 1):
                    n = h * (ST + 1) + i
                    rows, w = (P, P) if i < ST else (NS, NS)
                    act.wait_ge(S["mg_ready"], n + 1)
                    if n >= 2:
                        act.wait_ge(S["mst_ready"], n - 1)
                    ab = cat[0:rows, i, ROWS_F + h:ROWS_F + h + 1]
                    e = a.activation(me[0:rows, n % 2, 0:w], gm[0:rows, n % 2, 0:w], ACT.Exp, bias=ab)
                    if i < ST - 1:
                        e = a.activation(me[:, n % 2, P:SEQ - i * P], nmb[:, (i + 1) * P:SEQ], ACT.Exp, bias=ab)
                    e.then_inc(S["me_ready"], 1)
                act.wait_ge(S["mnd_done"], h * (ST + 1) + ST)
                a.activation(da[:, 0:SEQ], PS[:, 7, :], ACT.Abs).then_inc(S["mda_ready"], 1)
                act.wait_ge(S["mden_ready"], h + 1)
                a.activation(da[:, SEQ:T], ts2, ACT.Abs).then_inc(S["mda_ready"], 1)
                act.wait_ge(S["mss_done"], h + 1)
                a.activation(halves(dr), pair(0), ACT.Sqrt, bias=epsc[:, 0:1], scale=1.0 / DM)\
                    .then_inc(S["mroot"], 1)

            act.wait_ge(S["mmix"], HM)
            act.wait_ge(S["ct_out"], HM)
            for h in range(HF):
                act.wait_ge(S["fb_done"], h + 1)
                if h:
                    act.wait_ge(S["f_max"], ST * h)
                a.copy(ncb, PS[:, 0, :]).then_inc(S["fb_evac"], 1)
                for i in range(ST):
                    act.wait_ge(S["f_max"], h * ST + i + 1)
                    if h:
                        act.wait_ge(S["ft_done"], ST * h)
                    w = (i + 1) * P
                    a.activation(pp[:, i, 0:w], scp[:, i, 0:w], ACT.Exp, bias=fmx[:, 2, i:i + 1],
                                 accum_out=fmx[:, 3, i:i + 1]).then_inc(S["f_exp"], 1)
                for j in range(ST):
                    n = h * ST + j
                    act.wait_ge(S["ft_done"], n + 1)
                    if n >= 2:
                        act.wait_ge(S["fo_done"], n - 1)
                    a.copy(pts[:, j % 2, j * P:SEQ], PS[:, 5 + j % 2, j * P:SEQ]).then_inc(S["ft_evac"], 1)
                act.wait_ge(S["fo_done"], (h + 1) * ST)
                rows = slice((h % 2) * DF, (h % 2) * DF + DF)
                a.copy(hT[rows, NJ + h // 2, 0:SEQ], PS[0:DF, 7, :]).then_inc(S["fo_evac"], 1)

            act.wait_ge(S["fo_done"], HF * ST)
            act.wait_ge(S["out_dma"], 16 * OUT_EARLY)
            act.wait_ge(S["new_copied"], 3)

            def sample(b, qk, pv):
                if pv:
                    for c in range(CH):
                        act.wait_ge(S["pt_done"], (b - 1) * CH + c + 1)
                        if not (isinstance(b, int) and b == 1 and c < 3):
                            act.wait_ge(S["pv_done"], (b - 1) * CH + c - 2)
                        rows, w = (P, PC * NS) if c < NCH else (NS, NS)
                        a.copy(ptile[0:rows, c % 3, 0:w], PS[0:rows, 3 + c % 3, 0:w]).then_inc(S["pt_evac"], 1)
                if qk:
                    act.wait_ge(S["mx_ready"], b + 1)
                    for c in range(CH):
                        n = NS if c == NCH else PC * PAGE
                        if not (isinstance(b, int) and b == 0):
                            act.wait_ge(S["pt_done"], (b - 1) * CH + c + 1)
                        a.activation(probs[0:NS, c * 512:c * 512 + n], scores[0:NS, c * 512:c * 512 + n], ACT.Exp,
                                     bias=snm[:, 1:2], accum_out=ssum[:, c:c + 1]).then_inc(S["p_ready"], 1)

            sample(0, True, False)
            sample(1, True, True)
            with act.Fori(2, DB) as b:
                sample(b, True, True)
            sample(DB, False, True)

            root(1)
            act.wait_ge(S["pv_done"], DB * CH)
            with act.Fori(0, FT // 2) as i:
                for t in range(2):
                    act.wait_ge(S["tile_done"], 4 * i + (NT_IN + KT + 2 * t + 1))
                    dst = act_ff[:, bass.ds(2 * i + t, 1), :].rearrange("p a (g t) -> p (a g) t", g=2)
                    a.activation(dst, pair(4 * t), ACT.Silu).then_inc(S["silu_done"], 1)
            root(2)

        @blk.vector
        def _(dve):
            v = nc.vector

            def norm(n, out_sem):
                for kt in range(KT):
                    u = n * KT + kt
                    if u >= 2:
                        dve.wait_ge(S["sq_used"], u - 1)
                    v.tensor_tensor(sq[:, kt % 2, :], xT[:, kt, :], xT[:, kt, :], ALU.mult)\
                        .then_inc(S["sq_ready"], 1)
                dve.wait_ge(S["root_done"], n + 1)
                v.reciprocal(rb[:, :], rb[:, :]).then_inc(S["rinv_done"], 1)
                dve.wait_ge(S["rinv_done"], n + 1)
                for kt in range(KT):
                    v.scalar_tensor_tensor(out=hT[:, kt, :], in0=xT[:, kt, :],
                                           scalar=gains[:, n * KT + kt:n * KT + kt + 1],
                                           in1=rb[:, :], op0=ALU.mult, op1=ALU.mult).then_inc(S[out_sem], 1)

            dve.wait_ge(S["x_in"], 16)
            dve.wait_ge(S["const_in"], 3 * 16)
            norm(0, "h_ready")

            st = [0]

            def step(ins):
                st[0] += 1
                ins.then_inc(S["gate_step"], 1)
                dve.wait_ge(S["gate_step"], st[0])

            dve.wait_ge(S["small_in"], 5 * 16)
            dve.wait_ge(S["gate_done"], 1)
            v.tensor_scalar(halves(gx), PS[0:GR, 6:8, 0:TH], gbias[:, 0:1], None, ALU.add)\
                .then_inc(S["gate_evac"], 1)
            dve.wait_ge(S["gate_evac"], 1)
            step(v.scalar_tensor_tensor(out=gu, in0=gx, scalar=-1.0, in1=gx, op0=ALU.mult, op1=ALU.min))
            dve.wait_ge(S["gate_act"], 1)
            step(v.tensor_scalar(gu, ge, 1.0, None, ALU.add))
            step(v.tensor_scalar(gd, gu, 1.0, None, ALU.subtract))
            dve.wait_ge(S["gate_act"], 2)
            step(v.tensor_tensor(gu, gu, ge, ALU.mult))
            step(v.scalar_tensor_tensor(out=ge, in0=gd, scalar=0.0, in1=ge, op0=ALU.is_equal, op1=ALU.mult))
            step(v.scalar_tensor_tensor(out=gd, in0=gd, scalar=0.0, in1=gd, op0=ALU.is_equal, op1=ALU.add))
            step(v.reciprocal(gd, gd))
            step(v.tensor_tensor(gu, gu, gd, ALU.mult))
            step(v.tensor_tensor(gu, gu, ge, ALU.add))
            step(v.tensor_scalar(gd, gx, 0.0, None, ALU.min))
            step(v.tensor_tensor(gd, gd, gu, ALU.subtract))
            v.tensor_copy(li, gx[0:HM, :])
            v.tensor_copy(lfm, gd[ROWS_F:ROWS_F + HM, :])
            step(v.tensor_copy(lff[:, :], gd[ROWS_FF:ROWS_FF + HF, :]))

            step(v.tensor_tensor_scan(bm, keep[0:HM, :], lfm, 0.0, ALU.mult, ALU.add))
            step(v.tensor_tensor(a0, li, bm, ALU.subtract))
            dve.wait_ge(S["zeroed"], 2)
            v.tensor_copy(ca[ROWS_F:ROWS_F + HM, :], a0)
            v.memset(mprev[:, 0:SEQ], 0.0)
            step(v.tensor_copy(mprev[:, SEQ:T].rearrange("p (b q) -> p b q", b=DB),
                               mst[:, :].unsqueeze(2).broadcast_to([HM, DB, DS])))
            step(v.tensor_tensor_scan(m_top[:, :], drop[0:HM, :], a0, NEG, ALU.add, ALU.max))
            step(v.tensor_tensor(m_top[:, :], m_top[:, :], mprev, ALU.max))
            step(v.tensor_tensor(mt, bm, m_top[:, :], ALU.add))
            m_last = m_top[:, SEQ:T].rearrange("p (b q) -> p b q", b=DB)
            v.tensor_tensor(mprev[:, SEQ:T], mprev[:, SEQ:T], m_top[:, SEQ:T], ALU.subtract)
            v.tensor_tensor(dec[:, :], mst[:, :], m_last[:, :, DS - 1], ALU.subtract)
            v.tensor_scalar(nml[:, :], m_top[:, SEQ - 1:SEQ], -1.0, None, ALU.mult)
            a0_new = a0[:, SEQ:T].rearrange("p (b q) -> p b q", b=DB)
            v.tensor_tensor(a0_new, a0_new, m_last[:, :, DS - 1:DS].broadcast_to([HM, DB, DS]), ALU.subtract)
            v.tensor_copy(mout[:, 0:1], mt[:, SEQ - 1:SEQ])
            v.tensor_copy(mout[:, 1:1 + DB], mt[:, SEQ:T].rearrange("p (b q) -> p b q", b=DB)[:, :, DS - 1])
            step(v.tensor_tensor_scan(ncf[:, :], keep[:, :], lff[:, :], 0.0, ALU.mult, ALU.add))
            v.tensor_scalar(ncf[:, :], ncf[:, :], -1.0, None, ALU.mult).then_inc(S["rows_ready"], 1)

            dve.wait_ge(S["lg_in"], 32)
            for half in range(2):
                for h in range(HF):
                    last = v.tensor_tensor_scan(lg[:, half, h, :], ones, lg[:, half, h, :], 0.0, ALU.mult, ALU.add)
            last.then_inc(S["page_step"], 1)
            dve.wait_ge(S["page_step"], 1)
            v.tensor_copy(pgs[:, :, :], lg[:, :, :, PAGE - 1]).then_inc(S["page_step"], 1)
            dve.wait_ge(S["page_sum"], 1)
            for half in range(2):
                last = v.scalar_tensor_tensor(
                    out=lg[:, half], in0=lg[:, half], scalar=-1.0,
                    in1=PS[:, 5, half * HF:(half + 1) * HF].unsqueeze(2).broadcast_to([P, HF, PAGE]),
                    op0=ALU.mult, op1=ALU.add)
            last.then_inc(S["page_done"], 1)

            dve.wait_ge(S["tile_evac"], NT_IN)
            v.tensor_scalar(PT[:, KM:KM + HM, :], PT[:, KM:KM + HM, :], DM ** -0.5, None, ALU.mult)\
                .then_inc(S["qk_scaled"], 1)
            v.tensor_scalar(PT[:, QF:QF + NJ, :], PT[:, QF:QF + NJ, :], DF ** -0.5, None, ALU.mult)\
                .then_inc(S["qk_scaled"], 1)
            dve.wait_ge(S["qk_scaled"], 2)
            v.tensor_copy(qf_new[:, :, :], PT[:, QF:QF + NJ, SEQ:T]).then_inc(S["new_copied"], 1)
            v.tensor_copy(kf_new[:, :, :], PT[:, KF:KF + NJ, SEQ:T]).then_inc(S["new_copied"], 1)

            dve.wait_ge(S["rows_act"], 1)
            for n in range(0, 3 * (ST + 1), 2):
                rows = P if n % (ST + 1) < ST else NS
                dst = (knat, vnat, fnat)[n // (ST + 1)]
                dve.wait_ge(S["nat_done"], n + 1)
                v.tensor_copy(dst[0:rows, n % (ST + 1), :], PS[0:rows, n % 4, :]).then_inc(S["nat_out_v"], 1)
            dve.wait_ge(S["cat_done"], 1)
            R = ROWS_F + HM
            v.tensor_copy(cat[:, 0:ST, :], PS[:, 4, 0:ST * R].rearrange("p (i r) -> p i r", i=ST))
            v.tensor_copy(cat[0:NS, ST, :], PS[0:NS, 4, ST * R:(ST + 1) * R]).then_inc(S["cat_evac"], 1)
            v.tensor_copy(decb[:, :, :], PS[:, 5, 32:32 + HM * DB].rearrange("p (h b) -> p h b", h=HM))
            v.tensor_tensor(bias_new[:, :, :], new_mask[0:NS],
                            PS[0:NS, 5, 64:64 + NS].unsqueeze(1).broadcast_to([NS, DB, NS]), ALU.add)\
                .then_inc(S["cat_evac"], 1)
            dve.wait_ge(S["cat_evac"], 2)
            dve.wait_ge(S["nat_out_v"], 8)
            dve.wait_ge(S["nat_out_s"], 7)
            dve.wait_ge(S["state_in"], 16)
            dve.wait_ge(S["sig_ready"], 1)
            dve.wait_ge(S["bias_out"], 8 * 16)
            dve.wait_ge(S["out_dma"], 16 * 4)

            mdv = [0]

            def mstep(ins):
                mdv[0] += 1
                ins.then_inc(S["mdv"], 1)
                dve.wait_ge(S["mdv"], mdv[0])

            def weigh(h, i):
                n = h * (ST + 1) + i
                rows, w = (P, SEQ - i * P) if i < ST else (NS, NS)
                dve.wait_ge(S["me_ready"], n + 1)
                dve.wait_ge(S["ms_done"], n + 1)
                if n >= 2:
                    dve.wait_ge(S["mnd_done"], n - 1)
                v.tensor_tensor(mstt[0:rows, n % 2, 0:w], PS[0:rows, 4 + n % 2, 0:w], me[0:rows, n % 2, 0:w],
                                ALU.mult).then_inc(S["mst_ready"], 1)

            for h in range(HM):
                dve.wait_ge(S["mb_evac"], 3 * (h + 1))
                if h:
                    dve.wait_ge(S["ct_done"], 2 * h)
                mstep(v.tensor_scalar(wm[0:NS, :], block_of[0:NS, :], cat[0:NS, ST, h:h + 1], None, ALU.mult))
                v.tensor_tensor(vw[:, :, 0:P], vnat[:, 0:ST, h * P:(h + 1) * P],
                                cat[:, 0:ST, h:h + 1].broadcast_to([P, ST, P]), ALU.mult)
                v.tensor_copy(vw[:, :, P], cat[:, 0:ST, h])
                v.tensor_tensor(vmk[0:NS], vnat[0:NS, ST, h * P:(h + 1) * P].unsqueeze(1).broadcast_to([NS, DB, P]),
                                wm[0:NS, :].unsqueeze(2).broadcast_to([NS, DB, P]), ALU.mult)
                v.tensor_tensor(nq.rearrange("p (b q) -> p b q", b=DB),
                                PT[:, QM + h, SEQ:T].rearrange("p (b q) -> p b q", b=DB),
                                nst[:, h, :].unsqueeze(2).broadcast_to([P, DB, DS]), ALU.mult)\
                    .then_inc(S["vw_ready"], 1)
                for i in range(ST + 1):
                    n = h * (ST + 1) + i
                    rows, w = (P, P) if i < ST else (NS, NS)
                    if n >= 2:
                        dve.wait_ge(S["me_ready"], n - 1)
                    v.tensor_tensor(gm[0:rows, n % 2, 0:w], nmb[0:rows, i * P:i * P + w],
                                    causal_t if i < ST else causal_s[0:NS, :], ALU.add)\
                        .then_inc(S["mg_ready"], 1)
                    if i >= 1:
                        weigh(h, i - 1)
                weigh(h, ST)
                dve.wait_ge(S["mint_done"], h + 1)
                v.tensor_tensor(ts1, PS[:, 2, 0:NS], wib, ALU.mult)
                mstep(v.tensor_tensor(ts2, PS[:, 3, 0:NS], wib, ALU.mult))
                dve.wait_ge(S["mnd_done"], (h + 1) * (ST + 1))
                v.tensor_tensor(ts2, PS[:, 1, 0:NS], ts2, ALU.add).then_inc(S["mden_ready"], 1)
                v.tensor_tensor(hn, PS[:, 0, 0:NS], ts1, ALU.add)
                dve.wait_ge(S["mda_ready"], 2 * (h + 1))
                mstep(v.tensor_tensor(da, da, emb, ALU.max))
                mstep(v.reciprocal(dr, da))
                v.tensor_tensor(hh[:, 0:SEQ], PS[:, 6, :], dr[:, 0:SEQ], ALU.mult)
                mstep(v.tensor_tensor(hh[:, SEQ:T], hn, dr[:, SEQ:T], ALU.mult))
                v.tensor_tensor(hs, hh, hh, ALU.mult).then_inc(S["hs_ready"], 1)
                dve.wait_ge(S["ct_done"], 2 * h + 1)
                v.tensor_copy(ctp[:, h, :], PS[:, 4, 0:P + 1])
                v.tensor_tensor(ctm[:, h], ctm[:, h], decb[:, h, :].unsqueeze(2).broadcast_to([P, DB, P]), ALU.mult)
                mstep(v.tensor_tensor(nnew[:, h, :], nst[:, h, :], decb[:, h, :], ALU.mult))
                dve.wait_ge(S["ct_done"], 2 * h + 2)
                c2 = ctm[:, h].rearrange("p (a b) v -> p a (b v)", a=2)
                v.tensor_tensor(c2, PS[:, 2:4, :], c2, ALU.add)
                v.tensor_tensor(nnew[:, h, :], PS[:, 5, 0:DB], nnew[:, h, :], ALU.add).then_inc(S["ct_out"], 1)
                dve.wait_ge(S["mroot"], h + 1)
                mstep(v.reciprocal(dr, dr))
                mstep(v.scalar_tensor_tensor(out=hh, in0=hh, scalar=gains[:, 3 * KT + h:3 * KT + h + 1], in1=dr,
                                             op0=ALU.mult, op1=ALU.mult))
                v.tensor_tensor(hT[:, h, :], hh, PT[:, OM + h, :], ALU.mult).then_inc(S["mmix"], 1)
            dve.wait_ge(S["mmix"], HM)

            fd = [0]

            def fstep(ins):
                fd[0] += 1
                ins.then_inc(S["f_dve"], 1)
                dve.wait_ge(S["f_dve"], fd[0])

            for h in range(HF):
                dve.wait_ge(S["fb_evac"], h + 1)
                fstep(v.tensor_tensor(ncm[:, :, :], ncb.rearrange("p (i s) -> p i s", i=ST),
                                      causal_n.unsqueeze(1).broadcast_to([P, ST, P]), ALU.add))
                for i in range(ST):
                    lo = i * P
                    dve.wait_ge(S["fs_done"], h * ST + i + 1)
                    if h:
                        dve.wait_ge(S["f_exp"], (h - 1) * ST + i + 1)
                    fstep(v.tensor_tensor_reduce(scp[:, i, lo:lo + P], PS[:, 1 + i, lo:lo + P], ncm[:, i, :], 1.0,
                                                 NEG, ALU.add, ALU.max, fmx[:, 0, i:i + 1]))
                    if i:
                        fstep(v.tensor_tensor_reduce(scp[:, i, 0:lo], PS[:, 1 + i, 0:lo], ncb[:, 0:lo], 1.0,
                                                     NEG, ALU.add, ALU.max, fmx[:, 1, i:i + 1]))
                        fstep(v.tensor_tensor(fmx[:, 0, i:i + 1], fmx[:, 0, i:i + 1], fmx[:, 1, i:i + 1], ALU.max))
                    v.tensor_scalar(fmx[:, 2, i:i + 1], fmx[:, 0, i:i + 1], -1.0, None, ALU.mult)\
                        .then_inc(S["f_max"], 1)
                for i in range(ST):
                    dve.wait_ge(S["f_exp"], h * ST + i + 1)
                    fstep(v.reciprocal(fmx[:, 4, i:i + 1], fmx[:, 3, i:i + 1]))
                    v.tensor_scalar(pp[:, i, 0:(i + 1) * P], pp[:, i, 0:(i + 1) * P], fmx[:, 4, i:i + 1], None,
                                    ALU.mult).then_inc(S["f_pn"], 1)
            v.tensor_copy(vf_new[:, :], fnat[0:NS, ST, :]).then_inc(S["new_copied"], 1)

            dve.wait_ge(S["new_copied"], 3)
            dve.wait_ge(S["fo_done"], HF * ST)
            dve.wait_ge(S["fo_evac"], HF)
            dve.wait_ge(S["out_dma"], 16 * OUT_EARLY)

            def sample(b, par, qk, pv, ot):
                first = isinstance(b, int) and b == 0
                if qk:
                    for c in range(CH):
                        n = NS if c == NCH else PC * PAGE
                        chunk = scores[0:NS, c * 512:c * 512 + n]
                        if c == 0:
                            dve.wait_ge(bias_in[par], (b - par) * (8 * HF) + 16 * HF)
                        dve.wait_ge(S["sc_done"], b * CH + c + 1)
                        if not first:
                            dve.wait_ge(S["p_ready"], (b - 1) * CH + c + 1)
                        if c < NCH:
                            hold_here(dve)
                            v.tensor_tensor_reduce(chunk, PS[0:NS, c % 3, 0:n], bias[par][0:NS, c * 512:c * 512 + n],
                                                   1.0, NEG, ALU.add, ALU.max, smx[:, c:c + 1])\
                                .then_inc(S["sc_evac"], 1)
                        else:
                            nb = bias_new[:, bass.ds(b, 1), :].rearrange("p a k -> p (a k)")
                            v.tensor_tensor(chunk, PS[0:NS, c % 3, 0:n], nb, ALU.add).then_inc(S["sc_evac"], 1)
                    dve.wait_ge(S["sc_evac"], (b + 1) * CH)
                    v.tensor_reduce(smx[:, NCH:CH], scores[0:NS, PAST:PAST + NS], AX.X, ALU.max)\
                        .then_inc(S["s_step"], 1)
                    dve.wait_ge(S["s_step"], b * 4 + 1)
                    v.tensor_reduce(snm[:, 0:1], smx[:, :], AX.X, ALU.max).then_inc(S["s_step"], 1)
                    dve.wait_ge(S["s_step"], b * 4 + 2)
                    v.tensor_scalar(snm[:, 1:2], snm[:, 0:1], -1.0, None, ALU.mult).then_inc(S["mx_ready"], 1)
                if ot:
                    dve.wait_ge(S["ot_done"], b - 1)
                    for p2 in range(2):
                        rows = slice(p2 * DF, p2 * DF + DF)
                        src = stepped(PS[rows, 7, 0:NJ * NS], p2 * DS, [[NS + 2 * DS, NJ], [1, DS]])
                        v.tensor_copy(hT[rows, NJ:2 * NJ, bass.ds((b - 2) * DS + SEQ, DS)], src)\
                            .then_inc(S["ot_evac"], 1)
                if pv:
                    dve.wait_ge(S["pv_done"], b * CH)
                    if ot:
                        dve.wait_ge(S["ot_done"], b - 1)
                    v.tensor_scalar(osb[:, :], PS[0:NS, 6, :], sri[:, 1:2], None, ALU.mult)\
                        .then_inc(S["o_ready"], 1)
                if qk:
                    dve.wait_ge(S["p_ready"], (b + 1) * CH)
                    v.tensor_reduce(sri[:, 0:1], ssum[:, :], AX.X, ALU.add).then_inc(S["s_step"], 1)
                    dve.wait_ge(S["s_step"], b * 4 + 3)
                    v.reciprocal(sri[:, 1:2], sri[:, 0:1]).then_inc(S["s_step"], 1)
                    dve.wait_ge(S["s_step"], b * 4 + 4)

            sample(0, 0, True, False, False)
            sample(1, 1, True, True, False)
            with dve.Fori(1, DB // 2) as i:
                sample(2 * i, 0, True, True, True)
                sample(2 * i + 1, 1, True, True, True)
            sample(DB, 0, False, True, True)
            sample(DB + 1, 0, False, False, True)
            dve.wait_ge(S["ot_evac"], 2 * DB)

            def residual(tiles, per, base, banks):
                with dve.Fori(0, tiles // per) as i:
                    for t in range(per):
                        dve.wait_ge(S["tile_done"], i * per + (base + t + 1))
                        b0 = 2 * (t % banks)
                        dst = xT[:, bass.ds(i * per + t, 1), :].rearrange("p a (g t) -> p (a g) t", g=2)
                        v.tensor_tensor(dst, PS[:, b0:b0 + 2, 0:TH], dst, ALU.add).then_inc(S["tile_evac"], 1)

            dve.wait_ge(S["x_again"], 16)
            residual(KT, 4, NT_IN, 4)
            dve.wait_ge(S["tile_evac"], NT_IN + KT)
            norm(1, "h_ready")
            with dve.Fori(0, FT // 2) as i:
                for t in range(2):
                    dve.wait_ge(S["tile_done"], 4 * i + (NT_IN + KT + 2 * t + 2))
                    dve.wait_ge(S["silu_done"], 2 * i + (t + 1))
                    dst = act_ff[:, bass.ds(2 * i + t, 1), :].rearrange("p a (g t) -> p (a g) t", g=2)
                    v.tensor_tensor(dst, pair(4 * t + 2), dst, ALU.mult).then_inc(S["tile_evac"], 1)
            residual(KT, 2, NT_IN + KT + 2 * FT, 2)
            dve.wait_ge(S["tile_evac"], NT_IN + KT + FT + KT)
            norm(2, "y_ready")

        @blk.tensor
        def _(pe):
            mm = nc.tensor.matmul

            def ssq(n):
                for kt in range(KT):
                    pe.wait_ge(S["sq_ready"], n * KT + kt + 1)
                    for g in range(2):
                        last = mm(PS[:, g, 0:TH], ones, sq[:, kt % 2, g * TH:(g + 1) * TH],
                                  start=(kt == 0), stop=(kt == KT - 1))
                    last.then_inc(S["sq_used"], 1)

            def product(bk, weight, rhs, kts):
                for kt in range(kts):
                    for g in range(2):
                        last = mm(PS[:, bk + g, 0:TH], weight(kt), rhs[:, kt, g * TH:(g + 1) * TH],
                                  start=(kt == 0), stop=(kt == kts - 1))
                return last

            pe.wait_ge(S["const_in"], 3 * 16)
            ssq(0)
            pe.wait_ge(S["small_in"], 5 * 16)
            for kt in range(KT):
                pe.wait_ge(S["h_ready"], kt + 1)
                for g in range(2):
                    last = mm(PS[0:GR, 6 + g, 0:TH], wg[:, kt, :], hT[:, kt, g * TH:(g + 1) * TH],
                              start=(kt == 0), stop=(kt == KT - 1))
            last.then_inc(S["gate_done"], 1)


            def project(i, slots, ring, rhs, kts, u0, t0, waits):
                for s in slots:
                    pe.wait_ge(w_in[s], 16 * i + (8 * u0 + 16))
                    w = ring[s][:, 0:KT * UNIT_W].rearrange("p (k n) -> p k n", k=KT)
                    for ct in range(2):
                        t = 2 * s + ct
                        if waits:
                            pe.wait_ge(S["tile_evac"], 4 * i + (t0 + t - 3))
                        elif t == 3:
                            pe.wait_ge(S["gate_evac"], 1)
                        product(2 * t, lambda kt: w[:, kt, ct * P:(ct + 1) * P], rhs, kts)\
                            .then_inc(S["tile_done"], 1)

            pe.wait_ge(S["root_done"], 1)
            project(0, range(2), wring_in, hT, KT, 0, 0, False)
            with pe.Fori(1, U_IN // 2) as i:
                project(i, range(2), wring_in, hT, KT, 0, 0, True)

            pe.wait_ge(S["tile_evac"], NT_IN)
            pe.wait_ge(S["page_step"], 2)
            mm(PS[:, 5, 0:2 * HF], suffix, pgs[:, :, :].rearrange("p a h -> p (a h)"), start=True, stop=True)\
                .then_inc(S["page_sum"], 1)
            pe.wait_ge(S["qk_scaled"], 2)
            for n in range(3 * (ST + 1)):
                t0, i = (KM, VM, VF)[n // (ST + 1)], n % (ST + 1)
                w = P if i < ST else NS
                if n >= 4:
                    pe.wait_ge(S[("nat_out_v", "nat_out_s")[n % 2]], n // 2 - 1)
                for c in range(4):
                    last = nc.tensor.transpose(PS[0:w, n % 4, c * P:(c + 1) * P], PT[:, t0 + c, i * P:i * P + w],
                                               ident)
                last.then_inc(S["nat_done"], 1)
            R = ROWS_F + HM
            pe.wait_ge(S["rows_act"], 1)
            pe.wait_ge(S["rows_ready"], 1)
            for i in range(ST + 1):
                w = P if i < ST else NS
                nc.tensor.transpose(PS[0:w, 4, i * R:(i + 1) * R], ca[:, i * P:i * P + w], ident[0:R, 0:R])
            pe.wait_ge(S["page_done"], 1)
            for h in range(HM):
                mm(PS[:, 5, 32 + h * DB:32 + (h + 1) * DB], sel4[:, h * P:(h + 1) * P], dec[:, :],
                   start=True, stop=True)
            mm(PS[0:NS, 5, 64:64 + NS], selq, ncf[:, SEQ:T], start=True, stop=True).then_inc(S["cat_done"], 1)

            pe.wait_ge(S["cat_evac"], 2)
            pe.wait_ge(S["nat_out_v"], 8)
            pe.wait_ge(S["nat_out_s"], 7)
            pe.wait_ge(S["state_in"], 16)
            for h in range(HM):
                hc = slice(h * P, (h + 1) * P)
                if h:
                    pe.wait_ge(S["mroot"], h)
                    pe.wait_ge(S["ct_out"], h)
                    pe.wait_ge(S["hs_ready"], h)
                for g in range(2):
                    mm(PS[:, g, 0:TH], sel4[:, hc], m_top[:, g * TH:(g + 1) * TH], start=True, stop=True)
                    mm(PS[:, 2 + g, 0:TH], sel4[:, hc], emt[:, g * TH:(g + 1) * TH], start=True, stop=True)
                mm(PS[:, 3, TH:TH + NS], sel4[:, hc], winter[:, :], start=True, stop=True)\
                    .then_inc(S["mb_done"], 1)

                def logits(i):
                    n = h * (ST + 1) + i
                    if i >= 2:
                        pe.wait_ge(S["mst_ready"], n - 1)
                    rows = P if i < ST else NS
                    end = SEQ if i < ST else T
                    mm(PS[0:rows, 4 + n % 2, 0:end - i * P], PT[:, KM + h, i * P:i * P + rows],
                       PT[:, QM + h, i * P:end], start=True, stop=True).then_inc(S["ms_done"], 1)

                def outputs(i):
                    n = h * (ST + 1) + i
                    pe.wait_ge(S["mst_ready"], n + 1)
                    if i < ST:
                        mm(PS[:, 6, i * P:SEQ], vnat[:, i, hc], mstt[:, n % 2, 0:SEQ - i * P],
                           start=(i == 0), stop=(i == ST - 1))
                        mm(PS[:, 7, i * P:SEQ], ones, mstt[:, n % 2, 0:SEQ - i * P],
                           start=(i == 0), stop=(i == ST - 1)).then_inc(S["mnd_done"], 1)
                    else:
                        mm(PS[:, 0, 0:NS], vnat[0:NS, ST, hc], mstt[0:NS, n % 2, 0:NS], start=True, stop=True)
                        mm(PS[:, 1, 0:NS], ones[0:NS, :], mstt[0:NS, n % 2, 0:NS], start=True, stop=True)\
                            .then_inc(S["mnd_done"], 1)

                logits(0)
                logits(1)
                pe.wait_ge(S["mb_evac"], 3 * (h + 1))
                pe.wait_ge(S["vw_ready"], h + 1)
                for b in range(DB):
                    mm(PS[:, 2, b * DS:(b + 1) * DS], ctm[:, h, b, :], PT[:, QM + h, SEQ + b * DS:SEQ + (b + 1) * DS],
                       start=True, stop=True)
                mm(PS[:, 3, 0:NS], ones, nq, start=True, stop=True).then_inc(S["mint_done"], 1)
                for i in range(ST + 1):
                    if i >= 2:
                        logits(i)
                    if i >= 1:
                        outputs(i - 1)
                outputs(ST)
                for i in range(ST):
                    last = mm(PS[:, 4, 0:P + 1], knat[:, i, hc], vw[:, i, :], start=(i == 0), stop=(i == ST - 1))
                last.then_inc(S["ct_done"], 1)
                pe.wait_ge(S["mden_ready"], h + 1)
                for g in range(2):
                    mm(PS[:, 2 + g, :], knat[0:NS, ST, hc],
                       vmk[0:NS, 4 * g:4 * g + 4, :].rearrange("p b v -> p (b v)"), start=True, stop=True)
                mm(PS[:, 5, 0:DB], knat[0:NS, ST, hc], wm[0:NS, :], start=True, stop=True)\
                    .then_inc(S["ct_done"], 1)
                pe.wait_ge(S["hs_ready"], h + 1)
                for g in range(2):
                    last = mm(PS[:, g, 0:TH], ones, hs[:, g * TH:(g + 1) * TH], start=True, stop=True)
                last.then_inc(S["mss_done"], 1)

            pe.wait_ge(S["mroot"], HM)
            pe.wait_ge(S["ct_out"], HM)

            def fox_scores(h):
                rows = slice((h % 2) * DF, (h % 2) * DF + DF)
                if h:
                    pe.wait_ge(S["fb_evac"], h)
                mm(PS[:, 0, :], sel8[:, h * P:(h + 1) * P], ncf[:, 0:SEQ], start=True, stop=True)\
                    .then_inc(S["fb_done"], 1)
                for i in range(ST):
                    if h:
                        pe.wait_ge(S["f_max"], (h - 1) * ST + i + 1)
                    mm(PS[:, 1 + i, 0:(i + 1) * P], PT[rows, QF + h // 2, i * P:(i + 1) * P],
                       PT[rows, KF + h // 2, 0:(i + 1) * P], start=True, stop=True).then_inc(S["fs_done"], 1)

            def fox_outputs(h):
                def turn(j):
                    n = h * ST + j
                    if n >= 2:
                        pe.wait_ge(S["ft_evac"], n - 1)
                    for t in range(j, ST):
                        last = nc.tensor.transpose(PS[:, 5 + j % 2, t * P:(t + 1) * P], pp[:, t, j * P:(j + 1) * P],
                                                   ident)
                    last.then_inc(S["ft_done"], 1)

                def weigh_values(j):
                    pe.wait_ge(S["ft_evac"], h * ST + j + 1)
                    mm(PS[0:DF, 7, j * P:SEQ], fnat[:, j, h * DF:(h + 1) * DF], pts[:, j % 2, j * P:SEQ],
                       start=(j == 0), stop=(j == ST - 1)).then_inc(S["fo_done"], 1)

                pe.wait_ge(S["f_pn"], (h + 1) * ST)
                turn(0)
                turn(1)
                if h:
                    pe.wait_ge(S["fo_evac"], h)
                weigh_values(0)
                turn(2)
                weigh_values(1)
                turn(3)
                weigh_values(2)
                weigh_values(3)

            fox_scores(0)
            for h in range(HF):
                if h + 1 < HF:
                    fox_scores(h + 1)
                fox_outputs(h)

            pe.wait_ge(S["fo_evac"], HF)
            pe.wait_ge(S["f_max"], HF * ST)
            pe.wait_ge(S["new_copied"], 3)

            def sample(b, qk, pv, ot):
                for c in range(CH):
                    if pv:
                        m = (b - 1) * CH + c
                        pe.wait_ge(S["p_ready"], m + 1)
                        if not (isinstance(b, int) and b == 1 and c < 3):
                            pe.wait_ge(S["pt_evac"], m - 2)
                        hold_here(pe)
                        for g in range(PC if c < NCH else 1):
                            w = P if c < NCH else NS
                            k0 = c * 512 + g * P
                            last = nc.tensor.transpose(PS[0:w, 3 + c % 3, g * NS:(g + 1) * NS],
                                                       probs[0:NS, k0:k0 + w], ident[0:NS, 0:NS])
                        last.then_inc(S["pt_done"], 1)
                    if qk:
                        n = b * CH + c
                        if c == 0:
                            pe.wait_ge(S["q_ready"], 2 * b + 2)
                        if c < NCH:
                            pe.wait_ge(k_in[c % 4], 16 * PC * (2 * b + (c // 4 + 1)))
                        if not (isinstance(b, int) and b == 0 and c < 3):
                            pe.wait_ge(S["sc_evac"], n - 2)
                        w = PC * PAGE if c < NCH else NS
                        for j in range(NJ):
                            keys = kring[c % 4][:, :, j, :] if c < NCH else kf_new[:, j, :]
                            last = mm(PS[0:NS, c % 3, 0:w], qbd[:, j, :], keys, start=(j == 0), stop=(j == NJ - 1))
                        last.then_inc(S["sc_done"], 1)
                    if ot and c == 1:
                        turn_out(b - 2)
                    if pv and c >= 1:
                        values(b - 1, c - 1)
                if pv:
                    values(b - 1, NCH)

            def values(b, c):
                pe.wait_ge(S["pt_evac"], b * CH + c + 1)
                if c == 0 and not (isinstance(b, int) and b == 0):
                    pe.wait_ge(S["o_ready"], b)
                if c < NCH:
                    pe.wait_ge(v_in[c % 4], 16 * PC * (2 * b + (c // 4 + 1)))
                hold_here(pe)
                for g in range(PC if c < NCH else 1):
                    if c < NCH:
                        p_t, vals = ptile[:, c % 3, g * NS:(g + 1) * NS], vring[c % 4][:, g, :]
                    else:
                        p_t, vals = ptile[0:NS, c % 3, 0:NS], vf_new[:, :]
                    last = mm(PS[0:NS, 6, :], p_t, vals, start=(c == 0 and g == 0), stop=(c == NCH))
                last.then_inc(S["pv_done"], 1)

            def turn_out(b):
                pe.wait_ge(S["o_ready"], b + 1)
                if not (isinstance(b, int) and b == 0):
                    pe.wait_ge(S["ot_evac"], 2 * b)
                hold_here(pe)
                for j in range(NJ):
                    last = nc.tensor.transpose(PS[:, 7, j * NS:(j + 1) * NS], osb[:, j * P:(j + 1) * P],
                                               ident[0:NS, 0:NS])
                last.then_inc(S["ot_done"], 1)

            sample(0, True, False, False)
            sample(1, True, True, False)
            with pe.Fori(2, DB) as b:
                sample(b, True, True, True)
            sample(DB, False, True, True)
            turn_out(DB - 1)

            pe.wait_ge(S["ot_evac"], 2 * DB)
            pe.wait_ge(S["fo_evac"], HF)
            pe.wait_ge(S["mmix"], HM)
            with pe.Fori(0, U_OUT // 2) as i:
                project(i, range(2), wring, hT, KT, U0_OUT, T0_OUT, True)
            ssq(1)
            pe.wait_ge(S["h_ready"], 2 * KT)
            with pe.Fori(0, FT // 2) as i:
                for s in range(2):
                    pe.wait_ge(w_in[s], 16 * i + (8 * U0_GU + 16))
                    pe.wait_ge(S["tile_evac"], 2 * i + (NT_IN + KT + s - 1))
                    w = wring[s][:, 0:2 * KT * P].rearrange("p (a k n) -> p a k n", a=2, k=KT)
                    for t in range(2):
                        product(4 * s + 2 * t, lambda kt: w[:, t, kt, :], hT, KT).then_inc(S["tile_done"], 1)
            pe.wait_ge(S["tile_evac"], NT_IN + KT + FT)
            with pe.Fori(0, U_DN // 2) as i:
                for s in range(2):
                    pe.wait_ge(w_in[s], 16 * i + (8 * U0_DN + 16))
                    pe.wait_ge(S["tile_evac"], 2 * i + (NT_IN + KT + FT + s - 1))
                    w = wring[s][:, 0:FT * P].rearrange("p (k n) -> p k n", k=FT)
                    product(2 * s, lambda kt: w[:, kt, :], act_ff, FT).then_inc(S["tile_done"], 1)
            ssq(2)


def kernel(**inputs):
    import concourse.bacc as bacc
    from concourse.bass_utils import run_bass_kernel_spmd

    f = {k: np.asarray(v) for k, v in inputs.items()}

    def tiles(w):
        return w.reshape(w.shape[0] // P, P, w.shape[1]).transpose(1, 0, 2)

    def units(w, width):
        k, n = w.shape
        return w.reshape(k // P, P, n // width, width).transpose(2, 1, 0, 3).reshape(n // width, P, -1)

    w_in = f["w_in"][0]
    g0, f0 = 4 * HM * DM, 4 * HM * DM + 2 * HM
    wgate = np.zeros((D, GR), np.float32)
    wgate[:, 0:HM] = w_in[:, g0:g0 + HM]
    wgate[:, ROWS_F:ROWS_F + HM] = w_in[:, g0 + HM:g0 + 2 * HM]
    wgate[:, ROWS_FF:ROWS_FF + HF] = w_in[:, f0 + 3 * HF * DF:]
    gbias = np.zeros((GR, 1), np.float32)
    gbias[0:HM, 0] = f["b_m_igate"][0]
    gbias[ROWS_F:ROWS_F + HM, 0] = f["b_m_fgate"][0]
    gbias[ROWS_FF:, 0] = f["b_f_fgate"][0]
    cols = np.concatenate([w_in[:, :g0], w_in[:, f0:f0 + 3 * HF * DF]], axis=1)
    wide, rows = constants()
    gu = np.stack([units(f["w_gate"][0], P), units(f["w_up"][0], P)], axis=2)
    x = np.concatenate([f["x_prompt"].reshape(SEQ, D), f["x_sample"].reshape(NS, D)], axis=0)
    pool_k, pool_v, pool_f = f["cache_fox_k"][0], f["cache_fox_v"][0], f["cache_fox_logf"][0]
    npool = pool_k.shape[0]
    table = f["page_table"].reshape(-1)
    arrays = {
        "x": x.T.reshape(KT, P, T).transpose(1, 0, 2),
        "wide": wide,
        "rows": rows,
        "gains": np.concatenate([f["norm_mix_g"].reshape(KT, P), f["norm_ffn_g"].reshape(KT, P),
                                 f["norm_final_g"].reshape(KT, P), f["mlstm_head_g"].reshape(HM, P)]).T,
        "wgate": tiles(wgate),
        "gbias": gbias,
        "win": units(cols, UNIT_W),
        "wout": units(f["w_out"][0], UNIT_W),
        "wgu": gu.reshape(FT, P, -1),
        "wdown": units(f["w_down"][0], P),
        "ptab": table.reshape(1, -1),
        "pidx": table.reshape(2, P).T,
        "m": f["state_mlstm_m"][0].T,
        "n": f["state_mlstm_n"][0].transpose(2, 1, 0),
        "C": f["state_mlstm_C"][0].transpose(3, 1, 0, 2),
        "K": pool_k.reshape(npool, PAGE, NJ, 2 * DF).transpose(0, 3, 2, 1).reshape(npool, P, NJ * PAGE),
        "V": pool_v.reshape(npool, PAGE, HF * DF),
        "logf": pool_f.transpose(0, 2, 1).reshape(npool, HF * PAGE),
    }
    outs = {
        "o_y": (P, KT, T), "o_kf": (P, NJ, T), "o_vf": (P, NJ, T), "o_logf": (HF, T), "o_m": (HM, 1 + DB),
        "o_C": (P, HM, DB, DM), "o_n": (P, HM, DB), "o_Cp": (P, HM, DM + 1),
    }
    nc = bacc.Bacc("TRN2", target_bir_lowering=False, num_devices=1)
    arrays = {k: np.ascontiguousarray(a) for k, a in arrays.items()}
    A = {k: nc.dram_tensor("in_" + k, a.shape, mybir.dt.from_np(a.dtype), kind="ExternalInput").ap()
         for k, a in arrays.items()}
    for k, s in outs.items():
        A[k] = nc.dram_tensor(k, s, F32, kind="ExternalOutput").ap()
    A["npool"] = npool
    build(nc, A)
    got = run_bass_kernel_spmd(nc, [{"in_" + k: a for k, a in arrays.items()}], core_ids=[0]).results[0]

    def tokens(a):
        a = a.transpose(2, 1, 0).reshape(T, -1)
        return a[:SEQ], a[SEQ:].reshape(DB, DS, -1)

    y, kf, vf = tokens(got["o_y"]), tokens(got["o_kf"]), tokens(got["o_vf"])
    lf = got["o_logf"].T
    m, n, c, cp = got["o_m"], got["o_n"], got["o_C"], got["o_Cp"]
    return (y[0].reshape(1, SEQ, D), y[1],
            kf[0].reshape(1, 1, SEQ, HF, DF), vf[0].reshape(1, 1, SEQ, HF, DF), lf[:SEQ].reshape(1, 1, SEQ, HF),
            cp[:, :, :DM].transpose(1, 2, 0).reshape(1, 1, HM, DM, DM), cp[:, :, DM].T.reshape(1, 1, HM, DM),
            m[:, 0].reshape(1, 1, HM),
            kf[1].reshape(1, DB, DS, HF, DF), vf[1].reshape(1, DB, DS, HF, DF),
            lf[SEQ:].reshape(1, DB, DS, HF),
            c.transpose(2, 1, 3, 0).reshape(1, DB, HM, DM, DM), n.transpose(2, 1, 0).reshape(1, DB, HM, DM),
            m[:, 1:].T.reshape(1, DB, HM))
```

```python
from contextlib import ExitStack

import numpy as np

import concourse.bass as bass
from concourse import mybir

F32 = mybir.dt.float32
F32R = mybir.dt.float32r
I32 = mybir.dt.int32
ALU = mybir.AluOpType
ACT = mybir.ActivationFunctionType
AX = mybir.AxisListType

P = 128
D = 1024
KT = D // P
SEQ, DB, DS = 512, 8, 8
NS = DB * DS
T = SEQ + NS
TH = T // 2
ST = SEQ // P
HM, DM = 4, 128
HF, DF = 8, 64
NJ = HF // 2
DFF = 2816
FT = DFF // P
PAGES, PAGE = 32, 128
PC = 4
NCH = PAGES // PC
CH = NCH + 1
PAST = PAGES * PAGE
EPS = 1e-6
NEG = -1e30
ROWS_F, ROWS_FF = 32, 64
GR = ROWS_FF + HF

QM, KM, VM, OM, QF, KF, VF = 0, 4, 8, 12, 16, 20, 24
NT_IN = 28
WT = KT * P
WSLOT = 2 * WT
ROUNDS = (12, 10)
U0_OUT = NT_IN
U0_FF = NT_IN + KT
H_AT, X_AT, W_AT = 0, 2 * KT * T, 3 * KT * T
PT_AT = W_AT + 6 * WT
ROWS_AT = PT_AT + NT_IN * T
ACT_AT = W_AT + 6 * WSLOT
STAGE_AT = ACT_AT + 2 * ROUNDS[0] * T
ARENA = STAGE_AT + 2 * T + 448
HALF, OTHER_HALF = range(0, PC // 2), range(PC // 2, PC)
OUT_EARLY = 7


def constants():
    s, t = np.arange(P)[:, None], np.arange(P)[None, :]
    causal_t = np.where(s <= t, 0.0, NEG)
    causal_n = np.where(t <= s, 0.0, NEG)
    s6, t6 = np.arange(NS)[:, None], np.arange(NS)[None, :]
    causal_s = np.full((P, NS), NEG)
    causal_s[:NS] = np.where((s6 <= t6) & (s6 // DS == t6 // DS), 0.0, NEG)
    block = np.zeros((P, DB))
    block[:NS] = s6 // DS == np.arange(DB)[None, :]
    new_mask = np.full((P, DB, NS), NEG)
    for b in range(DB):
        for q in range(DS):
            for h in range(HF):
                new_mask[h * DS + q, b, b * DS:b * DS + q + 1] = 0.0
    suffix = (s >= t) & (s // PAGES == t // PAGES)
    fold = np.concatenate([np.eye(NS), np.eye(NS)])
    wide = np.concatenate([np.eye(P), causal_t, causal_n, causal_s, block, new_mask.reshape(P, -1),
                           suffix, np.ones((P, P)), fold], axis=1).astype(np.float32)
    sel4 = np.zeros((HM, HM, P))
    sel4[np.arange(HM), np.arange(HM)] = 1.0
    sel8 = np.zeros((HF, HF, P))
    sel8[np.arange(HF), np.arange(HF)] = 1.0
    selq = np.repeat(np.eye(HF), DS, axis=1)
    reset = np.ones(T)
    reset[0] = 0.0
    reset[SEQ::DS] = 0.0
    rows = np.zeros((HF, HM * P + HF * P + NS + 2 * T))
    rows[:HM, :HM * P] = sel4.reshape(HM, -1)
    rows[:, HM * P:HM * P + HF * P] = sel8.reshape(HF, -1)
    rows[:, HM * P + HF * P:HM * P + HF * P + NS] = selq
    rows[:, HM * P + HF * P + NS:HM * P + HF * P + NS + T] = reset
    rows[:, HM * P + HF * P + NS + T:] = (1.0 - reset) * NEG
    return wide, rows.astype(np.float32)


WIDE_COLS = 3 * P + NS + DB + DB * NS + 2 * P + NS
ROW_COLS = HM * P + HF * P + NS + 2 * T


def build(nc, A):
    ctx = ExitStack()
    with ctx:
        def sb(name, shape, dt=F32):
            return ctx.enter_context(nc.sbuf_tensor(name, shape, dt))

        def sem(name):
            return ctx.enter_context(nc.semaphore(name))

        PS = ctx.enter_context(nc.psum_tensor("PS", [P, 8, 512], F32))

        wide = sb("wide", [P, WIDE_COLS])
        rowc = sb("rowc", [HF, ROW_COLS])
        gains = sb("gains", [P, 3 * KT + HM])
        epsc = sb("epsc", [P, 1])
        o = 0
        ident = wide[:, o:o + P]; o += P
        causal_t = wide[:, o:o + P]; o += P
        causal_n = wide[:, o:o + P]; o += P
        causal_s = wide[:, o:o + NS]; o += NS
        block_of = wide[:, o:o + DB]; o += DB
        new_mask = wide[:, o:o + DB * NS].rearrange("p (b k) -> p b k", b=DB); o += DB * NS
        suffix = wide[:, o:o + P]; o += P
        ones = wide[:, o:o + P]; o += P
        fold = wide[:, o:o + NS]
        o = 0
        sel4 = rowc[0:HM, o:o + HM * P]; o += HM * P
        sel8 = rowc[:, o:o + HF * P]; o += HF * P
        selq = rowc[:, o:o + NS]; o += NS
        keep = rowc[:, o:o + T]; o += T
        drop = rowc[:, o:o + T]

        qbd = sb("qbd", [P, 2, NJ, NS])
        kf_new = sb("kf_new", [P, NJ, NS])
        qf_new = sb("qf_new", [P, NJ, NS])
        vf_new = sb("vf_new", [NS, HF * DF])
        bias_new = sb("bias_new", [NS, DB, NS])
        ptab = sb("ptab", [1, DB * PAGES], I32)
        pidx = sb("pidx", [P, 2], I32)
        pgs = sb("pgs", [P, 2, HF])
        gbias = sb("gbias", [GR, 1])
        wg = sb("wg", [P, KT, GR])
        m_top = sb("m_top", [HM, T])
        emt = sb("emt", [HM, T])
        winter = sb("winter", [HM, NS])
        ca = sb("ca", [ROWS_F + HM, T])
        cat = sb("cat", [P, ST + 1, ROWS_F + HM])
        lff = sb("lff", [HF, T])
        ncf = sb("ncf", [HF, T])
        mst = sb("mst", [HM, DB])
        dec = sb("dec", [HM, DB])
        nml = sb("nml", [HM, 1])
        mout = sb("mout", [HM, 1 + DB])
        decb = sb("decb", [P, HM, DB])
        nst = sb("nst", [P, HM, DB])
        nnew = sb("nnew", [P, HM, DB])
        ctp = sb("ctp", [P, HM, DM + 1])
        smx = sb("smx", [NS, CH])
        snm = sb("snm", [NS, 2])
        ssum = sb("ssum", [NS, CH])
        sri = sb("sri", [P, 2])
        osb = sb("osb", [P, HF * DF])
        fmx = sb("fmx", [P, 5, ST])

        base = -(-nc.sbuf_base // 32) * 32
        arena = sb("arena", [P, ARENA])
        assert nc.sbuf_base == base + 4 * ARENA
        at = [0]

        def take(words):
            at[0] += words
            assert at[0] <= ARENA, at[0]
            return arena[:, at[0] - words:at[0]]

        def rounded(name, words):
            at[0] += words
            assert at[0] <= ARENA, at[0]
            return nc.alloc_sbuf_tensor_at(name, [P, words], F32R, offset=base + 4 * (at[0] - words))[:, :]

        at[0] = H_AT
        h_hi = rounded("h_hi", KT * T).rearrange("p (k t) -> p k t", k=KT)
        h_lo = rounded("h_lo", KT * T).rearrange("p (k t) -> p k t", k=KT)
        at[0] = H_AT
        y = take(KT * T).rearrange("p (k t) -> p k t", k=KT)
        at[0] = X_AT
        xT = take(KT * T).rearrange("p (k t) -> p k t", k=KT)
        mixT = xT
        at[0] = W_AT
        w_raw_in = [take(WT) for _ in range(2)]
        w_hi_in = [rounded(f"w_hi_in{i}", WT) for i in range(2)]
        w_lo_in = [rounded(f"w_lo_in{i}", WT) for i in range(2)]
        assert at[0] == PT_AT
        PT = take(NT_IN * T).rearrange("p (n t) -> p n t", n=NT_IN)
        at[0] = X_AT
        lg = take(2 * HF * PAGE).rearrange("p (a h k) -> p a h k", a=2, h=HF)
        gu, gd = (take(T)[0:GR] for _ in range(2))
        at[0] = ROWS_AT
        gx, ge = (take(T)[0:GR] for _ in range(2))
        li, lfm, bm, mt, mprev, a0 = (take(T)[0:HM] for _ in range(6))
        at[0] = ACT_AT
        sq = take(2 * T).rearrange("p (a t) -> p a t", a=2)
        rb = take(T)
        at[0] = H_AT
        knat, vnat, fnat = (take((ST + 1) * 512).rearrange("p (i c) -> p i c", i=ST + 1) for _ in range(3))
        at[0] = W_AT
        ctm = take(HM * DB * DM).rearrange("p (h b v) -> p h b v", h=HM, b=DB)
        at[0] = ROWS_AT
        me = take(2 * 512).rearrange("p (i t) -> p i t", i=2)
        mstt = take(2 * 512).rearrange("p (i t) -> p i t", i=2)
        da = take(T); dr = take(T); hh = take(T)
        gm = take(2 * P).rearrange("p (i t) -> p i t", i=2)
        at[0] = PT_AT + VM * T
        nmb = take(T); emb = take(T); hs = take(T)
        vw = take(ST * (P + 1)).rearrange("p (i c) -> p i c", i=ST)
        assert at[0] <= PT_AT + OM * T
        at[0] = PT_AT + VF * T
        wib = take(NS); nq = take(NS); ts1 = take(NS); ts2 = take(NS); hn = take(NS)
        wm = take(DB)
        vmk = take(DB * P).rearrange("p (b v) -> p b v", b=DB)
        assert at[0] <= ROWS_AT
        at[0] = ROWS_AT
        ncb = take(512)
        ncm = take(512).rearrange("p (i s) -> p i s", i=ST)
        pts = take(2 * 512).rearrange("p (i s) -> p i s", i=2)
        at[0] = H_AT
        scp = take(ST * 512).rearrange("p (i s) -> p i s", i=ST)
        pp = take(ST * 512).rearrange("p (i s) -> p i s", i=ST)
        assert at[0] <= H_AT + 2 * (ST + 1) * 512
        at[0] = H_AT
        kring = [take(PC * NJ * P).rearrange("p (g j k) -> p g j k", g=PC, j=NJ) for _ in range(4)]
        vn_hi = rounded("vn_hi", HF * DF)
        vn_lo = rounded("vn_lo", HF * DF)
        assert at[0] <= X_AT
        at[0] = W_AT
        vring = [take(PC * 512).rearrange("p (g c) -> p g c", g=PC) for _ in range(4)]
        at[0] = W_AT
        v_lo = [rounded(f"v_lo{i}", PC * 512).rearrange("p (g c) -> p g c", g=PC) for i in range(4)]
        v_hi = [rounded(f"v_hi{i}", PC * 512).rearrange("p (g c) -> p g c", g=PC) for i in range(2)]
        p_t = [rounded(f"p_t{i}", PC * P).rearrange("p (g c) -> p g c", g=PC) for i in range(3)]
        scores = take(PAST + NS)
        probs = take(3 * PC * PAGE).rearrange("p (a k) -> p a k", a=3)
        bias = [take(PAST) for _ in range(2)]
        at[0] = W_AT
        w_raw = [take(WSLOT) for _ in range(2)]
        w_hi = [rounded(f"w_hi{i}", WSLOT) for i in range(2)]
        w_lo = [rounded(f"w_lo{i}", WSLOT) for i in range(2)]
        assert at[0] == ACT_AT
        act_hi = rounded("act_hi", ROUNDS[0] * T).rearrange("p (n t) -> p n t", n=ROUNDS[0])
        act_lo = rounded("act_lo", ROUNDS[0] * T).rearrange("p (n t) -> p n t", n=ROUNDS[0])
        stage = take(2 * T).rearrange("p (a t) -> p a t", a=2)

        bscr = nc.dram_tensor("bias_scratch", [DB, HF, PAST], F32, kind="Internal").ap()

        names = """const_in x_in0 x_in1 x_in2 x_in3 x_again small_in state_in idx_in lg_in w_in0 w_in1
            k_in0 k_in1 k_in2 k_in3 k_first0 k_first1 k_first2 k_first3
            v_last0 v_last1 v_last2 v_last3 v_in0 v_in1 v_in2 v_in3 bias_in0 bias_in1 bias_out out_dma zeroed
            sq_ready sq_used root_done rinv_done h_ready
            gate_evac gate_step gate_act rows_ready rows_act wg_used page_step page_sum page_done
            unit_done gate_done tile_evac silu_done act_ready act_hi_done act_done wh_ready wl_ready nh_ready nhi_ready mixed sig_ready qk_scaled new_copied
            nat_done nat_out_v nat_out_s cat_done cat_evac newb_ready
            mb_done mb_evac vw_ready mg_ready me_ready ms_done mst_ready mnd_done mint_done mden_ready
            mda_ready mdv hs_ready mss_done mroot mmix ct_done ct_out
            fb_done fb_evac fs_done f_dve f_max f_exp f_pn ft_done ft_evac fo_done fo_evac
            q_ready sc_done sc_evac max_step mx_ready p_ready pt_done ph_ready pl_ready vh_ready vl_ready vn_ready
            sum_read sum_ready pv_done o_ready ot_done ot_evac
            y_ready y_out passed""".split()
        S = {n: sem(n) for n in names}
        x_in = [S[f"x_in{i}"] for i in range(4)]
        w_in = [S["w_in0"], S["w_in1"]]
        k_in = [S[f"k_in{i}"] for i in range(4)]
        v_in = [S[f"v_in{i}"] for i in range(4)]
        k_first = [S[f"k_first{i}"] for i in range(4)]
        v_last = [S[f"v_last{i}"] for i in range(4)]
        bias_in = [S["bias_in0"], S["bias_in1"]]

        def pair(b):
            return PS[:, b:b + 2, 0:TH]

        def halves(ap):
            return ap.rearrange("p (a t) -> p a t", a=2)

        def stepped(ap, offset, dims):
            return bass.AP(ap.tensor, ap.offset + offset, [ap.ap[0], *dims])

        def hold_here(eng):
            eng.sem_inc(S["passed"], 1)

        def pages(eng, ring, sems, cache, b, c, part=range(PC)):
            hold_here(eng)
            slot = c % 4
            for g in part:
                pg = eng.value_load(ptab[0:1, bass.ds(b * PAGES + c * PC + g, 1)], min_val=0,
                                    max_val=A["npool"] - 1)
                dst = ring[slot][:, g]
                if cache is A["K"]:
                    dst = dst.rearrange("p j k -> p (j k)")
                eng.dma_start(dst, cache[bass.ds(pg, 1), :, :].rearrange("a p n -> p (a n)"))\
                   .then_inc(sems[slot], 16)

        blk = ctx.enter_context(nc.Block())

        @blk.sync
        def _(sp):
            for i in range(4):
                sp.dma_start(xT[:, 2 * i:2 * i + 2, :], A["x"][:, 2 * i:2 * i + 2, :]).then_inc(x_in[i], 16)
            sp.dma_start(wide[:, :], A["wide"]).then_inc(S["const_in"], 16)
            sp.dma_start(rowc[:, :], A["rows"]).then_inc(S["const_in"], 16)
            sp.dma_start(gains[:, :], A["gains"]).then_inc(S["const_in"], 16)
            sp.dma_start(wg[:, :, :], A["wgate"]).then_inc(S["small_in"], 16)
            sp.dma_start(gbias[:, :], A["gbias"]).then_inc(S["small_in"], 16)
            sp.dma_start(ptab[:, :], A["ptab"]).then_inc(S["small_in"], 16)
            sp.dma_start(mst[:, :], A["m"]).then_inc(S["small_in"], 16)
            sp.dma_start(nst[:, :, :], A["n"]).then_inc(S["small_in"], 16)

            def stream(slots, src, n, words, u0, then=lambda: None):
                def load(i, s):
                    v = i * 2 + (u0 + s - 1)
                    if not (isinstance(i, int) and v < 1):
                        sp.wait_ge(S["wl_ready"], v)
                    a = src[i * 2 + s] if isinstance(i, int) else \
                        src[bass.ds(i * 2 + s, 1), :, :].rearrange("a p n -> p (a n)")
                    sp.dma_start(slots[s][:, 0:words], a).then_inc(w_in[s], 16)

                for s in range(2):
                    load(0, s)
                then()
                with sp.Fori(1, n // 2) as i:
                    for s in range(2):
                        load(i, s)

            stream(w_raw_in, A["win"], NT_IN, WT, 0)
            sp.wait_ge(S["unit_done"], NT_IN)
            sp.dma_start(ctm[:, :, :, :], A["C"]).then_inc(S["state_in"], 16)

            def load_keys(b, c):
                if c >= 4:
                    sp.wait_ge(S["sc_done"], b * CH + c - 3)
                elif not (isinstance(b, int) and b == 0):
                    sp.wait_ge(S["sc_done"], (b - 1) * CH + c + 5)
                pages(sp, kring, k_in, A["K"], b, c, HALF if isinstance(b, int) and b == 0 else range(PC))

            def load_bias(b, par, wait):
                if wait:
                    sp.wait_ge(S["sc_evac"], (b - 1) * CH)
                for h in range(HF):
                    src = bass.AP(bscr.tensor, b * (HF * PAST) + h * PAST, [[0, DS], [1, PAST]])
                    sp.dma_start(bias[par][h * DS:(h + 1) * DS, :], src).then_inc(bias_in[par], 16)

            sp.wait_ge(S["small_in"], 5 * 16)
            sp.wait_ge(S["bias_out"], 8 * 16)
            sp.wait_ge(S["fo_done"], HF * ST)
            sp.wait_ge(S["fo_evac"], HF)
            sp.wait_ge(S["new_copied"], 3)
            sp.wait_ge(S["out_dma"], 16 * OUT_EARLY)
            load_keys(0, 0)
            load_bias(0, 0, False)
            load_bias(1, 1, False)
            for c in range(1, NCH):
                load_keys(0, c)

            def batch(b, next_par):
                for c in range(NCH):
                    load_keys(b, c)
                    if c == 3 and next_par is not None:
                        load_bias(b + 1, next_par, True)

            batch(1, 0)
            with sp.Fori(1, DB // 2 - 1) as i:
                batch(2 * i, 1)
                batch(2 * i + 1, 0)
            batch(DB - 2, 1)
            batch(DB - 1, None)
            for c in range(NCH):
                sp.wait_ge(S["pv_done"], (DB - 1) * CH + c - 3 if c >= 4 else (DB - 2) * CH + c + 5)
                pages(sp, vring, v_last, A["V"], DB - 1, c, OTHER_HALF)

            sp.wait_ge(S["pv_done"], DB * CH)

            def x_again():
                sp.wait_ge(S["mixed"], KT)
                sp.dma_start(xT[:, :, :], A["x"]).then_inc(S["x_again"], 16)

            stream(w_raw, A["wout"], KT, WT, U0_OUT, x_again)
            u0 = U0_FF
            for r, n in enumerate(ROUNDS):
                stream(w_raw, A[f"wgu{r}"], n, 2 * WT, u0)
                stream(w_raw, A[f"wdown{r}"], KT, n * P, u0 + n)
                u0 += n + KT
            for kt in range(KT):
                sp.wait_ge(S["y_ready"], kt + 1)
                sp.dma_start(A["o_y"][:, kt, :], y[:, kt, :]).then_inc(S["y_out"], 16)
            sp.wait_ge(S["y_out"], KT * 16)

        @blk.gpsimd
        def _(pool):
            nc.gpsimd.memset(epsc[:, :], EPS).then_inc(S["zeroed"], 1)
            nc.gpsimd.memset(ca[:, :], 0.0).then_inc(S["zeroed"], 1)
            nc.gpsimd.memset(qbd[:, :, :, :], 0.0).then_inc(S["zeroed"], 1)
            pool.dma_start(pidx[:, :], A["pidx"]).then_inc(S["idx_in"], 16)
            pool.wait_ge(S["idx_in"], 16)

            def split_low(i, s, raw, hi, lo, words, u0):
                u = i * 2 + (u0 + s)
                pool.wait_ge(S["wh_ready"], u + 1)
                nc.gpsimd.tensor_tensor(lo[s][:, 0:words], raw[s][:, 0:words], hi[s][:, 0:words].bitcast(F32),
                                        ALU.subtract).then_inc(S["wl_ready"], 1)

            def split_lows(n, raw, hi, lo, words, u0, first=0):
                with pool.Fori(first, n // 2) as i:
                    for s in range(2):
                        split_low(i, s, raw, hi, lo, words, u0)

            for s in range(2):
                split_low(0, s, w_raw_in, w_hi_in, w_lo_in, WT, 0)
            pool.wait_ge(S["nh_ready"], KT)
            for half in range(2):
                nc.gpsimd.indirect_dma_start(
                    lg[:, half, :, :].rearrange("p h k -> p (h k)"), None, A["logf"],
                    bass.IndirectOffsetOnAxis(ap=pidx[:, half:half + 1], axis=0)).then_inc(S["lg_in"], 16)
            split_lows(NT_IN, w_raw_in, w_hi_in, w_lo_in, WT, 0, first=1)

            pool.wait_ge(S["page_done"], 1)
            for b in range(DB):
                pool.dma_start(bscr[b].rearrange("h (g k) -> g h k", g=PAGES),
                               lg[(b % 4) * PAGES:(b % 4 + 1) * PAGES, b // 4, :, :]).then_inc(S["bias_out"], 16)
            pool.wait_ge(S["rows_ready"], 1)
            pool.dma_start(A["o_logf"], lff[:, :]).then_inc(S["out_dma"], 16)
            pool.dma_start(A["o_m"], mout[:, :]).then_inc(S["out_dma"], 16)
            pool.wait_ge(S["tile_evac"], NT_IN)
            pool.dma_start(A["o_kf"], PT[:, KF:KF + NJ, :]).then_inc(S["out_dma"], 16)
            pool.dma_start(A["o_vf"], PT[:, VF:VF + NJ, :]).then_inc(S["out_dma"], 16)
            pool.wait_ge(S["ct_out"], HM)
            pool.dma_start(A["o_C"], ctm[:, :, :, :]).then_inc(S["out_dma"], 16)
            pool.dma_start(A["o_n"], nnew[:, :, :]).then_inc(S["out_dma"], 16)
            pool.dma_start(A["o_Cp"], ctp[:, :, :]).then_inc(S["out_dma"], 16)

            pool.wait_ge(S["new_copied"], 2)
            pool.wait_ge(S["zeroed"], 3)

            def queries(b, par):
                if not (isinstance(b, int) and b < 2):
                    pool.wait_ge(S["sc_done"], (b - 1) * CH)
                for p2 in range(2):
                    rows = slice(p2 * DF, p2 * DF + DF)
                    dst = stepped(qbd[rows, par, :, :], p2 * DS, [[NS + 2 * DS, NJ], [1, DS]])
                    nc.gpsimd.tensor_copy(dst, qf_new[rows, :, bass.ds(b * DS, DS)]).then_inc(S["q_ready"], 1)

            queries(0, 0)
            queries(1, 1)
            pool.wait_ge(S["fo_done"], HF * ST)
            pool.wait_ge(S["fo_evac"], HF)
            pool.wait_ge(S["new_copied"], 3)
            pool.wait_ge(S["out_dma"], 16 * OUT_EARLY)

            for c in range(NCH):
                if c >= 4:
                    pool.wait_ge(S["sc_done"], c - 3)
                pages(pool, kring, k_first, A["K"], 0, c, OTHER_HALF)

            def batch(b, par):
                for c in range(NCH):
                    if c >= 4:
                        pool.wait_ge(S["pv_done"], b * CH + c - 3)
                    elif not (isinstance(b, int) and b == 0):
                        pool.wait_ge(S["pv_done"], (b - 1) * CH + c + 5)
                    pages(pool, vring, v_in, A["V"], b, c, HALF if isinstance(b, int) and b == DB - 1 else range(PC))
                    if c == 2 and par is not None:
                        queries(b + 2, par)

            batch(0, 0)
            batch(1, 1)
            with pool.Fori(1, DB // 2 - 1) as i:
                batch(2 * i, 0)
                batch(2 * i + 1, 1)
            batch(DB - 2, None)
            batch(DB - 1, None)

            split_lows(KT, w_raw, w_hi, w_lo, WT, U0_OUT)
            u0 = U0_FF
            for n in ROUNDS:
                split_lows(n, w_raw, w_hi, w_lo, 2 * WT, u0)
                split_lows(KT, w_raw, w_hi, w_lo, n * P, u0 + n)
                u0 += n + KT

        @blk.scalar
        def _(act):
            a = nc.scalar

            def root(n):
                act.wait_ge(S["sq_used"], KT * (n + 1))
                a.activation(halves(rb[:, :]), pair(4), ACT.Sqrt, bias=epsc[:, 0:1], scale=1.0 / D)\
                    .then_inc(S["root_done"], 1)

            act.wait_ge(S["zeroed"], 2)
            root(0)
            def split_high(u, s, raw, hi, words, first=False):
                act.wait_ge(w_in[s], (u - s) * 8 + 16)
                if not first:
                    act.wait_ge(S["unit_done"], u - 1)
                    act.wait_ge(S["wl_ready"], u - 1)
                a.copy(hi[s][:, 0:words], raw[s][:, 0:words]).then_inc(S["wh_ready"], 1)

            def normalised(n):
                for kt in range(KT):
                    act.wait_ge(S["nh_ready"], n * KT + kt + 1)
                    a.copy(h_hi[:, kt, :], sq[:, kt % 2, :]).then_inc(S["nhi_ready"], 1)

            split_high(0, 0, w_raw_in, w_hi_in, WT, True)
            split_high(1, 1, w_raw_in, w_hi_in, WT, True)
            normalised(0)
            act.wait_ge(S["gate_step"], 1)
            a.activation(ge, gu, ACT.Exp).then_inc(S["gate_act"], 1)
            act.wait_ge(S["gate_step"], 3)
            a.activation(gu, gu, ACT.Ln).then_inc(S["gate_act"], 1)

            def projected(i, ahead):
                for t in range(4):
                    u = i * 4 + t
                    if t < ahead:
                        split_high(u + 2, t % 2, w_raw_in, w_hi_in, WT)
                    act.wait_ge(S["unit_done"], u + 1)
                    dst = PT[:, bass.ds(u, 1), :].rearrange("p a (g t) -> p (a g) t", g=2)
                    a.copy(dst, pair(2 * t)).then_inc(S["tile_evac"], 1)

            with act.Fori(0, NT_IN // 4 - 1) as i:
                projected(i, 4)
            projected(NT_IN // 4 - 1, 2)

            act.wait_ge(S["tile_evac"], NT_IN)
            act.wait_ge(S["rows_ready"], 1)
            a.activation(emt[:, :], mt, ACT.Exp, scale=-1.0)
            a.activation(winter[:, :], mprev[:, SEQ:T], ACT.Exp)
            a.activation(dec[:, :], dec[:, :], ACT.Exp)
            a.activation(ca[0:HM, 0:SEQ], a0[:, 0:SEQ], ACT.Exp, bias=nml[:, 0:1])
            a.activation(ca[0:HM, SEQ:T], a0[:, SEQ:T], ACT.Exp).then_inc(S["rows_act"], 1)
            act.wait_ge(S["rows_act"], 1)
            for n in range(1, 3 * (ST + 1), 2):
                rows = P if n % (ST + 1) < ST else NS
                dst = (knat, vnat, fnat)[n // (ST + 1)]
                act.wait_ge(S["nat_done"], n + 1)
                a.copy(dst[0:rows, n % (ST + 1), :], PS[0:rows, n % 4, :]).then_inc(S["nat_out_s"], 1)
            a.activation(PT[:, OM:OM + HM, :], PT[:, OM:OM + HM, :], ACT.Sigmoid).then_inc(S["sig_ready"], 1)
            act.wait_ge(S["cat_evac"], 2)
            act.wait_ge(S["nat_out_v"], 8)
            act.wait_ge(S["nat_out_s"], 7)
            act.wait_ge(S["out_dma"], 16 * 4)

            for h in range(HM):
                act.wait_ge(S["mb_done"], h + 1)
                if h:
                    act.wait_ge(S["mmix"], h)
                a.activation(halves(nmb), pair(0), ACT.Copy, scale=-1.0).then_inc(S["mb_evac"], 1)
                a.copy(halves(emb), pair(2)).then_inc(S["mb_evac"], 1)
                a.copy(wib, PS[:, 3, TH:TH + NS]).then_inc(S["mb_evac"], 1)
                act.wait_ge(S["mb_evac"], 3 * h + 3)
                for i in range(ST + 1):
                    n = h * (ST + 1) + i
                    rows, w = (P, P) if i < ST else (NS, NS)
                    act.wait_ge(S["mg_ready"], n + 1)
                    if n >= 2:
                        act.wait_ge(S["mst_ready"], n - 1)
                    ab = cat[0:rows, i, ROWS_F + h:ROWS_F + h + 1]
                    e = a.activation(me[0:rows, n % 2, 0:w], gm[0:rows, n % 2, 0:w], ACT.Exp, bias=ab)
                    if i < ST - 1:
                        e = a.activation(me[:, n % 2, P:SEQ - i * P], nmb[:, (i + 1) * P:SEQ], ACT.Exp, bias=ab)
                    e.then_inc(S["me_ready"], 1)
                act.wait_ge(S["mnd_done"], h * (ST + 1) + ST)
                a.activation(da[:, 0:SEQ], PS[:, 7, :], ACT.Abs).then_inc(S["mda_ready"], 1)
                act.wait_ge(S["mden_ready"], h + 1)
                a.activation(da[:, SEQ:T], ts2, ACT.Abs).then_inc(S["mda_ready"], 1)
                act.wait_ge(S["mss_done"], h + 1)
                a.activation(halves(dr), pair(0), ACT.Sqrt, bias=epsc[:, 0:1], scale=1.0 / DM)\
                    .then_inc(S["mroot"], 1)

            act.wait_ge(S["mmix"], HM)
            act.wait_ge(S["ct_out"], HM)

            def fox_biases(h):
                act.wait_ge(S["fb_done"], h + 1)
                if h:
                    act.wait_ge(S["f_max"], ST * h)
                a.copy(ncb, PS[:, 0, :]).then_inc(S["fb_evac"], 1)

            for h in range(HF):
                if h == 0:
                    fox_biases(0)
                for i in range(ST):
                    act.wait_ge(S["f_max"], h * ST + i + 1)
                    if h:
                        act.wait_ge(S["ft_done"], ST * h)
                    w = (i + 1) * P
                    a.activation(pp[:, i, 0:w], scp[:, i, 0:w], ACT.Exp, bias=fmx[:, 2, i:i + 1],
                                 accum_out=fmx[:, 3, i:i + 1]).then_inc(S["f_exp"], 1)
                if h + 1 < HF:
                    fox_biases(h + 1)
                for j in range(ST):
                    n = h * ST + j
                    act.wait_ge(S["ft_done"], n + 1)
                    if n >= 2:
                        act.wait_ge(S["fo_done"], n - 1)
                    a.copy(pts[:, j % 2, j * P:SEQ], PS[:, 5 + j % 2, j * P:SEQ]).then_inc(S["ft_evac"], 1)
                act.wait_ge(S["fo_done"], (h + 1) * ST)
                rows = slice((h % 2) * DF, (h % 2) * DF + DF)
                a.copy(mixT[rows, NJ + h // 2, 0:SEQ], PS[0:DF, 7, :]).then_inc(S["fo_evac"], 1)

            act.wait_ge(S["fo_done"], HF * ST)
            act.wait_ge(S["out_dma"], 16 * OUT_EARLY)
            act.wait_ge(S["new_copied"], 3)

            a.copy(vn_hi[0:NS, :], vf_new[:, :]).then_inc(S["vh_ready"], 1)

            def sample(b):
                first = isinstance(b, int) and b == 0
                for c in range(CH + 1):
                    if c < CH:
                        n = NS if c == NCH else PC * PAGE
                        if c == 0:
                            act.wait_ge(S["mx_ready"], b + 1)
                            if not first:
                                act.wait_ge(S["sum_read"], b)
                        if not (first and c < 3):
                            act.wait_ge(S["pt_done"], b * CH + c - 2)
                        a.activation(probs[0:NS, c % 3, 0:n], scores[0:NS, c * 512:c * 512 + n], ACT.Exp,
                                     bias=snm[:, 1:2], accum_out=ssum[:, c:c + 1]).then_inc(S["p_ready"], 1)
                    if c >= 1:
                        d = c - 1
                        act.wait_ge(S["pt_done"], b * CH + d + 1)
                        if not (first and d < 3):
                            act.wait_ge(S["pv_done"], b * CH + d - 2)
                        rows, g = (P, PC) if d < NCH else (NS, 1)
                        a.copy(p_t[d % 3][0:rows, 0:g, 0:NS],
                               PS[0:rows, 3 + d % 3, 0:g * NS].rearrange("p (g c) -> p g c", g=g))\
                            .then_inc(S["ph_ready"], 1)
                    if c < NCH:
                        if isinstance(b, int) and b == DB - 1:
                            act.wait_ge(v_in[c % 4], 16 * PC * 2 * b + 8 * PC * (c // 4 + 1))
                            act.wait_ge(v_last[c % 4], 8 * PC * (c // 4 + 1))
                        else:
                            act.wait_ge(v_in[c % 4], 16 * PC * (2 * b + (c // 4 + 1)))
                        if c >= 2:
                            act.wait_ge(S["pv_done"], b * CH + c - 1)
                        elif not first:
                            act.wait_ge(S["pv_done"], b * CH + c - 2)
                        for g in (0, 2):
                            a.copy(v_hi[c % 2][:, g:g + 2, :], vring[c % 4][:, g:g + 2, :])\
                                .then_inc(S["vh_ready"], 1)

            sample(0)
            with act.Fori(1, DB - 1) as b:
                sample(b)
            sample(DB - 1)

            act.wait_ge(S["pv_done"], DB * CH)
            act.wait_ge(S["ot_evac"], 2 * DB)
            for kt in range(KT):
                a.copy(h_hi[:, kt, :], mixT[:, kt, :]).then_inc(S["nhi_ready"], 1)

            def split_highs(n, words, u0):
                with act.Fori(0, n // 2) as i:
                    for s in range(2):
                        split_high(i * 2 + (u0 + s), s, w_raw, w_hi, words)

            split_highs(KT, WT, U0_OUT)
            split_high(U0_FF, 0, w_raw, w_hi, 2 * WT)
            split_high(U0_FF + 1, 1, w_raw, w_hi, 2 * WT)
            root(1)
            normalised(1)
            u0, f0 = U0_FF, 0
            for r, n in enumerate(ROUNDS):

                def hidden(i, ahead, u0=u0, f0=f0):
                    for t in range(2):
                        m = i * 2 + t
                        if ahead:
                            split_high(m + (u0 + 2), t, w_raw, w_hi, 2 * WT)
                        act.wait_ge(S["gate_done"], m + (f0 + 1))
                        if not (f0 == 0 and isinstance(i, int) and i == 0):
                            act.wait_ge(S["act_done"], m + (f0 - 1))
                        a.activation(halves(stage[:, t, :]), pair(4 * t), ACT.Silu).then_inc(S["silu_done"], 1)
                        act.wait_ge(S["act_ready"], m + (f0 + 1))
                        a.copy(act_hi[:, bass.ds(m, 1), :].rearrange("p a t -> p (a t)"), stage[:, t, :])\
                            .then_inc(S["act_hi_done"], 1)

                hidden(0, True)
                with act.Fori(1, n // 2 - 1) as i:
                    hidden(i, True)
                hidden(n // 2 - 1, False)
                split_highs(KT, n * P, u0 + n)
                u0 += n + KT
                f0 += n
                if r + 1 < len(ROUNDS):
                    split_high(u0, 0, w_raw, w_hi, 2 * WT)
                    split_high(u0 + 1, 1, w_raw, w_hi, 2 * WT)
            root(2)

        @blk.vector
        def _(dve):
            v = nc.vector

            def square(kt, u, t):
                if not (isinstance(u, int) and u < 2):
                    dve.wait_ge(S["sq_used"], u - 1)
                x_tile = xT[:, bass.ds(kt, 1), :].rearrange("p a t -> p (a t)")
                v.tensor_tensor(stage[:, t, :], x_tile, x_tile, ALU.mult).then_inc(S["sq_ready"], 1)

            def norm(n, highs):
                dve.wait_ge(S["root_done"], n + 1)
                v.reciprocal(rb, rb).then_inc(S["rinv_done"], 1)
                dve.wait_ge(S["rinv_done"], n + 1)

                def scaled(kt, out, done):
                    v.scalar_tensor_tensor(out=out, in0=xT[:, kt, :],
                                           scalar=gains[:, n * KT + kt:n * KT + kt + 1],
                                           in1=rb, op0=ALU.mult, op1=ALU.mult).then_inc(S[done], 1)

                def low_half(kt):
                    dve.wait_ge(S["nhi_ready"], highs + kt + 1)
                    v.tensor_tensor(h_lo[:, kt, :], sq[:, kt % 2, :], h_hi[:, kt, :].bitcast(F32), ALU.subtract)\
                        .then_inc(S["h_ready"], 1)

                if n == 2:
                    for kt in range(KT):
                        scaled(kt, y[:, kt, :], "y_ready")
                    return
                for kt in range(KT):
                    if kt >= 2:
                        low_half(kt - 2)
                        dve.wait_ge(S["h_ready"], n * KT + kt - 1)
                        if n == 0:
                            dve.wait_ge(S["wg_used"], kt - 1)
                    scaled(kt, sq[:, kt % 2, :], "nh_ready")
                low_half(KT - 2)
                low_half(KT - 1)

            for kt in range(KT):
                if kt % 2 == 0:
                    dve.wait_ge(x_in[kt // 2], 16)
                square(kt, kt, kt % 2)
            dve.wait_ge(S["const_in"], 3 * 16)
            norm(0, 0)

            st = [0]

            def step(ins):
                st[0] += 1
                ins.then_inc(S["gate_step"], 1)
                dve.wait_ge(S["gate_step"], st[0])

            dve.wait_ge(S["small_in"], 5 * 16)
            dve.wait_ge(S["wg_used"], KT)
            v.tensor_scalar(halves(gx), PS[0:GR, 6:8, 0:TH], gbias[:, 0:1], None, ALU.add)\
                .then_inc(S["gate_evac"], 1)
            dve.wait_ge(S["gate_evac"], 1)
            step(v.scalar_tensor_tensor(out=gu, in0=gx, scalar=-1.0, in1=gx, op0=ALU.mult, op1=ALU.min))
            dve.wait_ge(S["gate_act"], 1)
            step(v.tensor_scalar(gu, ge, 1.0, None, ALU.add))
            step(v.tensor_scalar(gd, gu, 1.0, None, ALU.subtract))
            dve.wait_ge(S["gate_act"], 2)
            step(v.tensor_tensor(gu, gu, ge, ALU.mult))
            step(v.scalar_tensor_tensor(out=ge, in0=gd, scalar=0.0, in1=ge, op0=ALU.is_equal, op1=ALU.mult))
            step(v.scalar_tensor_tensor(out=gd, in0=gd, scalar=0.0, in1=gd, op0=ALU.is_equal, op1=ALU.add))
            step(v.reciprocal(gd, gd))
            step(v.tensor_tensor(gu, gu, gd, ALU.mult))
            step(v.tensor_tensor(gu, gu, ge, ALU.add))
            step(v.tensor_scalar(gd, gx, 0.0, None, ALU.min))
            step(v.tensor_tensor(gd, gd, gu, ALU.subtract))
            v.tensor_copy(li, gx[0:HM, :])
            v.tensor_copy(lfm, gd[ROWS_F:ROWS_F + HM, :])
            step(v.tensor_copy(lff[:, :], gd[ROWS_FF:ROWS_FF + HF, :]))

            step(v.tensor_tensor_scan(bm, keep[0:HM, :], lfm, 0.0, ALU.mult, ALU.add))
            step(v.tensor_tensor(a0, li, bm, ALU.subtract))
            dve.wait_ge(S["zeroed"], 2)
            v.tensor_copy(ca[ROWS_F:ROWS_F + HM, :], a0)
            v.memset(mprev[:, 0:SEQ], 0.0)
            step(v.tensor_copy(mprev[:, SEQ:T].rearrange("p (b q) -> p b q", b=DB),
                               mst[:, :].unsqueeze(2).broadcast_to([HM, DB, DS])))
            step(v.tensor_tensor_scan(m_top[:, :], drop[0:HM, :], a0, NEG, ALU.add, ALU.max))
            step(v.tensor_tensor(m_top[:, :], m_top[:, :], mprev, ALU.max))
            step(v.tensor_tensor(mt, bm, m_top[:, :], ALU.add))
            m_last = m_top[:, SEQ:T].rearrange("p (b q) -> p b q", b=DB)
            v.tensor_tensor(mprev[:, SEQ:T], mprev[:, SEQ:T], m_top[:, SEQ:T], ALU.subtract)
            v.tensor_tensor(dec[:, :], mst[:, :], m_last[:, :, DS - 1], ALU.subtract)
            v.tensor_scalar(nml[:, :], m_top[:, SEQ - 1:SEQ], -1.0, None, ALU.mult)
            a0_new = a0[:, SEQ:T].rearrange("p (b q) -> p b q", b=DB)
            v.tensor_tensor(a0_new, a0_new, m_last[:, :, DS - 1:DS].broadcast_to([HM, DB, DS]), ALU.subtract)
            v.tensor_copy(mout[:, 0:1], mt[:, SEQ - 1:SEQ])
            v.tensor_copy(mout[:, 1:1 + DB], mt[:, SEQ:T].rearrange("p (b q) -> p b q", b=DB)[:, :, DS - 1])
            step(v.tensor_tensor_scan(ncf[:, :], keep[:, :], lff[:, :], 0.0, ALU.mult, ALU.add))
            v.tensor_scalar(ncf[:, :], ncf[:, :], -1.0, None, ALU.mult).then_inc(S["rows_ready"], 1)

            dve.wait_ge(S["lg_in"], 32)
            for half in range(2):
                for h in range(HF):
                    last = v.tensor_tensor_scan(lg[:, half, h, :], ones, lg[:, half, h, :], 0.0, ALU.mult, ALU.add)
            last.then_inc(S["page_step"], 1)
            dve.wait_ge(S["page_step"], 1)
            v.tensor_copy(pgs[:, :, :], lg[:, :, :, PAGE - 1]).then_inc(S["page_step"], 1)
            dve.wait_ge(S["page_sum"], 1)
            for half in range(2):
                last = v.scalar_tensor_tensor(
                    out=lg[:, half], in0=lg[:, half], scalar=-1.0,
                    in1=PS[:, 5, half * HF:(half + 1) * HF].unsqueeze(2).broadcast_to([P, HF, PAGE]),
                    op0=ALU.mult, op1=ALU.add)
            last.then_inc(S["page_done"], 1)

            dve.wait_ge(S["tile_evac"], NT_IN)
            v.tensor_scalar(PT[:, KM:KM + HM, :], PT[:, KM:KM + HM, :], DM ** -0.5, None, ALU.mult)\
                .then_inc(S["qk_scaled"], 1)
            v.tensor_scalar(PT[:, QF:QF + NJ, :], PT[:, QF:QF + NJ, :], DF ** -0.5, None, ALU.mult)\
                .then_inc(S["qk_scaled"], 1)
            dve.wait_ge(S["qk_scaled"], 2)
            v.tensor_copy(qf_new[:, :, :], PT[:, QF:QF + NJ, SEQ:T]).then_inc(S["new_copied"], 1)
            v.tensor_copy(kf_new[:, :, :], PT[:, KF:KF + NJ, SEQ:T]).then_inc(S["new_copied"], 1)

            dve.wait_ge(S["rows_act"], 1)
            for n in range(0, 3 * (ST + 1), 2):
                rows = P if n % (ST + 1) < ST else NS
                dst = (knat, vnat, fnat)[n // (ST + 1)]
                dve.wait_ge(S["nat_done"], n + 1)
                v.tensor_copy(dst[0:rows, n % (ST + 1), :], PS[0:rows, n % 4, :]).then_inc(S["nat_out_v"], 1)
            dve.wait_ge(S["cat_done"], 1)
            R = ROWS_F + HM
            v.tensor_copy(cat[:, 0:ST, :], PS[:, 4, 0:ST * R].rearrange("p (i r) -> p i r", i=ST))
            v.tensor_copy(cat[0:NS, ST, :], PS[0:NS, 4, ST * R:(ST + 1) * R]).then_inc(S["cat_evac"], 1)
            v.tensor_copy(decb[:, :, :], PS[:, 5, 32:32 + HM * DB].rearrange("p (h b) -> p h b", h=HM))
            v.tensor_tensor(bias_new[:, :, :], new_mask[0:NS],
                            PS[0:NS, 5, 64:64 + NS].unsqueeze(1).broadcast_to([NS, DB, NS]), ALU.add)\
                .then_inc(S["cat_evac"], 1)
            dve.wait_ge(S["cat_evac"], 2)
            dve.wait_ge(S["nat_out_v"], 8)
            dve.wait_ge(S["nat_out_s"], 7)
            dve.wait_ge(S["state_in"], 16)
            dve.wait_ge(S["sig_ready"], 1)
            dve.wait_ge(S["bias_out"], 8 * 16)
            dve.wait_ge(S["out_dma"], 16 * 4)

            mdv = [0]

            def mstep(ins):
                mdv[0] += 1
                ins.then_inc(S["mdv"], 1)
                dve.wait_ge(S["mdv"], mdv[0])

            def weigh(h, i):
                n = h * (ST + 1) + i
                rows, w = (P, SEQ - i * P) if i < ST else (NS, NS)
                dve.wait_ge(S["me_ready"], n + 1)
                dve.wait_ge(S["ms_done"], n + 1)
                if n >= 2:
                    dve.wait_ge(S["mnd_done"], n - 1)
                v.tensor_tensor(mstt[0:rows, n % 2, 0:w], PS[0:rows, 4 + n % 2, 0:w], me[0:rows, n % 2, 0:w],
                                ALU.mult).then_inc(S["mst_ready"], 1)

            for h in range(HM):
                dve.wait_ge(S["mb_evac"], 3 * (h + 1))
                if h:
                    dve.wait_ge(S["ct_done"], 2 * h)
                mstep(v.tensor_scalar(wm[0:NS, :], block_of[0:NS, :], cat[0:NS, ST, h:h + 1], None, ALU.mult))
                v.tensor_tensor(vw[:, :, 0:P], vnat[:, 0:ST, h * P:(h + 1) * P],
                                cat[:, 0:ST, h:h + 1].broadcast_to([P, ST, P]), ALU.mult)
                v.tensor_copy(vw[:, :, P], cat[:, 0:ST, h])
                v.tensor_tensor(vmk[0:NS], vnat[0:NS, ST, h * P:(h + 1) * P].unsqueeze(1).broadcast_to([NS, DB, P]),
                                wm[0:NS, :].unsqueeze(2).broadcast_to([NS, DB, P]), ALU.mult)
                v.tensor_tensor(nq.rearrange("p (b q) -> p b q", b=DB),
                                PT[:, QM + h, SEQ:T].rearrange("p (b q) -> p b q", b=DB),
                                nst[:, h, :].unsqueeze(2).broadcast_to([P, DB, DS]), ALU.mult)\
                    .then_inc(S["vw_ready"], 1)
                for i in range(ST + 1):
                    n = h * (ST + 1) + i
                    rows, w = (P, P) if i < ST else (NS, NS)
                    if n >= 2:
                        dve.wait_ge(S["me_ready"], n - 1)
                    v.tensor_tensor(gm[0:rows, n % 2, 0:w], nmb[0:rows, i * P:i * P + w],
                                    causal_t if i < ST else causal_s[0:NS, :], ALU.add)\
                        .then_inc(S["mg_ready"], 1)
                    if i >= 1:
                        weigh(h, i - 1)
                weigh(h, ST)
                dve.wait_ge(S["mint_done"], h + 1)
                v.tensor_tensor(ts1, PS[:, 2, 0:NS], wib, ALU.mult)
                mstep(v.tensor_tensor(ts2, PS[:, 3, 0:NS], wib, ALU.mult))
                dve.wait_ge(S["mnd_done"], (h + 1) * (ST + 1))
                v.tensor_tensor(ts2, PS[:, 1, 0:NS], ts2, ALU.add).then_inc(S["mden_ready"], 1)
                v.tensor_tensor(hn, PS[:, 0, 0:NS], ts1, ALU.add)
                dve.wait_ge(S["mda_ready"], 2 * (h + 1))
                mstep(v.tensor_tensor(da, da, emb, ALU.max))
                mstep(v.reciprocal(dr, da))
                v.tensor_tensor(hh[:, 0:SEQ], PS[:, 6, :], dr[:, 0:SEQ], ALU.mult)
                mstep(v.tensor_tensor(hh[:, SEQ:T], hn, dr[:, SEQ:T], ALU.mult))
                v.tensor_tensor(hs, hh, hh, ALU.mult).then_inc(S["hs_ready"], 1)
                dve.wait_ge(S["ct_done"], 2 * h + 1)
                v.tensor_copy(ctp[:, h, :], PS[:, 4, 0:P + 1])
                v.tensor_tensor(ctm[:, h], ctm[:, h], decb[:, h, :].unsqueeze(2).broadcast_to([P, DB, P]), ALU.mult)
                mstep(v.tensor_tensor(nnew[:, h, :], nst[:, h, :], decb[:, h, :], ALU.mult))
                dve.wait_ge(S["ct_done"], 2 * h + 2)
                c2 = ctm[:, h].rearrange("p (a b) v -> p a (b v)", a=2)
                v.tensor_tensor(c2, PS[:, 2:4, :], c2, ALU.add)
                v.tensor_tensor(nnew[:, h, :], PS[:, 5, 0:DB], nnew[:, h, :], ALU.add).then_inc(S["ct_out"], 1)
                dve.wait_ge(S["mroot"], h + 1)
                mstep(v.reciprocal(dr, dr))
                mstep(v.scalar_tensor_tensor(out=hh, in0=hh, scalar=gains[:, 3 * KT + h:3 * KT + h + 1], in1=dr,
                                             op0=ALU.mult, op1=ALU.mult))
                v.tensor_tensor(mixT[:, h, :], hh, PT[:, OM + h, :], ALU.mult).then_inc(S["mmix"], 1)
            dve.wait_ge(S["mmix"], HM)

            fd = [0]

            def fstep(ins):
                fd[0] += 1
                ins.then_inc(S["f_dve"], 1)
                dve.wait_ge(S["f_dve"], fd[0])

            for h in range(HF):
                dve.wait_ge(S["fb_evac"], h + 1)
                fstep(v.tensor_tensor(ncm[:, :, :], ncb.rearrange("p (i s) -> p i s", i=ST),
                                      causal_n.unsqueeze(1).broadcast_to([P, ST, P]), ALU.add))
                for i in range(ST):
                    lo = i * P
                    dve.wait_ge(S["fs_done"], h * ST + i + 1)
                    if h:
                        dve.wait_ge(S["f_exp"], (h - 1) * ST + i + 1)
                    fstep(v.tensor_tensor_reduce(scp[:, i, lo:lo + P], PS[:, 1 + i, lo:lo + P], ncm[:, i, :], 1.0,
                                                 NEG, ALU.add, ALU.max, fmx[:, 0, i:i + 1]))
                    if i:
                        fstep(v.tensor_tensor_reduce(scp[:, i, 0:lo], PS[:, 1 + i, 0:lo], ncb[:, 0:lo], 1.0,
                                                     NEG, ALU.add, ALU.max, fmx[:, 1, i:i + 1]))
                        fstep(v.tensor_tensor(fmx[:, 0, i:i + 1], fmx[:, 0, i:i + 1], fmx[:, 1, i:i + 1], ALU.max))
                    v.tensor_scalar(fmx[:, 2, i:i + 1], fmx[:, 0, i:i + 1], -1.0, None, ALU.mult)\
                        .then_inc(S["f_max"], 1)
                for i in range(ST):
                    dve.wait_ge(S["f_exp"], h * ST + i + 1)
                    fstep(v.reciprocal(fmx[:, 4, i:i + 1], fmx[:, 3, i:i + 1]))
                    v.tensor_scalar(pp[:, i, 0:(i + 1) * P], pp[:, i, 0:(i + 1) * P], fmx[:, 4, i:i + 1], None,
                                    ALU.mult).then_inc(S["f_pn"], 1)
            v.tensor_copy(vf_new[:, :], fnat[0:NS, ST, :]).then_inc(S["new_copied"], 1)

            dve.wait_ge(S["new_copied"], 3)
            dve.wait_ge(S["fo_done"], HF * ST)
            dve.wait_ge(S["fo_evac"], HF)
            dve.wait_ge(S["out_dma"], 16 * OUT_EARLY)

            dve.wait_ge(S["vh_ready"], 1)
            v.tensor_tensor(vn_lo[0:NS, :], vf_new[:, :], vn_hi[0:NS, :].bitcast(F32), ALU.subtract)\
                .then_inc(S["vn_ready"], 1)

            def score(b, par, c):
                n = NS if c == NCH else PC * PAGE
                chunk = scores[0:NS, c * 512:c * 512 + n]
                if c == 0:
                    dve.wait_ge(bias_in[par], (b - par) * (8 * HF) + 16 * HF)
                dve.wait_ge(S["sc_done"], b * CH + c + 1)
                if not (isinstance(b, int) and b == 0):
                    dve.wait_ge(S["p_ready"], (b - 1) * CH + c + 1)
                if c < NCH:
                    hold_here(dve)
                    v.tensor_tensor_reduce(chunk, PS[0:NS, c % 3, 0:n], bias[par][0:NS, c * 512:c * 512 + n],
                                           1.0, NEG, ALU.add, ALU.max, smx[:, c:c + 1])\
                        .then_inc(S["sc_evac"], 1)
                else:
                    nb = bias_new[:, bass.ds(b, 1), :].rearrange("p a k -> p (a k)")
                    v.tensor_tensor(chunk, PS[0:NS, c % 3, 0:n], nb, ALU.add).then_inc(S["sc_evac"], 1)

            def low_values(b, c):
                for g in (0, 2):
                    dve.wait_ge(S["vh_ready"], b * (2 * NCH) + (2 * c + g // 2 + 2))
                    v.tensor_tensor(v_lo[c % 4][:, g:g + 2, :], vring[c % 4][:, g:g + 2, :],
                                    v_hi[c % 2][:, g:g + 2, :].bitcast(F32), ALU.subtract)\
                        .then_inc(S["vl_ready"], 1)

            def low_probs(b, c):
                rows, g = (P, PC) if c < NCH else (NS, 1)
                dve.wait_ge(S["ph_ready"], b * CH + c + 1)
                v.tensor_tensor(p_t[c % 3][0:rows, 0:g, NS:2 * NS],
                                PS[0:rows, 3 + c % 3, 0:g * NS].rearrange("p (g c) -> p g c", g=g),
                                p_t[c % 3][0:rows, 0:g, 0:NS].bitcast(F32), ALU.subtract)\
                    .then_inc(S["pl_ready"], 1)

            def sample(b, par, qk, pv, ot):
                for c in range(CH):
                    if qk:
                        score(b, par, c)
                    if pv and c >= 1:
                        low_probs(b - 1, c - 1)
                    if pv and c < NCH:
                        low_values(b - 1, c)
                    if ot and c == 2:
                        dve.wait_ge(S["ot_done"], b - 1)
                        for p2 in range(2):
                            rows = slice(p2 * DF, p2 * DF + DF)
                            src = stepped(PS[rows, 7, 0:NJ * NS], p2 * DS, [[NS + 2 * DS, NJ], [1, DS]])
                            v.tensor_copy(mixT[rows, NJ:2 * NJ, bass.ds((b - 2) * DS + SEQ, DS)], src)\
                                .then_inc(S["ot_evac"], 1)
                if qk:
                    dve.wait_ge(S["sc_evac"], (b + 1) * CH)
                    v.tensor_reduce(smx[:, NCH:CH], scores[0:NS, PAST:PAST + NS], AX.X, ALU.max)\
                        .then_inc(S["max_step"], 1)
                    dve.wait_ge(S["max_step"], b * 2 + 1)
                    v.tensor_reduce(snm[:, 0:1], smx[:, :], AX.X, ALU.max).then_inc(S["max_step"], 1)
                    dve.wait_ge(S["max_step"], b * 2 + 2)
                    v.tensor_scalar(snm[:, 1:2], snm[:, 0:1], -1.0, None, ALU.mult).then_inc(S["mx_ready"], 1)
                if pv:
                    low_probs(b - 1, NCH)
                    dve.wait_ge(S["p_ready"], b * CH)
                    v.tensor_reduce(sri[0:NS, 0:1], ssum[:, :], AX.X, ALU.add).then_inc(S["sum_read"], 1)
                    dve.wait_ge(S["sum_read"], b * 1)
                    v.reciprocal(sri[0:NS, 1:2], sri[0:NS, 0:1])
                    v.reciprocal(sri[NS:2 * NS, 1:2], sri[0:NS, 0:1]).then_inc(S["sum_ready"], 1)
                    dve.wait_ge(S["sum_ready"], b * 1)
                    dve.wait_ge(S["pv_done"], b * CH)
                    if ot:
                        dve.wait_ge(S["ot_done"], b - 1)
                    v.tensor_scalar(osb[:, :], PS[:, 6, :], sri[:, 1:2], None, ALU.mult)\
                        .then_inc(S["o_ready"], 1)

            sample(0, 0, True, False, False)
            sample(1, 1, True, True, False)
            with dve.Fori(1, DB // 2) as i:
                sample(2 * i, 0, True, True, True)
                sample(2 * i + 1, 1, True, True, True)
            sample(DB, 0, False, True, True)
            sample(DB + 1, 0, False, False, True)
            dve.wait_ge(S["ot_evac"], 2 * DB)

            for kt in range(KT):
                dve.wait_ge(S["nhi_ready"], KT + kt + 1)
                v.tensor_tensor(h_lo[:, kt, :], mixT[:, kt, :], h_hi[:, kt, :].bitcast(F32), ALU.subtract)\
                    .then_inc(S["mixed"], 1)

            def residual(u0, evacuated, squares=None):
                with dve.Fori(0, KT // 2) as i:
                    for t in range(2):
                        dve.wait_ge(S["unit_done"], i * 2 + (u0 + t + 1))
                        dst = xT[:, bass.ds(i * 2 + t, 1), :].rearrange("p a (g t) -> p (a g) t", g=2)
                        v.tensor_tensor(dst, pair(2 * t), dst, ALU.add).then_inc(S["tile_evac"], 1)
                        if squares is not None:
                            dve.wait_ge(S["tile_evac"], i * 2 + (evacuated + t + 1))
                            square(i * 2 + t, i * 2 + (squares * KT + t), t)

            dve.wait_ge(S["x_again"], 16)
            residual(U0_OUT, U0_OUT, squares=1)
            dve.wait_ge(S["tile_evac"], U0_FF)
            norm(1, 2 * KT)
            u0, f0 = U0_FF, 0
            for r, n in enumerate(ROUNDS):
                with dve.Fori(0, n // 2) as i:
                    for t in range(2):
                        m = i * 2 + t
                        dve.wait_ge(S["unit_done"], m + (u0 + 1))
                        dve.wait_ge(S["silu_done"], m + (f0 + 1))
                        v.tensor_tensor(halves(stage[:, t, :]), pair(4 * t + 2), halves(stage[:, t, :]), ALU.mult)\
                            .then_inc(S["act_ready"], 1)
                        dve.wait_ge(S["act_hi_done"], m + (f0 + 1))
                        v.tensor_tensor(act_lo[:, bass.ds(m, 1), :].rearrange("p a t -> p (a t)"), stage[:, t, :],
                                        act_hi[:, bass.ds(m, 1), :].rearrange("p a t -> p (a t)").bitcast(F32),
                                        ALU.subtract).then_inc(S["act_done"], 1)
                residual(u0 + n, U0_FF + r * KT, squares=2 if n == ROUNDS[-1] else None)
                u0 += n + KT
                f0 += n
            dve.wait_ge(S["tile_evac"], U0_FF + 2 * KT)
            norm(2, 3 * KT)

        @blk.tensor
        def _(pe):
            mm = nc.tensor.matmul

            def ssq(n, kt, t):
                pe.wait_ge(S["sq_ready"], kt + (n * KT + 1))
                for g in range(2):
                    last = mm(PS[:, 4 + g, 0:TH], ones, stage[:, t, g * TH:(g + 1) * TH],
                              start=(isinstance(kt, int) and kt == 0), stop=(isinstance(kt, int) and kt == KT - 1))
                last.then_inc(S["sq_used"], 1)

            def product_step(bk, hi, lo, x_hi, x_lo, kt, kts):
                for n, (w, x) in enumerate(((hi, x_hi), (hi, x_lo), (lo, x_hi))):
                    for g in range(2):
                        last = mm(PS[:, bk + g, 0:TH], w(kt), x[:, kt, g * TH:(g + 1) * TH],
                                  start=(kt == 0 and n == 0), stop=(kt == kts - 1 and n == 2))
                return last

            def product(bk, hi, lo, x_hi, x_lo, kts):
                for kt in range(kts):
                    last = product_step(bk, hi, lo, x_hi, x_lo, kt, kts)
                return last

            def weight_tile(ring, s, n, kts):
                w = ring[s][:, n * kts * P:(n + 1) * kts * P].rearrange("p (k c) -> p k c", k=kts)
                return lambda kt: w[:, kt, :]

            pe.wait_ge(S["const_in"], 3 * 16)
            for kt in range(KT):
                ssq(0, kt, kt % 2)
            pe.wait_ge(S["small_in"], 5 * 16)
            for kt in range(KT + 2):
                if kt < KT:
                    pe.wait_ge(S["nh_ready"], kt + 1)
                    for g in range(2):
                        last = mm(PS[0:GR, 6 + g, 0:TH], wg[:, kt, :], sq[:, kt % 2, g * TH:(g + 1) * TH],
                                  start=(kt == 0), stop=(kt == KT - 1))
                    last.then_inc(S["wg_used"], 1)
                if kt >= 2:
                    if kt == 2:
                        pe.wait_ge(S["wl_ready"], 2)
                    pe.wait_ge(S["h_ready"], kt - 1)
                    for t in range(2):
                        last = product_step(2 * t, weight_tile(w_hi_in, t, 0, KT), weight_tile(w_lo_in, t, 0, KT),
                                            h_hi, h_lo, kt - 2, KT)
                        if kt - 2 == KT - 1:
                            last.then_inc(S["unit_done"], 1)

            def projected(i, first=False):
                for t in range(2 if first else 0, 4):
                    u = i * 4 + t
                    pe.wait_ge(S["wl_ready"], u + 1)
                    if not first:
                        pe.wait_ge(S["tile_evac"], u - 3)
                    elif t == 3:
                        pe.wait_ge(S["gate_evac"], 1)
                    product(2 * t, weight_tile(w_hi_in, t % 2, 0, KT), weight_tile(w_lo_in, t % 2, 0, KT),
                            h_hi, h_lo, KT).then_inc(S["unit_done"], 1)

            projected(0, True)
            with pe.Fori(1, NT_IN // 4) as i:
                projected(i)

            pe.wait_ge(S["tile_evac"], NT_IN)
            pe.wait_ge(S["page_step"], 2)
            mm(PS[:, 5, 0:2 * HF], suffix, pgs[:, :, :].rearrange("p a h -> p (a h)"), start=True, stop=True)\
                .then_inc(S["page_sum"], 1)
            pe.wait_ge(S["qk_scaled"], 2)
            for n in range(3 * (ST + 1)):
                t0, i = (KM, VM, VF)[n // (ST + 1)], n % (ST + 1)
                w = P if i < ST else NS
                if n >= 4:
                    pe.wait_ge(S[("nat_out_v", "nat_out_s")[n % 2]], n // 2 - 1)
                for c in range(4):
                    last = nc.tensor.transpose(PS[0:w, n % 4, c * P:(c + 1) * P], PT[:, t0 + c, i * P:i * P + w],
                                               ident)
                last.then_inc(S["nat_done"], 1)
            R = ROWS_F + HM
            pe.wait_ge(S["rows_act"], 1)
            pe.wait_ge(S["rows_ready"], 1)
            for i in range(ST + 1):
                w = P if i < ST else NS
                nc.tensor.transpose(PS[0:w, 4, i * R:(i + 1) * R], ca[:, i * P:i * P + w], ident[0:R, 0:R])
            pe.wait_ge(S["page_done"], 1)
            for h in range(HM):
                mm(PS[:, 5, 32 + h * DB:32 + (h + 1) * DB], sel4[:, h * P:(h + 1) * P], dec[:, :],
                   start=True, stop=True)
            mm(PS[0:NS, 5, 64:64 + NS], selq, ncf[:, SEQ:T], start=True, stop=True).then_inc(S["cat_done"], 1)

            pe.wait_ge(S["cat_evac"], 2)
            pe.wait_ge(S["nat_out_v"], 8)
            pe.wait_ge(S["nat_out_s"], 7)
            pe.wait_ge(S["state_in"], 16)
            for h in range(HM):
                hc = slice(h * P, (h + 1) * P)
                if h:
                    pe.wait_ge(S["mroot"], h)
                    pe.wait_ge(S["ct_out"], h)
                    pe.wait_ge(S["hs_ready"], h)
                for g in range(2):
                    mm(PS[:, g, 0:TH], sel4[:, hc], m_top[:, g * TH:(g + 1) * TH], start=True, stop=True)
                    mm(PS[:, 2 + g, 0:TH], sel4[:, hc], emt[:, g * TH:(g + 1) * TH], start=True, stop=True)
                mm(PS[:, 3, TH:TH + NS], sel4[:, hc], winter[:, :], start=True, stop=True)\
                    .then_inc(S["mb_done"], 1)

                def logits(i):
                    n = h * (ST + 1) + i
                    if i >= 2:
                        pe.wait_ge(S["mst_ready"], n - 1)
                    rows = P if i < ST else NS
                    end = SEQ if i < ST else T
                    mm(PS[0:rows, 4 + n % 2, 0:end - i * P], PT[:, KM + h, i * P:i * P + rows],
                       PT[:, QM + h, i * P:end], start=True, stop=True).then_inc(S["ms_done"], 1)

                def outputs(i):
                    n = h * (ST + 1) + i
                    pe.wait_ge(S["mst_ready"], n + 1)
                    if i < ST:
                        mm(PS[:, 6, i * P:SEQ], vnat[:, i, hc], mstt[:, n % 2, 0:SEQ - i * P],
                           start=(i == 0), stop=(i == ST - 1))
                        mm(PS[:, 7, i * P:SEQ], ones, mstt[:, n % 2, 0:SEQ - i * P],
                           start=(i == 0), stop=(i == ST - 1)).then_inc(S["mnd_done"], 1)
                    else:
                        mm(PS[:, 0, 0:NS], vnat[0:NS, ST, hc], mstt[0:NS, n % 2, 0:NS], start=True, stop=True)
                        mm(PS[:, 1, 0:NS], ones[0:NS, :], mstt[0:NS, n % 2, 0:NS], start=True, stop=True)\
                            .then_inc(S["mnd_done"], 1)

                logits(0)
                logits(1)
                pe.wait_ge(S["mb_evac"], 3 * (h + 1))
                pe.wait_ge(S["vw_ready"], h + 1)
                for b in range(DB):
                    mm(PS[:, 2, b * DS:(b + 1) * DS], ctm[:, h, b, :], PT[:, QM + h, SEQ + b * DS:SEQ + (b + 1) * DS],
                       start=True, stop=True)
                mm(PS[:, 3, 0:NS], ones, nq, start=True, stop=True).then_inc(S["mint_done"], 1)
                for i in range(ST + 1):
                    if i >= 2:
                        logits(i)
                    if i >= 1:
                        outputs(i - 1)
                outputs(ST)
                for i in range(ST):
                    last = mm(PS[:, 4, 0:P + 1], knat[:, i, hc], vw[:, i, :], start=(i == 0), stop=(i == ST - 1))
                last.then_inc(S["ct_done"], 1)
                pe.wait_ge(S["mden_ready"], h + 1)
                for g in range(2):
                    mm(PS[:, 2 + g, :], knat[0:NS, ST, hc],
                       vmk[0:NS, 4 * g:4 * g + 4, :].rearrange("p b v -> p (b v)"), start=True, stop=True)
                mm(PS[:, 5, 0:DB], knat[0:NS, ST, hc], wm[0:NS, :], start=True, stop=True)\
                    .then_inc(S["ct_done"], 1)
                pe.wait_ge(S["hs_ready"], h + 1)
                for g in range(2):
                    last = mm(PS[:, g, 0:TH], ones, hs[:, g * TH:(g + 1) * TH], start=True, stop=True)
                last.then_inc(S["mss_done"], 1)

            pe.wait_ge(S["mroot"], HM)
            pe.wait_ge(S["ct_out"], HM)

            def fox_scores(h):
                rows = slice((h % 2) * DF, (h % 2) * DF + DF)
                if h:
                    pe.wait_ge(S["fb_evac"], h)
                mm(PS[:, 0, :], sel8[:, h * P:(h + 1) * P], ncf[:, 0:SEQ], start=True, stop=True)\
                    .then_inc(S["fb_done"], 1)
                for i in range(ST):
                    if h:
                        pe.wait_ge(S["f_max"], (h - 1) * ST + i + 1)
                    mm(PS[:, 1 + i, 0:(i + 1) * P], PT[rows, QF + h // 2, i * P:(i + 1) * P],
                       PT[rows, KF + h // 2, 0:(i + 1) * P], start=True, stop=True).then_inc(S["fs_done"], 1)

            def fox_outputs(h):
                def turn(j):
                    n = h * ST + j
                    if n >= 2:
                        pe.wait_ge(S["ft_evac"], n - 1)
                    for t in range(j, ST):
                        last = nc.tensor.transpose(PS[:, 5 + j % 2, t * P:(t + 1) * P], pp[:, t, j * P:(j + 1) * P],
                                                   ident)
                    last.then_inc(S["ft_done"], 1)

                def weigh_values(j):
                    pe.wait_ge(S["ft_evac"], h * ST + j + 1)
                    mm(PS[0:DF, 7, j * P:SEQ], fnat[:, j, h * DF:(h + 1) * DF], pts[:, j % 2, j * P:SEQ],
                       start=(j == 0), stop=(j == ST - 1)).then_inc(S["fo_done"], 1)

                pe.wait_ge(S["f_pn"], (h + 1) * ST)
                turn(0)
                turn(1)
                if h:
                    pe.wait_ge(S["fo_evac"], h)
                weigh_values(0)
                turn(2)
                weigh_values(1)
                turn(3)
                weigh_values(2)
                weigh_values(3)

            fox_scores(0)
            for h in range(HF):
                if h + 1 < HF:
                    fox_scores(h + 1)
                fox_outputs(h)

            pe.wait_ge(S["fo_evac"], HF)
            pe.wait_ge(S["f_max"], HF * ST)
            pe.wait_ge(S["new_copied"], 3)

            def keys_by_queries(b, par, c):
                if c == 0:
                    pe.wait_ge(S["q_ready"], 2 * b + 2)
                if c < NCH:
                    if isinstance(b, int) and b == 0:
                        pe.wait_ge(k_first[c % 4], 8 * PC * (c // 4 + 1))
                        pe.wait_ge(k_in[c % 4], 8 * PC * (c // 4 + 1))
                    else:
                        pe.wait_ge(k_in[c % 4], 16 * PC * (2 * b + c // 4))
                if not (isinstance(b, int) and b == 0 and c < 3):
                    pe.wait_ge(S["sc_evac"], b * CH + c - 2)
                w = PC * PAGE if c < NCH else NS
                for j in range(NJ):
                    keys = kring[c % 4][:, :, j, :] if c < NCH else kf_new[:, j, :]
                    last = mm(PS[0:NS, c % 3, 0:w], qbd[:, par, j, :], keys, start=(j == 0), stop=(j == NJ - 1))
                last.then_inc(S["sc_done"], 1)

            def turn_probs(b, c):
                pe.wait_ge(S["p_ready"], b * CH + c + 1)
                if not (isinstance(b, int) and b == 0 and c < 3):
                    pe.wait_ge(S["pl_ready"], b * CH + c - 2)
                hold_here(pe)
                for g in range(PC if c < NCH else 1):
                    w = P if c < NCH else NS
                    last = nc.tensor.transpose(PS[0:w, 3 + c % 3, g * NS:(g + 1) * NS],
                                               probs[0:NS, c % 3, g * P:g * P + w], ident[0:NS, 0:NS])
                last.then_inc(S["pt_done"], 1)

            def values(b, c):
                pe.wait_ge(S["pl_ready"], b * CH + c + 1)
                if c == 0 and not (isinstance(b, int) and b == 0):
                    pe.wait_ge(S["o_ready"], b)
                if c < NCH:
                    for g in range(PC):
                        if g % 2 == 0:
                            pe.wait_ge(S["vl_ready"], b * (2 * NCH) + (2 * c + g // 2 + 1))
                        mm(PS[:, 6, :], p_t[c % 3][:, g, :], v_hi[c % 2][:, g, :], start=(c == 0 and g == 0), stop=False)
                        last = mm(PS[:, 6, :], p_t[c % 3][:, g, :], v_lo[c % 4][:, g, :], start=False, stop=False)
                else:
                    mm(PS[:, 6, :], p_t[c % 3][0:NS, 0, :], vn_hi[0:NS, :], start=False, stop=False)
                    last = mm(PS[:, 6, :], p_t[c % 3][0:NS, 0, :], vn_lo[0:NS, :], start=False, stop=True)
                last.then_inc(S["pv_done"], 1)

            def turn_out(b):
                pe.wait_ge(S["o_ready"], b + 1)
                if not (isinstance(b, int) and b == 0):
                    pe.wait_ge(S["ot_evac"], 2 * b)
                for j in range(NJ):
                    last = mm(PS[:, 7, j * NS:(j + 1) * NS], osb[:, j * P:(j + 1) * P], fold, start=True, stop=True)
                last.then_inc(S["ot_done"], 1)

            def sample(b, par, qk, pv, ot):
                for c in range(CH + 2):
                    if qk and c < CH:
                        keys_by_queries(b, par, c)
                    if ot and c == 1:
                        turn_out(b - 2)
                    if pv and 1 <= c <= CH:
                        turn_probs(b - 1, c - 1)
                    if pv and c >= 2:
                        values(b - 1, c - 2)

            pe.wait_ge(S["vn_ready"], 1)
            sample(0, 0, True, False, False)
            sample(1, 1, True, True, False)
            with pe.Fori(1, DB // 2) as i:
                sample(2 * i, 0, True, True, True)
                sample(2 * i + 1, 1, True, True, True)
            sample(DB, 0, False, True, True)
            turn_out(DB - 1)

            pe.wait_ge(S["ot_evac"], 2 * DB)
            pe.wait_ge(S["mixed"], KT)

            def model_tiles(u0, evacuated, x_hi, x_lo, kts, squares=None):
                def two(i):
                    for s in range(2):
                        pe.wait_ge(S["wl_ready"], i * 2 + (u0 + s + 1))
                        pe.wait_ge(S["tile_evac"], i * 2 + (evacuated + s - 1))
                        product(2 * s, weight_tile(w_hi, s, 0, kts), weight_tile(w_lo, s, 0, kts), x_hi, x_lo, kts)\
                            .then_inc(S["unit_done"], 1)
                        if squares is not None and not (isinstance(i, int) and s == 0):
                            ssq(squares, i * 2 + (s - 1), 1 - s)

                two(0)
                with pe.Fori(1, KT // 2) as i:
                    two(i)
                if squares is not None:
                    ssq(squares, KT - 1, 1)

            model_tiles(U0_OUT, U0_OUT, h_hi, h_lo, KT, squares=1)
            u0, f0, down0 = U0_FF, 0, U0_FF
            for n in ROUNDS:
                def hidden(i, u0=u0, f0=f0):
                    for s in range(2):
                        first = f0 == 0 and isinstance(i, int)
                        pe.wait_ge(S["wl_ready"], i * 2 + (u0 + s + 1))
                        if not first:
                            pe.wait_ge(S["act_ready"], i * 2 + (f0 + s - 1))
                        for kt in range(KT):
                            if first and s == 0:
                                pe.wait_ge(S["h_ready"], KT + kt + 1)
                            for t in range(2):
                                last = product_step(4 * s + 2 * t, weight_tile(w_hi, s, t, KT),
                                                    weight_tile(w_lo, s, t, KT), h_hi, h_lo, kt, KT)
                                if kt == KT - 1:
                                    last.then_inc(S[("gate_done", "unit_done")[t]], 1)

                pe.wait_ge(S["tile_evac"], down0)
                hidden(0)
                with pe.Fori(1, n // 2) as i:
                    hidden(i)
                f0 += n
                pe.wait_ge(S["act_done"], f0)
                model_tiles(u0 + n, down0, act_hi, act_lo, n, squares=2 if n == ROUNDS[-1] else None)
                u0 += n + KT
                down0 += KT


def kernel(**inputs):
    import concourse.bacc as bacc
    from concourse.bass_utils import run_bass_kernel_spmd

    f = {k: np.asarray(v) for k, v in inputs.items()}

    def tiles(w):
        return w.reshape(w.shape[0] // P, P, w.shape[1]).transpose(1, 0, 2)

    def units(w, width):
        k, n = w.shape
        return w.reshape(k // P, P, n // width, width).transpose(2, 1, 0, 3).reshape(n // width, P, -1)

    w_in = f["w_in"][0]
    g0, f0 = 4 * HM * DM, 4 * HM * DM + 2 * HM
    wgate = np.zeros((D, GR), np.float32)
    wgate[:, 0:HM] = w_in[:, g0:g0 + HM]
    wgate[:, ROWS_F:ROWS_F + HM] = w_in[:, g0 + HM:g0 + 2 * HM]
    wgate[:, ROWS_FF:ROWS_FF + HF] = w_in[:, f0 + 3 * HF * DF:]
    gbias = np.zeros((GR, 1), np.float32)
    gbias[0:HM, 0] = f["b_m_igate"][0]
    gbias[ROWS_F:ROWS_F + HM, 0] = f["b_m_fgate"][0]
    gbias[ROWS_FF:, 0] = f["b_f_fgate"][0]
    cols = np.concatenate([w_in[:, :g0], w_in[:, f0:f0 + 3 * HF * DF]], axis=1)
    wide, rows = constants()
    gate_up = np.concatenate([units(f["w_gate"][0], P), units(f["w_up"][0], P)], axis=2)
    x = np.concatenate([f["x_prompt"].reshape(SEQ, D), f["x_sample"].reshape(NS, D)], axis=0)
    pool_k, pool_v, pool_f = f["cache_fox_k"][0], f["cache_fox_v"][0], f["cache_fox_logf"][0]
    npool = pool_k.shape[0]
    table = f["page_table"].reshape(-1)
    arrays = {
        "x": x.T.reshape(KT, P, T).transpose(1, 0, 2),
        "wide": wide,
        "rows": rows,
        "gains": np.concatenate([f["norm_mix_g"].reshape(KT, P), f["norm_ffn_g"].reshape(KT, P),
                                 f["norm_final_g"].reshape(KT, P), f["mlstm_head_g"].reshape(HM, P)]).T,
        "wgate": tiles(wgate),
        "gbias": gbias,
        "win": units(cols, P),
        "wout": units(f["w_out"][0], P),
        "ptab": table.reshape(1, -1),
        "pidx": table.reshape(2, P).T,
        "m": f["state_mlstm_m"][0].T,
        "n": f["state_mlstm_n"][0].transpose(2, 1, 0),
        "C": f["state_mlstm_C"][0].transpose(3, 1, 0, 2),
        "K": pool_k.reshape(npool, PAGE, NJ, 2 * DF).transpose(0, 3, 2, 1).reshape(npool, P, NJ * PAGE),
        "V": pool_v.reshape(npool, PAGE, HF * DF),
        "logf": pool_f.transpose(0, 2, 1).reshape(npool, HF * PAGE),
    }
    first = 0
    for r, n in enumerate(ROUNDS):
        arrays[f"wgu{r}"] = gate_up[first:first + n]
        arrays[f"wdown{r}"] = units(f["w_down"][0][first * P:(first + n) * P], P)
        first += n
    outs = {
        "o_y": (P, KT, T), "o_kf": (P, NJ, T), "o_vf": (P, NJ, T), "o_logf": (HF, T), "o_m": (HM, 1 + DB),
        "o_C": (P, HM, DB, DM), "o_n": (P, HM, DB), "o_Cp": (P, HM, DM + 1),
    }
    nc = bacc.Bacc("TRN2", target_bir_lowering=False, num_devices=1)
    arrays = {k: np.ascontiguousarray(a) for k, a in arrays.items()}
    A = {k: nc.dram_tensor("in_" + k, a.shape, mybir.dt.from_np(a.dtype), kind="ExternalInput").ap()
         for k, a in arrays.items()}
    for k, s in outs.items():
        A[k] = nc.dram_tensor(k, s, F32, kind="ExternalOutput").ap()
    A["npool"] = npool
    build(nc, A)
    got = run_bass_kernel_spmd(nc, [{"in_" + k: a for k, a in arrays.items()}], core_ids=[0]).results[0]

    def tokens(a):
        a = a.transpose(2, 1, 0).reshape(T, -1)
        return a[:SEQ], a[SEQ:].reshape(DB, DS, -1)

    y, kf, vf = tokens(got["o_y"]), tokens(got["o_kf"]), tokens(got["o_vf"])
    lf = got["o_logf"].T
    m, n, c, cp = got["o_m"], got["o_n"], got["o_C"], got["o_Cp"]
    return (y[0].reshape(1, SEQ, D), y[1],
            kf[0].reshape(1, 1, SEQ, HF, DF), vf[0].reshape(1, 1, SEQ, HF, DF), lf[:SEQ].reshape(1, 1, SEQ, HF),
            cp[:, :, :DM].transpose(1, 2, 0).reshape(1, 1, HM, DM, DM), cp[:, :, DM].T.reshape(1, 1, HM, DM),
            m[:, 0].reshape(1, 1, HM),
            kf[1].reshape(1, DB, DS, HF, DF), vf[1].reshape(1, DB, DS, HF, DF),
            lf[SEQ:].reshape(1, DB, DS, HF),
            c.transpose(2, 1, 3, 0).reshape(1, DB, HM, DM, DM), n.transpose(2, 1, 0).reshape(1, DB, HM, DM),
            m[:, 1:].T.reshape(1, DB, HM))
```

```python
from contextlib import ExitStack

import numpy as np

import concourse.bass as bass
from concourse import mybir

F32 = mybir.dt.float32
F32R = mybir.dt.float32r
I32 = mybir.dt.int32
ALU = mybir.AluOpType
ACT = mybir.ActivationFunctionType
AX = mybir.AxisListType

P = 128
D = 1024
KT = D // P
SEQ, DB, DS = 512, 8, 8
NS = DB * DS
T = SEQ + NS
TH = T // 2
ST = SEQ // P
HM, DM = 4, 128
HF, DF = 8, 64
NJ = HF // 2
DFF = 2816
PAGES, PAGE = 32, 128
PC = 4
NCH = PAGES // PC
CH = NCH + 1
PAST = PAGES * PAGE
EPS = 1e-6
NEG = -1e30
ROWS_F, ROWS_FF = 32, 64
GR = ROWS_FF + HF

QM, KM, VM, OM, QF, KF, VF = 0, 4, 8, 12, 16, 20, 24
NT_IN = 28
WT = KT * P
WSLOT = 2 * WT
ROUNDS = (12, 10)
assert sum(ROUNDS) * P == DFF
U0_OUT = NT_IN
U0_FF = NT_IN + KT
H_AT, X_AT, W_AT = 0, 2 * KT * T, 3 * KT * T
PT_AT = W_AT + 6 * WT
ROWS_AT = PT_AT + NT_IN * T
ACT_AT = W_AT + 6 * WSLOT
STAGE_AT = ACT_AT + 2 * ROUNDS[0] * T
DECODE = PAST + NS + 3 * PC * PAGE + 2 * PAST + (4 + 2) * PC * HF * DF + 3 * PC * P
ARENA = max(STAGE_AT + 2 * T, W_AT + DECODE)
HALF, OTHER_HALF = range(0, PC // 2), range(PC // 2, PC)
K_AHEAD = 2
OUT_EARLY = 7


def constants():
    s, t = np.arange(P)[:, None], np.arange(P)[None, :]
    causal_t = np.where(s <= t, 0.0, NEG)
    causal_n = np.where(t <= s, 0.0, NEG)
    s6, t6 = np.arange(NS)[:, None], np.arange(NS)[None, :]
    causal_s = np.full((P, NS), NEG)
    causal_s[:NS] = np.where((s6 <= t6) & (s6 // DS == t6 // DS), 0.0, NEG)
    block = np.zeros((P, DB))
    block[:NS] = s6 // DS == np.arange(DB)[None, :]
    new_mask = np.full((P, DB, NS), NEG)
    for b in range(DB):
        for q in range(DS):
            for h in range(HF):
                new_mask[h * DS + q, b, b * DS:b * DS + q + 1] = 0.0
    suffix = (s >= t) & (s // PAGES == t // PAGES)
    fold = np.concatenate([np.eye(NS), np.eye(NS)])
    one_at = np.zeros((P, 2 * HM - 1))
    one_at[:, HM - 1] = 1.0
    wide = np.concatenate([np.eye(P), causal_t, causal_n, causal_s, block, new_mask.reshape(P, -1),
                           suffix, np.ones((P, P)), fold, one_at], axis=1).astype(np.float32)
    sel4 = np.zeros((HM, HM, P))
    sel4[np.arange(HM), np.arange(HM)] = 1.0
    sel8 = np.zeros((HF, HF, P))
    sel8[np.arange(HF), np.arange(HF)] = 1.0
    selq = np.repeat(np.eye(HF), DS, axis=1)
    reset = np.ones(T)
    reset[0] = 0.0
    reset[SEQ::DS] = 0.0
    rows = np.zeros((HF, HM * P + HF * P + NS + 2 * T))
    rows[:HM, :HM * P] = sel4.reshape(HM, -1)
    rows[:, HM * P:HM * P + HF * P] = sel8.reshape(HF, -1)
    rows[:, HM * P + HF * P:HM * P + HF * P + NS] = selq
    rows[:, HM * P + HF * P + NS:HM * P + HF * P + NS + T] = reset
    rows[:, HM * P + HF * P + NS + T:] = (1.0 - reset) * NEG
    return wide, rows.astype(np.float32)


WIDE_COLS = 3 * P + NS + DB + DB * NS + 2 * P + NS + 2 * HM - 1
ROW_COLS = HM * P + HF * P + NS + 2 * T


def build(nc, A):
    ctx = ExitStack()
    with ctx:
        def sb(name, shape, dt=F32):
            return ctx.enter_context(nc.sbuf_tensor(name, shape, dt))

        def sem(name):
            return ctx.enter_context(nc.semaphore(name))

        PS = ctx.enter_context(nc.psum_tensor("PS", [P, 8, 512], F32))

        wide = sb("wide", [P, WIDE_COLS])
        rowc = sb("rowc", [HF, ROW_COLS])
        gains = sb("gains", [P, 3 * KT + HM])
        epsc = sb("epsc", [P, 1])
        o = 0
        ident = wide[:, o:o + P]; o += P
        causal_t = wide[:, o:o + P]; o += P
        causal_n = wide[:, o:o + P]; o += P
        causal_s = wide[:, o:o + NS]; o += NS
        block_of = wide[:, o:o + DB]; o += DB
        new_mask = wide[:, o:o + DB * NS].rearrange("p (b k) -> p b k", b=DB); o += DB * NS
        suffix = wide[:, o:o + P]; o += P
        ones = wide[:, o:o + P]; o += P
        fold = wide[:, o:o + NS]; o += NS
        one_at = wide[:, o:o + 2 * HM - 1]
        o = 0
        sel4 = rowc[0:HM, o:o + HM * P]; o += HM * P
        sel8 = rowc[:, o:o + HF * P]; o += HF * P
        selq = rowc[:, o:o + NS]; o += NS
        keep = rowc[:, o:o + T]; o += T
        drop = rowc[:, o:o + T]

        qbd = sb("qbd", [P, 2, NJ, NS])
        kf_new = sb("kf_new", [P, NJ, NS])
        qf_new = sb("qf_new", [P, NJ, NS])
        vf_new = sb("vf_new", [NS, HF * DF])
        bias_new = sb("bias_new", [NS, DB, NS])
        ptab = sb("ptab", [1, DB * PAGES], I32)
        pidx = sb("pidx", [P, 2], I32)
        pgs = sb("pgs", [P, 2, HF])
        gbias = sb("gbias", [GR, 1])
        wg = sb("wg", [P, KT, GR])
        m_top = sb("m_top", [HM, T])
        emt = sb("emt", [HM, T])
        winter = sb("winter", [HM, NS])
        ca = sb("ca", [ROWS_F + HM, T])
        cat = sb("cat", [P, ST + 1, ROWS_F + HM])
        lff = sb("lff", [HF, T])
        ncf = sb("ncf", [HF, T])
        mst = sb("mst", [HM, DB])
        dec = sb("dec", [HM, DB])
        nml = sb("nml", [HM, 1])
        mout = sb("mout", [HM, 1 + DB])
        decb = sb("decb", [P, HM, DB])
        nst = sb("nst", [P, HM, DB])
        nnew = sb("nnew", [P, HM, DB])
        ctp = sb("ctp", [P, HM, DM + 1 + DB])
        smx = sb("smx", [NS, CH])
        snm = sb("snm", [NS, 2])
        ssum = sb("ssum", [NS, CH])
        sri = sb("sri", [P, 2])
        osb = sb("osb", [P, HF * DF])
        fmx = sb("fmx", [P, 5, ST])

        base = -(-nc.sbuf_base // 32) * 32
        arena = sb("arena", [P, ARENA])
        assert nc.sbuf_base == base + 4 * ARENA
        at = [0]

        def take(words):
            at[0] += words
            assert at[0] <= ARENA, at[0]
            return arena[:, at[0] - words:at[0]]

        def rounded(name, words):
            at[0] += words
            assert at[0] <= ARENA, at[0]
            return nc.alloc_sbuf_tensor_at(name, [P, words], F32R, offset=base + 4 * (at[0] - words))[:, :]

        at[0] = H_AT
        h_hi = rounded("h_hi", KT * T).rearrange("p (k t) -> p k t", k=KT)
        h_lo = rounded("h_lo", KT * T).rearrange("p (k t) -> p k t", k=KT)
        at[0] = H_AT
        y = take(KT * T).rearrange("p (k t) -> p k t", k=KT)
        at[0] = X_AT
        xT = take(KT * T).rearrange("p (k t) -> p k t", k=KT)
        mixT = xT
        at[0] = W_AT
        w_raw_in = [take(WT) for _ in range(2)]
        w_hi_in = [rounded(f"w_hi_in{i}", WT) for i in range(2)]
        w_lo_in = [rounded(f"w_lo_in{i}", WT) for i in range(2)]
        assert at[0] == PT_AT
        PT = take(NT_IN * T).rearrange("p (n t) -> p n t", n=NT_IN)
        at[0] = X_AT
        lg = take(2 * HF * PAGE).rearrange("p (a h k) -> p a h k", a=2, h=HF)
        gu, gd = (take(T)[0:GR] for _ in range(2))
        at[0] = ROWS_AT
        gx, ge = (take(T)[0:GR] for _ in range(2))
        li, lfm, bm, mt, mprev, a0 = (take(T)[0:HM] for _ in range(6))
        at[0] = ACT_AT
        sq = take(2 * T).rearrange("p (a t) -> p a t", a=2)
        rb = take(T)
        at[0] = H_AT
        knat, vnat = (take((ST + 1) * 512).rearrange("p (i c) -> p i c", i=ST + 1) for _ in range(2))
        at[0] = X_AT - (ST + 1) * 512
        fnat = take((ST + 1) * 512).rearrange("p (i c) -> p i c", i=ST + 1)
        at[0] = W_AT
        ctm = take(HM * DB * DM).rearrange("p (h b v) -> p h b v", h=HM, b=DB)
        at[0] = ROWS_AT
        me = take(2 * 512).rearrange("p (i t) -> p i t", i=2)
        mstt = take(2 * 512).rearrange("p (i t) -> p i t", i=2)
        gm = take(2 * P).rearrange("p (i t) -> p i t", i=2)
        hs = take(HM * T).rearrange("p (h t) -> p h t", h=HM)
        at[0] = PT_AT + VM * T
        nmb = take(T)
        vw = take(ST * (P + 1)).rearrange("p (i c) -> p i c", i=ST)
        den = take(T)[0:HM]
        wib = take(2 * NS).rearrange("p (i t) -> p i t", i=2)
        nq = take(NS); ts1 = take(NS)
        wm = take(DB)
        assert at[0] <= PT_AT + OM * T
        at[0] = PT_AT + VF * T
        vmk = take(DB * P).rearrange("p (b v) -> p b v", b=DB)
        rden, rnorm = (take(T)[0:HM] for _ in range(2))
        assert at[0] <= ROWS_AT
        at[0] = ROWS_AT
        ncb = take(512)
        ncm = take(512).rearrange("p (i s) -> p i s", i=ST)
        pts = take(2 * 512).rearrange("p (i s) -> p i s", i=2)
        pp = take(ST * 512).rearrange("p (i s) -> p i s", i=ST)
        at[0] = H_AT + K_AHEAD * PC * 512
        scp = take(ST * 512).rearrange("p (i s) -> p i s", i=ST)
        assert at[0] <= X_AT - (ST + 1) * 512
        at[0] = H_AT
        kring = [take(PC * NJ * P).rearrange("p (g j k) -> p g j k", g=PC, j=NJ) for _ in range(4)]
        vn_hi = rounded("vn_hi", HF * DF)
        vn_lo = rounded("vn_lo", HF * DF)
        assert at[0] <= X_AT
        at[0] = W_AT
        scores = take(PAST + NS)
        probs = take(3 * PC * PAGE).rearrange("p (a k) -> p a k", a=3)
        bias = [take(PAST) for _ in range(2)]
        assert at[0] <= PT_AT + QF * T
        vring = [take(PC * 512).rearrange("p (g c) -> p g c", g=PC) for _ in range(4)]
        at[0] -= 4 * PC * 512
        v_lo = [rounded(f"v_lo{i}", PC * 512).rearrange("p (g c) -> p g c", g=PC) for i in range(4)]
        v_hi = [rounded(f"v_hi{i}", PC * 512).rearrange("p (g c) -> p g c", g=PC) for i in range(2)]
        p_t = [rounded(f"p_t{i}", PC * P).rearrange("p (g c) -> p g c", g=PC) for i in range(3)]
        at[0] = W_AT
        w_raw = [take(WSLOT) for _ in range(2)]
        w_hi = [rounded(f"w_hi{i}", WSLOT) for i in range(2)]
        w_lo = [rounded(f"w_lo{i}", WSLOT) for i in range(2)]
        assert at[0] == ACT_AT
        act_hi = rounded("act_hi", ROUNDS[0] * T).rearrange("p (n t) -> p n t", n=ROUNDS[0])
        act_lo = rounded("act_lo", ROUNDS[0] * T).rearrange("p (n t) -> p n t", n=ROUNDS[0])
        stage = take(2 * T).rearrange("p (a t) -> p a t", a=2)

        bscr = nc.dram_tensor("bias_scratch", [DB, HF, PAST], F32, kind="Internal").ap()

        names = """wide_in const_in x_in0 x_in1 x_in2 x_in3 x_again small_in state_in idx_in lg_in w_in0 w_in1
            k_in0 k_in1 k_in2 k_in3 k_first0 k_first1 k_first2 k_first3
            v_last0 v_last1 v_last2 v_last3 v_in0 v_in1 v_in2 v_in3 bias_in0 bias_in1 bias_out out_dma zeroed
            sq_ready sq_used root_done rinv_done h_ready
            gate_evac gate_step gate_act rows_ready rows_act wg_used page_step page_sum page_done
            unit_done gate_done tile_evac silu_done act_ready act_hi_done act_done wh_ready wl_ready
            nh_ready nhi_ready mixed sig_ready qk_scaled new_copied
            nat_done nat_out_v nat_out_s cat_done cat_evac
            mb_done mb_evac wm_ready nq_ready vw_ready gated mg_ready me_ready ms_done mst_ready mnd_done
            mint_done num_out hn_ready
            squared den_abs mdv mss_done ms2_ready mroot mf_ready mf_done mmix ct_done ctp_out ct_out
            fb_done fb_evac fs_done f_dve f_max f_exp f_pn ft_done ft_evac fo_done fo_evac
            q_ready sc_done sc_evac max_step mx_ready p_ready pt_done ph_ready pl_ready vh_ready vl_ready vn_ready
            sum_read sum_ready pv_done o_ready ot_done ot_evac
            y_ready y_out passed""".split()
        S = {n: sem(n) for n in names}
        x_in = [S[f"x_in{i}"] for i in range(4)]
        w_in = [S["w_in0"], S["w_in1"]]
        k_in = [S[f"k_in{i}"] for i in range(4)]
        v_in = [S[f"v_in{i}"] for i in range(4)]
        k_first = [S[f"k_first{i}"] for i in range(4)]
        v_last = [S[f"v_last{i}"] for i in range(4)]
        bias_in = [S["bias_in0"], S["bias_in1"]]

        def pair(b):
            return PS[:, b:b + 2, 0:TH]

        def halves(ap):
            return ap.rearrange("p (a t) -> p a t", a=2)

        def stepped(ap, offset, dims):
            return bass.AP(ap.tensor, ap.offset + offset, [ap.ap[0], *dims])

        def hold_here(eng):
            eng.sem_inc(S["passed"], 1)

        def pages(eng, ring, sems, cache, b, c, part=range(PC)):
            hold_here(eng)
            slot = c % 4
            for g in part:
                pg = eng.value_load(ptab[0:1, bass.ds(b * PAGES + c * PC + g, 1)], min_val=0,
                                    max_val=A["npool"] - 1)
                dst = ring[slot][:, g]
                if cache is A["K"]:
                    dst = dst.rearrange("p j k -> p (j k)")
                eng.dma_start(dst, cache[bass.ds(pg, 1), :, :].rearrange("a p n -> p (a n)"))\
                   .then_inc(sems[slot], 16)

        blk = ctx.enter_context(nc.Block())

        @blk.sync
        def _(sp):
            sp.dma_start(wide[:, :], A["wide"]).then_inc(S["wide_in"], 16)
            for i in range(4):
                sp.dma_start(xT[:, 2 * i:2 * i + 2, :], A["x"][:, 2 * i:2 * i + 2, :]).then_inc(x_in[i], 16)
            sp.dma_start(rowc[:, :], A["rows"]).then_inc(S["const_in"], 16)
            sp.dma_start(gains[:, :], A["gains"]).then_inc(S["const_in"], 16)
            sp.dma_start(wg[:, :, :], A["wgate"]).then_inc(S["small_in"], 16)
            sp.dma_start(gbias[:, :], A["gbias"]).then_inc(S["small_in"], 16)
            sp.dma_start(ptab[:, :], A["ptab"]).then_inc(S["small_in"], 16)
            sp.dma_start(mst[:, :], A["m"]).then_inc(S["small_in"], 16)
            sp.dma_start(nst[:, :, :], A["n"]).then_inc(S["small_in"], 16)

            def stream(slots, src, n, words, u0, then=lambda: None):
                def load(i, s):
                    v = i * 2 + (u0 + s - 1)
                    if not (isinstance(i, int) and v < 1):
                        sp.wait_ge(S["wl_ready"], v)
                    a = src[i * 2 + s] if isinstance(i, int) else \
                        src[bass.ds(i * 2 + s, 1), :, :].rearrange("a p n -> p (a n)")
                    sp.dma_start(slots[s][:, 0:words], a).then_inc(w_in[s], 16)

                for s in range(2):
                    load(0, s)
                then()
                with sp.Fori(1, n // 2) as i:
                    for s in range(2):
                        load(i, s)

            stream(w_raw_in, A["win"], NT_IN, WT, 0)
            sp.wait_ge(S["unit_done"], NT_IN)
            sp.dma_start(ctm[:, :, :, :], A["C"]).then_inc(S["state_in"], 16)

            def load_keys(b, c):
                if c >= 4:
                    sp.wait_ge(S["sc_done"], b * CH + c - 3)
                elif not (isinstance(b, int) and b == 0):
                    sp.wait_ge(S["sc_done"], (b - 1) * CH + c + 5)
                pages(sp, kring, k_in, A["K"], b, c, HALF if isinstance(b, int) and b == 0 else range(PC))

            def load_bias(b, par, wait):
                if wait:
                    sp.wait_ge(S["sc_evac"], (b - 1) * CH)
                for h in range(HF):
                    src = bass.AP(bscr.tensor, b * (HF * PAST) + h * PAST, [[0, DS], [1, PAST]])
                    sp.dma_start(bias[par][h * DS:(h + 1) * DS, :], src).then_inc(bias_in[par], 16)

            sp.wait_ge(S["small_in"], 5 * 16)
            sp.wait_ge(S["bias_out"], 8 * 16)
            sp.wait_ge(S["ct_done"], 2 * HM)
            for c in range(K_AHEAD):
                load_keys(0, c)
            sp.wait_ge(S["mmix"], HM)
            load_bias(0, 0, False)
            load_bias(1, 1, False)
            sp.wait_ge(S["fo_done"], HF * ST)
            sp.wait_ge(S["fo_evac"], HF)
            sp.wait_ge(S["new_copied"], 3)
            sp.wait_ge(S["out_dma"], 16 * OUT_EARLY)
            for c in range(K_AHEAD, NCH):
                load_keys(0, c)

            def batch(b, next_par):
                for c in range(NCH):
                    load_keys(b, c)
                    if c == 3 and next_par is not None:
                        load_bias(b + 1, next_par, True)

            batch(1, 0)
            with sp.Fori(1, DB // 2 - 1) as i:
                batch(2 * i, 1)
                batch(2 * i + 1, 0)
            batch(DB - 2, 1)
            batch(DB - 1, None)
            for c in range(NCH):
                sp.wait_ge(S["pv_done"], (DB - 1) * CH + c - 3 if c >= 4 else (DB - 2) * CH + c + 5)
                pages(sp, vring, v_last, A["V"], DB - 1, c, OTHER_HALF)

            assert 2 * WSLOT <= PAST + NS
            sp.wait_ge(S["p_ready"], DB * CH)

            def x_again():
                sp.wait_ge(S["mixed"], KT)
                sp.dma_start(xT[:, :, :], A["x"]).then_inc(S["x_again"], 16)

            stream(w_raw, A["wout"], KT, WT, U0_OUT, x_again)
            u0 = U0_FF
            for r, n in enumerate(ROUNDS):
                stream(w_raw, A[f"wgu{r}"], n, 2 * WT, u0)
                stream(w_raw, A[f"wdown{r}"], KT, n * P, u0 + n)
                u0 += n + KT
            for kt in range(KT):
                sp.wait_ge(S["y_ready"], kt + 1)
                sp.dma_start(A["o_y"][:, kt, :], y[:, kt, :]).then_inc(S["y_out"], 16)
            sp.wait_ge(S["y_out"], KT * 16)

        @blk.gpsimd
        def _(pool):
            nc.gpsimd.memset(epsc[:, :], EPS).then_inc(S["zeroed"], 1)
            nc.gpsimd.memset(ca[:, :], 0.0).then_inc(S["zeroed"], 1)
            nc.gpsimd.memset(qbd[:, :, :, :], 0.0).then_inc(S["zeroed"], 1)
            pool.dma_start(pidx[:, :], A["pidx"]).then_inc(S["idx_in"], 16)
            pool.wait_ge(S["idx_in"], 16)

            def split_low(i, s, raw, hi, lo, words, u0):
                u = i * 2 + (u0 + s)
                pool.wait_ge(S["wh_ready"], u + 1)
                nc.gpsimd.tensor_tensor(lo[s][:, 0:words], raw[s][:, 0:words], hi[s][:, 0:words].bitcast(F32),
                                        ALU.subtract).then_inc(S["wl_ready"], 1)

            def split_lows(n, raw, hi, lo, words, u0, first=0):
                with pool.Fori(first, n // 2) as i:
                    for s in range(2):
                        split_low(i, s, raw, hi, lo, words, u0)

            for s in range(2):
                split_low(0, s, w_raw_in, w_hi_in, w_lo_in, WT, 0)
            pool.wait_ge(S["nh_ready"], KT)
            for half in range(2):
                nc.gpsimd.indirect_dma_start(
                    lg[:, half, :, :].rearrange("p h k -> p (h k)"), None, A["logf"],
                    bass.IndirectOffsetOnAxis(ap=pidx[:, half:half + 1], axis=0)).then_inc(S["lg_in"], 16)
            split_lows(NT_IN, w_raw_in, w_hi_in, w_lo_in, WT, 0, first=1)

            pool.wait_ge(S["page_done"], 1)
            for b in range(DB):
                pool.dma_start(bscr[b].rearrange("h (g k) -> g h k", g=PAGES),
                               lg[(b % 4) * PAGES:(b % 4 + 1) * PAGES, b // 4, :, :]).then_inc(S["bias_out"], 16)
            pool.wait_ge(S["rows_ready"], 1)
            pool.dma_start(A["o_logf"], lff[:, :]).then_inc(S["out_dma"], 16)
            pool.dma_start(A["o_m"], mout[:, :]).then_inc(S["out_dma"], 16)
            pool.wait_ge(S["tile_evac"], NT_IN)
            pool.dma_start(A["o_kf"], PT[:, KF:KF + NJ, :]).then_inc(S["out_dma"], 16)
            pool.dma_start(A["o_vf"], PT[:, VF:VF + NJ, :]).then_inc(S["out_dma"], 16)

            pool.wait_ge(S["cat_evac"], 2)
            pool.wait_ge(S["nat_out_v"], 8)
            pool.wait_ge(S["nat_out_s"], 7)
            pool.wait_ge(S["out_dma"], 16 * 4)
            p = nc.gpsimd
            for h in range(HM):
                if h:
                    pool.wait_ge(S["ct_done"], 2 * h)
                p.tensor_scalar(wm[0:NS, :], block_of[0:NS, :], cat[0:NS, ST, h:h + 1], None, ALU.mult)\
                    .then_inc(S["wm_ready"], 1)
                pool.wait_ge(S["wm_ready"], h + 1)
                p.tensor_tensor(nq.rearrange("p (b q) -> p b q", b=DB),
                                PT[:, QM + h, SEQ:T].rearrange("p (b q) -> p b q", b=DB),
                                nst[:, h, :].unsqueeze(2).broadcast_to([P, DB, DS]), ALU.mult)\
                    .then_inc(S["nq_ready"], 1)
                p.tensor_tensor(vw[:, :, 0:P], vnat[:, 0:ST, h * P:(h + 1) * P],
                                cat[:, 0:ST, h:h + 1].broadcast_to([P, ST, P]), ALU.mult)
                p.tensor_copy(vw[:, :, P], cat[:, 0:ST, h])
                p.tensor_tensor(vmk[0:NS], vnat[0:NS, ST, h * P:(h + 1) * P].unsqueeze(1).broadcast_to([NS, DB, P]),
                                wm[0:NS, :].unsqueeze(2).broadcast_to([NS, DB, P]), ALU.mult)\
                    .then_inc(S["vw_ready"], 1)
            for h in range(HM):
                pool.wait_ge(S["squared"], h + 1)
                p.tensor_tensor(mixT[:, h, :], mixT[:, h, :], PT[:, OM + h, :], ALU.mult).then_inc(S["gated"], 1)
            pool.wait_ge(S["ct_out"], HM)
            pool.dma_start(A["o_C"], ctm[:, :, :, :]).then_inc(S["out_dma"], 16)
            pool.dma_start(A["o_n"], nnew[:, :, :]).then_inc(S["out_dma"], 16)
            pool.dma_start(A["o_Cp"], ctp[:, :, 0:DM + 1]).then_inc(S["out_dma"], 16)

            def first_keys(c):
                if c >= 4:
                    pool.wait_ge(S["sc_done"], c - 3)
                pages(pool, kring, k_first, A["K"], 0, c, OTHER_HALF)

            pool.wait_ge(S["small_in"], 5 * 16)
            for c in range(K_AHEAD):
                first_keys(c)

            pool.wait_ge(S["gated"], HM)
            pool.wait_ge(S["new_copied"], 2)
            pool.wait_ge(S["zeroed"], 3)

            def queries(b, par):
                if not (isinstance(b, int) and b < 2):
                    pool.wait_ge(S["sc_done"], (b - 1) * CH)
                for p2 in range(2):
                    rows = slice(p2 * DF, p2 * DF + DF)
                    dst = stepped(qbd[rows, par, :, :], p2 * DS, [[NS + 2 * DS, NJ], [1, DS]])
                    nc.gpsimd.tensor_copy(dst, qf_new[rows, :, bass.ds(b * DS, DS)]).then_inc(S["q_ready"], 1)

            queries(0, 0)
            queries(1, 1)
            pool.wait_ge(S["fo_done"], HF * ST)
            pool.wait_ge(S["fo_evac"], HF)
            pool.wait_ge(S["new_copied"], 3)
            pool.wait_ge(S["out_dma"], 16 * OUT_EARLY)

            for c in range(K_AHEAD, NCH):
                first_keys(c)

            def batch(b, par):
                for c in range(NCH):
                    if c >= 4:
                        pool.wait_ge(S["pv_done"], b * CH + c - 3)
                    elif not (isinstance(b, int) and b == 0):
                        pool.wait_ge(S["pv_done"], (b - 1) * CH + c + 5)
                    pages(pool, vring, v_in, A["V"], b, c, HALF if isinstance(b, int) and b == DB - 1 else range(PC))
                    if c == 2 and par is not None:
                        queries(b + 2, par)

            batch(0, 0)
            batch(1, 1)
            with pool.Fori(1, DB // 2 - 1) as i:
                batch(2 * i, 0)
                batch(2 * i + 1, 1)
            batch(DB - 2, None)
            batch(DB - 1, None)

            split_lows(KT, w_raw, w_hi, w_lo, WT, U0_OUT)
            u0 = U0_FF
            for n in ROUNDS:
                split_lows(n, w_raw, w_hi, w_lo, 2 * WT, u0)
                split_lows(KT, w_raw, w_hi, w_lo, n * P, u0 + n)
                u0 += n + KT

        @blk.scalar
        def _(act):
            a = nc.scalar

            def root(n):
                act.wait_ge(S["sq_used"], KT * (n + 1))
                a.activation(halves(rb[:, :]), pair(4), ACT.Sqrt, bias=epsc[:, 0:1], scale=1.0 / D)\
                    .then_inc(S["root_done"], 1)

            act.wait_ge(S["zeroed"], 2)
            root(0)
            def split_high(u, s, raw, hi, words, first=False):
                act.wait_ge(w_in[s], (u - s) * 8 + 16)
                if not first:
                    act.wait_ge(S["unit_done"], u - 1)
                    act.wait_ge(S["wl_ready"], u - 1)
                a.copy(hi[s][:, 0:words], raw[s][:, 0:words]).then_inc(S["wh_ready"], 1)

            def normalised(n):
                for kt in range(KT):
                    act.wait_ge(S["nh_ready"], n * KT + kt + 1)
                    a.copy(h_hi[:, kt, :], sq[:, kt % 2, :]).then_inc(S["nhi_ready"], 1)

            split_high(0, 0, w_raw_in, w_hi_in, WT, True)
            split_high(1, 1, w_raw_in, w_hi_in, WT, True)
            normalised(0)
            act.wait_ge(S["gate_step"], 1)
            a.activation(ge, gu, ACT.Exp).then_inc(S["gate_act"], 1)
            act.wait_ge(S["gate_step"], 3)
            a.activation(gu, gu, ACT.Ln).then_inc(S["gate_act"], 1)

            def projected(i, ahead):
                for t in range(4):
                    u = i * 4 + t
                    if t < ahead:
                        split_high(u + 2, t % 2, w_raw_in, w_hi_in, WT)
                    act.wait_ge(S["unit_done"], u + 1)
                    dst = PT[:, bass.ds(u, 1), :].rearrange("p a (g t) -> p (a g) t", g=2)
                    a.copy(dst, pair(2 * t)).then_inc(S["tile_evac"], 1)

            with act.Fori(0, NT_IN // 4 - 2) as i:
                projected(i, 4)
            act.wait_ge(S["rows_ready"], 1)
            a.activation(emt[:, :], mt, ACT.Exp, scale=-1.0)
            a.activation(winter[:, :], mprev[:, SEQ:T], ACT.Exp)
            a.activation(dec[:, :], dec[:, :], ACT.Exp)
            a.activation(ca[0:HM, 0:SEQ], a0[:, 0:SEQ], ACT.Exp, bias=nml[:, 0:1])
            a.activation(ca[0:HM, SEQ:T], a0[:, SEQ:T], ACT.Exp).then_inc(S["rows_act"], 1)
            projected(NT_IN // 4 - 2, 4)
            act.wait_ge(S["tile_evac"], OM + HM)
            a.activation(PT[:, OM:OM + HM, :], PT[:, OM:OM + HM, :], ACT.Sigmoid).then_inc(S["sig_ready"], 1)
            projected(NT_IN // 4 - 1, 2)
            for n in range(1, 3 * (ST + 1), 2):
                rows = P if n % (ST + 1) < ST else NS
                dst = (knat, vnat, fnat)[n // (ST + 1)]
                act.wait_ge(S["nat_done"], n + 1)
                a.copy(dst[0:rows, n % (ST + 1), :], PS[0:rows, n % 4, :]).then_inc(S["nat_out_s"], 1)
            act.wait_ge(S["cat_evac"], 2)
            act.wait_ge(S["nat_out_v"], 8)
            act.wait_ge(S["nat_out_s"], 7)

            def head_rows(h):
                act.wait_ge(S["mb_done"], h + 1)
                if h >= 2:
                    act.wait_ge(S["hn_ready"], h - 1)
                a.activation(halves(nmb), pair(0), ACT.Copy, scale=-1.0).then_inc(S["mb_evac"], 1)
                a.copy(wib[:, h % 2, :], PS[:, 1, TH:TH + NS]).then_inc(S["mb_evac"], 1)

            def square_head(h):
                act.wait_ge(S["hn_ready"], h + 1)
                act.wait_ge(S["num_out"], h + 1)
                a.activation(hs[:, h, :], mixT[:, h, :], ACT.Square).then_inc(S["squared"], 1)

            head_rows(0)
            for h in range(HM):
                act.wait_ge(S["mb_evac"], 2 * h + 2)
                for i in range(ST + 1):
                    n = h * (ST + 1) + i
                    rows, w = (P, P) if i < ST else (NS, NS)
                    act.wait_ge(S["mg_ready"], n + 1)
                    if n >= 2:
                        act.wait_ge(S["mst_ready"], n - 1)
                    ab = cat[0:rows, i, ROWS_F + h:ROWS_F + h + 1]
                    e = a.activation(me[0:rows, n % 2, 0:w], gm[0:rows, n % 2, 0:w], ACT.Exp, bias=ab)
                    if i < ST - 1:
                        e = a.activation(me[:, n % 2, P:SEQ - i * P], nmb[:, (i + 1) * P:SEQ], ACT.Exp, bias=ab)
                    e.then_inc(S["me_ready"], 1)
                if h + 1 < HM:
                    head_rows(h + 1)
                act.wait_ge(S["mnd_done"], h * (ST + 1) + ST)
                if h == 0:
                    act.wait_ge(S["bias_out"], 8 * 16)
                a.copy(mixT[:, h, 0:SEQ], PS[:, 6, :]).then_inc(S["num_out"], 1)
                act.wait_ge(S["ct_done"], 2 * h + 1)
                a.copy(ctp[:, h, :], PS[:, 4, 0:P + 1 + DB]).then_inc(S["ctp_out"], 1)
                if h:
                    square_head(h - 1)
            a.activation(den[:, 0:SEQ], PS[0:HM, 7, :], ACT.Abs).then_inc(S["den_abs"], 1)
            square_head(HM - 1)
            a.activation(den[:, SEQ:T], den[:, SEQ:T], ACT.Abs).then_inc(S["den_abs"], 1)
            act.wait_ge(S["ms2_ready"], 1)
            a.activation(rnorm, rnorm, ACT.Sqrt, bias=epsc[0:HM, 0:1], scale=1.0 / DM).then_inc(S["mroot"], 1)

            act.wait_ge(S["ct_done"], 2 * HM)
            act.wait_ge(S["mst_ready"], HM * (ST + 1))

            def fox_biases(h):
                act.wait_ge(S["fb_done"], h + 1)
                if h:
                    act.wait_ge(S["f_max"], ST * h)
                a.copy(ncb, PS[:, 0, :]).then_inc(S["fb_evac"], 1)

            for h in range(HF):
                if h == 0:
                    fox_biases(0)
                for i in range(ST):
                    act.wait_ge(S["f_max"], h * ST + i + 1)
                    if h:
                        act.wait_ge(S["ft_done"], ST * h)
                    w = (i + 1) * P
                    a.activation(pp[:, i, 0:w], scp[:, i, 0:w], ACT.Exp, bias=fmx[:, 2, i:i + 1],
                                 accum_out=fmx[:, 3, i:i + 1]).then_inc(S["f_exp"], 1)
                if h + 1 < HF:
                    fox_biases(h + 1)
                for j in range(ST):
                    n = h * ST + j
                    act.wait_ge(S["ft_done"], n + 1)
                    if n >= 2:
                        act.wait_ge(S["fo_done"], n - 1)
                    a.copy(pts[:, j % 2, j * P:SEQ], PS[:, 5 + j % 2, j * P:SEQ]).then_inc(S["ft_evac"], 1)
                act.wait_ge(S["fo_done"], (h + 1) * ST)
                rows = slice((h % 2) * DF, (h % 2) * DF + DF)
                a.copy(mixT[rows, NJ + h // 2, 0:SEQ], PS[0:DF, 7, :]).then_inc(S["fo_evac"], 1)

            act.wait_ge(S["fo_done"], HF * ST)
            act.wait_ge(S["out_dma"], 16 * OUT_EARLY)
            act.wait_ge(S["new_copied"], 3)

            a.copy(vn_hi[0:NS, :], vf_new[:, :]).then_inc(S["vh_ready"], 1)

            def sample(b):
                first = isinstance(b, int) and b == 0
                for c in range(CH + 1):
                    if c < CH:
                        n = NS if c == NCH else PC * PAGE
                        if c == 0:
                            act.wait_ge(S["mx_ready"], b + 1)
                            if not first:
                                act.wait_ge(S["sum_read"], b)
                        if not (first and c < 3):
                            act.wait_ge(S["pt_done"], b * CH + c - 2)
                        a.activation(probs[0:NS, c % 3, 0:n], scores[0:NS, c * 512:c * 512 + n], ACT.Exp,
                                     bias=snm[:, 1:2], accum_out=ssum[:, c:c + 1]).then_inc(S["p_ready"], 1)
                    if c >= 1:
                        d = c - 1
                        act.wait_ge(S["pt_done"], b * CH + d + 1)
                        if not (first and d < 3):
                            act.wait_ge(S["pv_done"], b * CH + d - 2)
                        rows, g = (P, PC) if d < NCH else (NS, 1)
                        a.copy(p_t[d % 3][0:rows, 0:g, 0:NS],
                               PS[0:rows, 3 + d % 3, 0:g * NS].rearrange("p (g c) -> p g c", g=g))\
                            .then_inc(S["ph_ready"], 1)
                    if c < NCH:
                        if isinstance(b, int) and b == DB - 1:
                            act.wait_ge(v_in[c % 4], 16 * PC * 2 * b + 8 * PC * (c // 4 + 1))
                            act.wait_ge(v_last[c % 4], 8 * PC * (c // 4 + 1))
                        else:
                            act.wait_ge(v_in[c % 4], 16 * PC * (2 * b + (c // 4 + 1)))
                        if c >= 2:
                            act.wait_ge(S["pv_done"], b * CH + c - 1)
                        elif not first:
                            act.wait_ge(S["pv_done"], b * CH + c - 2)
                        for g in (0, 2):
                            a.copy(v_hi[c % 2][:, g:g + 2, :], vring[c % 4][:, g:g + 2, :])\
                                .then_inc(S["vh_ready"], 1)

            sample(0)
            with act.Fori(1, DB - 1) as b:
                sample(b)
            sample(DB - 1)

            def mixed_highs(tiles):
                for kt in tiles:
                    a.copy(h_hi[:, kt, :], mixT[:, kt, :]).then_inc(S["nhi_ready"], 1)

            def split_highs(n, words, u0, first=0):
                with act.Fori(first, n // 2) as i:
                    for s in range(2):
                        split_high(i * 2 + (u0 + s), s, w_raw, w_hi, words)

            act.wait_ge(S["sc_done"], DB * CH)
            mixed_highs(range(HM))
            act.wait_ge(S["pt_done"], DB * CH)
            for s in range(2):
                split_high(U0_OUT + s, s, w_raw, w_hi, WT)
            act.wait_ge(S["pv_done"], DB * CH)
            act.wait_ge(S["ot_evac"], 2 * DB)
            mixed_highs(range(HM, KT))
            split_highs(KT, WT, U0_OUT, first=1)
            split_high(U0_FF, 0, w_raw, w_hi, 2 * WT)
            split_high(U0_FF + 1, 1, w_raw, w_hi, 2 * WT)
            root(1)
            normalised(1)
            u0, f0 = U0_FF, 0
            for r, n in enumerate(ROUNDS):

                def hidden(i, words, u0=u0, f0=f0):
                    for t in range(2):
                        m = i * 2 + t
                        split_high(m + (u0 + 2), t, w_raw, w_hi, words)
                        act.wait_ge(S["gate_done"], m + (f0 + 1))
                        if not (f0 == 0 and isinstance(i, int) and i == 0):
                            act.wait_ge(S["act_done"], m + (f0 - 1))
                        a.activation(halves(stage[:, t, :]), pair(4 * t), ACT.Silu).then_inc(S["silu_done"], 1)
                        act.wait_ge(S["act_ready"], m + (f0 + 1))
                        a.copy(act_hi[:, bass.ds(m, 1), :].rearrange("p a t -> p (a t)"), stage[:, t, :])\
                            .then_inc(S["act_hi_done"], 1)

                hidden(0, 2 * WT)
                with act.Fori(1, n // 2 - 1) as i:
                    hidden(i, 2 * WT)
                hidden(n // 2 - 1, n * P)
                split_highs(KT, n * P, u0 + n, first=1)
                u0 += n + KT
                f0 += n
                if r + 1 < len(ROUNDS):
                    split_high(u0, 0, w_raw, w_hi, 2 * WT)
                    split_high(u0 + 1, 1, w_raw, w_hi, 2 * WT)
            root(2)

        @blk.vector
        def _(dve):
            v = nc.vector

            def square(kt, u, t):
                if not (isinstance(u, int) and u < 2):
                    dve.wait_ge(S["sq_used"], u - 1)
                x_tile = xT[:, bass.ds(kt, 1), :].rearrange("p a t -> p (a t)")
                v.tensor_tensor(stage[:, t, :], x_tile, x_tile, ALU.mult).then_inc(S["sq_ready"], 1)

            def norm(n, highs):
                dve.wait_ge(S["root_done"], n + 1)
                v.reciprocal(rb, rb).then_inc(S["rinv_done"], 1)
                dve.wait_ge(S["rinv_done"], n + 1)

                def scaled(kt, out, done):
                    v.scalar_tensor_tensor(out=out, in0=xT[:, kt, :],
                                           scalar=gains[:, n * KT + kt:n * KT + kt + 1],
                                           in1=rb, op0=ALU.mult, op1=ALU.mult).then_inc(S[done], 1)

                def low_half(kt):
                    dve.wait_ge(S["nhi_ready"], highs + kt + 1)
                    v.tensor_tensor(h_lo[:, kt, :], sq[:, kt % 2, :], h_hi[:, kt, :].bitcast(F32), ALU.subtract)\
                        .then_inc(S["h_ready"], 1)

                if n == 2:
                    for kt in range(KT):
                        scaled(kt, y[:, kt, :], "y_ready")
                    return
                for kt in range(KT):
                    if kt >= 2:
                        low_half(kt - 2)
                        dve.wait_ge(S["h_ready"], n * KT + kt - 1)
                        if n == 0:
                            dve.wait_ge(S["wg_used"], kt - 1)
                    scaled(kt, sq[:, kt % 2, :], "nh_ready")
                low_half(KT - 2)
                low_half(KT - 1)

            for kt in range(KT):
                if kt % 2 == 0:
                    dve.wait_ge(x_in[kt // 2], 16)
                square(kt, kt, kt % 2)
            dve.wait_ge(S["wide_in"], 16)
            dve.wait_ge(S["const_in"], 2 * 16)
            norm(0, 0)

            st = [0]

            def step(ins):
                st[0] += 1
                ins.then_inc(S["gate_step"], 1)
                dve.wait_ge(S["gate_step"], st[0])

            dve.wait_ge(S["small_in"], 5 * 16)
            dve.wait_ge(S["wg_used"], KT)
            v.tensor_scalar(halves(gx), PS[0:GR, 6:8, 0:TH], gbias[:, 0:1], None, ALU.add)\
                .then_inc(S["gate_evac"], 1)
            dve.wait_ge(S["gate_evac"], 1)
            step(v.scalar_tensor_tensor(out=gu, in0=gx, scalar=-1.0, in1=gx, op0=ALU.mult, op1=ALU.min))
            dve.wait_ge(S["gate_act"], 1)
            step(v.tensor_scalar(gu, ge, 1.0, None, ALU.add))
            step(v.tensor_scalar(gd, gu, 1.0, None, ALU.subtract))
            dve.wait_ge(S["gate_act"], 2)
            step(v.tensor_tensor(gu, gu, ge, ALU.mult))
            step(v.scalar_tensor_tensor(out=ge, in0=gd, scalar=0.0, in1=ge, op0=ALU.is_equal, op1=ALU.mult))
            step(v.scalar_tensor_tensor(out=gd, in0=gd, scalar=0.0, in1=gd, op0=ALU.is_equal, op1=ALU.add))
            step(v.reciprocal(gd, gd))
            step(v.tensor_tensor(gu, gu, gd, ALU.mult))
            step(v.tensor_tensor(gu, gu, ge, ALU.add))
            step(v.tensor_scalar(gd, gx, 0.0, None, ALU.min))
            step(v.tensor_tensor(gd, gd, gu, ALU.subtract))
            v.tensor_copy(li, gx[0:HM, :])
            v.tensor_copy(lfm, gd[ROWS_F:ROWS_F + HM, :])
            step(v.tensor_copy(lff[:, :], gd[ROWS_FF:ROWS_FF + HF, :]))

            step(v.tensor_tensor_scan(bm, keep[0:HM, :], lfm, 0.0, ALU.mult, ALU.add))
            step(v.tensor_tensor(a0, li, bm, ALU.subtract))
            dve.wait_ge(S["zeroed"], 2)
            v.tensor_copy(ca[ROWS_F:ROWS_F + HM, :], a0)
            v.memset(mprev[:, 0:SEQ], 0.0)
            step(v.tensor_copy(mprev[:, SEQ:T].rearrange("p (b q) -> p b q", b=DB),
                               mst[:, :].unsqueeze(2).broadcast_to([HM, DB, DS])))
            step(v.tensor_tensor_scan(m_top[:, :], drop[0:HM, :], a0, NEG, ALU.add, ALU.max))
            step(v.tensor_tensor(m_top[:, :], m_top[:, :], mprev, ALU.max))
            step(v.tensor_tensor(mt, bm, m_top[:, :], ALU.add))
            m_last = m_top[:, SEQ:T].rearrange("p (b q) -> p b q", b=DB)
            v.tensor_tensor(mprev[:, SEQ:T], mprev[:, SEQ:T], m_top[:, SEQ:T], ALU.subtract)
            v.tensor_tensor(dec[:, :], mst[:, :], m_last[:, :, DS - 1], ALU.subtract)
            v.tensor_scalar(nml[:, :], m_top[:, SEQ - 1:SEQ], -1.0, None, ALU.mult)
            a0_new = a0[:, SEQ:T].rearrange("p (b q) -> p b q", b=DB)
            v.tensor_tensor(a0_new, a0_new, m_last[:, :, DS - 1:DS].broadcast_to([HM, DB, DS]), ALU.subtract)
            v.tensor_copy(mout[:, 0:1], mt[:, SEQ - 1:SEQ])
            v.tensor_copy(mout[:, 1:1 + DB], mt[:, SEQ:T].rearrange("p (b q) -> p b q", b=DB)[:, :, DS - 1])
            step(v.tensor_tensor_scan(ncf[:, :], keep[:, :], lff[:, :], 0.0, ALU.mult, ALU.add))
            v.tensor_scalar(ncf[:, :], ncf[:, :], -1.0, None, ALU.mult).then_inc(S["rows_ready"], 1)

            dve.wait_ge(S["lg_in"], 32)
            for half in range(2):
                for h in range(HF):
                    last = v.tensor_tensor_scan(lg[:, half, h, :], ones, lg[:, half, h, :], 0.0, ALU.mult, ALU.add)
            last.then_inc(S["page_step"], 1)
            dve.wait_ge(S["page_step"], 1)
            v.tensor_copy(pgs[:, :, :], lg[:, :, :, PAGE - 1]).then_inc(S["page_step"], 1)
            dve.wait_ge(S["tile_evac"], KM + HM)
            v.tensor_scalar(PT[:, KM:KM + HM, :], PT[:, KM:KM + HM, :], DM ** -0.5, None, ALU.mult)\
                .then_inc(S["qk_scaled"], 1)
            dve.wait_ge(S["tile_evac"], QF + NJ)
            v.tensor_scalar(PT[:, QF:QF + NJ, :], PT[:, QF:QF + NJ, :], DF ** -0.5, None, ALU.mult)\
                .then_inc(S["qk_scaled"], 1)
            dve.wait_ge(S["qk_scaled"], 2)
            v.tensor_copy(qf_new[:, :, :], PT[:, QF:QF + NJ, SEQ:T]).then_inc(S["new_copied"], 1)
            dve.wait_ge(S["tile_evac"], KF + NJ)
            v.tensor_copy(kf_new[:, :, :], PT[:, KF:KF + NJ, SEQ:T]).then_inc(S["new_copied"], 1)
            dve.wait_ge(S["page_sum"], 1)
            for half in range(2):
                last = v.scalar_tensor_tensor(
                    out=lg[:, half], in0=lg[:, half], scalar=-1.0,
                    in1=PS[:, 5, half * HF:(half + 1) * HF].unsqueeze(2).broadcast_to([P, HF, PAGE]),
                    op0=ALU.mult, op1=ALU.add)
            last.then_inc(S["page_done"], 1)

            dve.wait_ge(S["rows_act"], 1)
            for n in range(0, 3 * (ST + 1), 2):
                rows = P if n % (ST + 1) < ST else NS
                dst = (knat, vnat, fnat)[n // (ST + 1)]
                dve.wait_ge(S["nat_done"], n + 1)
                v.tensor_copy(dst[0:rows, n % (ST + 1), :], PS[0:rows, n % 4, :]).then_inc(S["nat_out_v"], 1)
            dve.wait_ge(S["cat_done"], 1)
            R = ROWS_F + HM
            v.tensor_copy(cat[:, 0:ST, :], PS[:, 4, 0:ST * R].rearrange("p (i r) -> p i r", i=ST))
            v.tensor_copy(cat[0:NS, ST, :], PS[0:NS, 4, ST * R:(ST + 1) * R]).then_inc(S["cat_evac"], 1)
            v.tensor_copy(decb[:, :, :], PS[:, 5, 32:32 + HM * DB].rearrange("p (h b) -> p h b", h=HM))
            v.tensor_tensor(bias_new[:, :, :], new_mask[0:NS],
                            PS[0:NS, 5, 64:64 + NS].unsqueeze(1).broadcast_to([NS, DB, NS]), ALU.add)\
                .then_inc(S["cat_evac"], 1)
            dve.wait_ge(S["cat_evac"], 2)
            dve.wait_ge(S["nat_out_v"], 8)
            dve.wait_ge(S["nat_out_s"], 7)
            dve.wait_ge(S["state_in"], 16)
            dve.wait_ge(S["sig_ready"], 1)
            mdv = [0]

            def mstep(ins):
                mdv[0] += 1
                ins.then_inc(S["mdv"], 1)
                dve.wait_ge(S["mdv"], mdv[0])

            def weigh(h, i):
                n = h * (ST + 1) + i
                rows, w = (P, SEQ - i * P) if i < ST else (NS, NS)
                dve.wait_ge(S["me_ready"], n + 1)
                dve.wait_ge(S["ms_done"], n + 1)
                if n >= 2:
                    dve.wait_ge(S["mnd_done"], n - 1)
                v.tensor_tensor(mstt[0:rows, n % 2, 0:w], PS[0:rows, 4 + n % 2, 0:w], me[0:rows, n % 2, 0:w],
                                ALU.mult).then_inc(S["mst_ready"], 1)

            def states(h):
                v.tensor_tensor(ctm[:, h], ctm[:, h], decb[:, h, :].unsqueeze(2).broadcast_to([P, DB, P]), ALU.mult)
                mstep(v.tensor_tensor(nnew[:, h, :], nst[:, h, :], decb[:, h, :], ALU.mult))
                dve.wait_ge(S["ct_done"], 2 * h + 2)
                c2 = ctm[:, h].rearrange("p (a b) v -> p a (b v)", a=2)
                v.tensor_tensor(c2, PS[:, 2:4, :], c2, ALU.add)
                dve.wait_ge(S["ctp_out"], h + 1)
                v.tensor_tensor(nnew[:, h, :], ctp[:, h, DM + 1:], nnew[:, h, :], ALU.add)\
                    .then_inc(S["ct_out"], 1)

            for h in range(HM):
                dve.wait_ge(S["mb_evac"], 2 * (h + 1))
                for i in range(ST + 1):
                    n = h * (ST + 1) + i
                    rows, w = (P, P) if i < ST else (NS, NS)
                    if n >= 2:
                        dve.wait_ge(S["me_ready"], n - 1)
                    v.tensor_tensor(gm[0:rows, n % 2, 0:w], nmb[0:rows, i * P:i * P + w],
                                    causal_t if i < ST else causal_s[0:NS, :], ALU.add)\
                        .then_inc(S["mg_ready"], 1)
                    if i >= 1:
                        weigh(h, i - 1)
                weigh(h, ST)
                if h:
                    states(h - 1)
                dve.wait_ge(S["mint_done"], h + 1)
                if h == 0:
                    dve.wait_ge(S["bias_out"], 8 * 16)
                    dve.wait_ge(S["out_dma"], 16 * 4)
                v.tensor_tensor(ts1, PS[:, 0, TH + NS:TH + 2 * NS], wib[:, h % 2, :], ALU.mult)
                carried = (rden if h else den)[:, SEQ:T]
                mstep(v.tensor_tensor(carried, PS[0:HM, 1, TH + 2 * NS:TH + 3 * NS], winter[:, :], ALU.mult))
                if h:
                    mstep(v.tensor_tensor(den[:, SEQ:T], den[:, SEQ:T], carried, ALU.add))
                mstep(v.tensor_tensor(den[:, SEQ:T], PS[0:HM, 1, TH + NS:TH + 2 * NS], den[:, SEQ:T], ALU.add))
                v.tensor_tensor(mixT[:, h, SEQ:T], PS[:, 0, TH:TH + NS], ts1, ALU.add).then_inc(S["hn_ready"], 1)
            states(HM - 1)
            dve.wait_ge(S["den_abs"], 2)
            mstep(v.tensor_tensor(den, den, emt[:, :], ALU.max))
            mstep(v.reciprocal(rden, den))
            mstep(v.tensor_tensor(rnorm, rden, rden, ALU.mult))
            dve.wait_ge(S["mss_done"], 1)
            v.tensor_tensor(halves(rnorm), PS[0:HM, 5:7, 0:TH], halves(rnorm), ALU.mult).then_inc(S["ms2_ready"], 1)
            dve.wait_ge(S["mroot"], 1)
            mstep(v.reciprocal(rnorm, rnorm))
            v.tensor_tensor(rnorm, rnorm, rden, ALU.mult).then_inc(S["mf_ready"], 1)
            for h in range(HM):
                dve.wait_ge(S["gated"], h + 1)
                dve.wait_ge(S["mf_done"], h + 1)
                v.scalar_tensor_tensor(out=halves(mixT[:, h, :]), in0=halves(mixT[:, h, :]),
                                       scalar=gains[:, 3 * KT + h:3 * KT + h + 1], in1=pair((5, 2)[h % 2]),
                                       op0=ALU.mult, op1=ALU.mult)\
                    .then_inc(S["mmix"], 1)
            dve.wait_ge(S["mnd_done"], HM * (ST + 1))
            dve.wait_ge(S["ct_done"], 2 * HM)

            v.tensor_copy(vf_new[:, :], fnat[0:NS, ST, :]).then_inc(S["new_copied"], 1)
            fd = [0]

            def fstep(ins):
                fd[0] += 1
                ins.then_inc(S["f_dve"], 1)
                dve.wait_ge(S["f_dve"], fd[0])

            for h in range(HF):
                dve.wait_ge(S["fb_evac"], h + 1)
                fstep(v.tensor_tensor(ncm[:, :, :], ncb.rearrange("p (i s) -> p i s", i=ST),
                                      causal_n.unsqueeze(1).broadcast_to([P, ST, P]), ALU.add))
                for i in range(ST):
                    lo = i * P
                    dve.wait_ge(S["fs_done"], h * ST + i + 1)
                    if h:
                        dve.wait_ge(S["f_exp"], (h - 1) * ST + i + 1)
                    fstep(v.tensor_tensor_reduce(scp[:, i, lo:lo + P], PS[:, 1 + i, lo:lo + P], ncm[:, i, :], 1.0,
                                                 NEG, ALU.add, ALU.max, fmx[:, 0, i:i + 1]))
                    if i:
                        fstep(v.tensor_tensor_reduce(scp[:, i, 0:lo], PS[:, 1 + i, 0:lo], ncb[:, 0:lo], 1.0,
                                                     NEG, ALU.add, ALU.max, fmx[:, 1, i:i + 1]))
                        fstep(v.tensor_tensor(fmx[:, 0, i:i + 1], fmx[:, 0, i:i + 1], fmx[:, 1, i:i + 1], ALU.max))
                    v.tensor_scalar(fmx[:, 2, i:i + 1], fmx[:, 0, i:i + 1], -1.0, None, ALU.mult)\
                        .then_inc(S["f_max"], 1)
                for i in range(ST):
                    dve.wait_ge(S["f_exp"], h * ST + i + 1)
                    fstep(v.reciprocal(fmx[:, 4, i:i + 1], fmx[:, 3, i:i + 1]))
                    v.tensor_scalar(pp[:, i, 0:(i + 1) * P], pp[:, i, 0:(i + 1) * P], fmx[:, 4, i:i + 1], None,
                                    ALU.mult).then_inc(S["f_pn"], 1)

            dve.wait_ge(S["new_copied"], 3)
            dve.wait_ge(S["fo_done"], HF * ST)
            dve.wait_ge(S["fo_evac"], HF)
            dve.wait_ge(S["out_dma"], 16 * OUT_EARLY)

            dve.wait_ge(S["vh_ready"], 1)
            v.tensor_tensor(vn_lo[0:NS, :], vf_new[:, :], vn_hi[0:NS, :].bitcast(F32), ALU.subtract)\
                .then_inc(S["vn_ready"], 1)

            def score(b, par, c):
                n = NS if c == NCH else PC * PAGE
                chunk = scores[0:NS, c * 512:c * 512 + n]
                if c == 0:
                    dve.wait_ge(bias_in[par], (b - par) * (8 * HF) + 16 * HF)
                dve.wait_ge(S["sc_done"], b * CH + c + 1)
                if not (isinstance(b, int) and b == 0):
                    dve.wait_ge(S["p_ready"], (b - 1) * CH + c + 1)
                if c < NCH:
                    hold_here(dve)
                    v.tensor_tensor_reduce(chunk, PS[0:NS, c % 3, 0:n], bias[par][0:NS, c * 512:c * 512 + n],
                                           1.0, NEG, ALU.add, ALU.max, smx[:, c:c + 1])\
                        .then_inc(S["sc_evac"], 1)
                else:
                    nb = bias_new[:, bass.ds(b, 1), :].rearrange("p a k -> p (a k)")
                    v.tensor_tensor(chunk, PS[0:NS, c % 3, 0:n], nb, ALU.add).then_inc(S["sc_evac"], 1)

            def low_values(b, c):
                for g in (0, 2):
                    dve.wait_ge(S["vh_ready"], b * (2 * NCH) + (2 * c + g // 2 + 2))
                    v.tensor_tensor(v_lo[c % 4][:, g:g + 2, :], vring[c % 4][:, g:g + 2, :],
                                    v_hi[c % 2][:, g:g + 2, :].bitcast(F32), ALU.subtract)\
                        .then_inc(S["vl_ready"], 1)

            def low_probs(b, c):
                rows, g = (P, PC) if c < NCH else (NS, 1)
                dve.wait_ge(S["ph_ready"], b * CH + c + 1)
                v.tensor_tensor(p_t[c % 3][0:rows, 0:g, NS:2 * NS],
                                PS[0:rows, 3 + c % 3, 0:g * NS].rearrange("p (g c) -> p g c", g=g),
                                p_t[c % 3][0:rows, 0:g, 0:NS].bitcast(F32), ALU.subtract)\
                    .then_inc(S["pl_ready"], 1)

            def sample(b, par, qk, pv, ot):
                for c in range(CH):
                    if qk:
                        score(b, par, c)
                    if pv and c >= 1:
                        low_probs(b - 1, c - 1)
                    if pv and c < NCH:
                        low_values(b - 1, c)
                    if ot and c == 2:
                        dve.wait_ge(S["ot_done"], b - 1)
                        for p2 in range(2):
                            rows = slice(p2 * DF, p2 * DF + DF)
                            src = stepped(PS[rows, 7, 0:NJ * NS], p2 * DS, [[NS + 2 * DS, NJ], [1, DS]])
                            v.tensor_copy(mixT[rows, NJ:2 * NJ, bass.ds((b - 2) * DS + SEQ, DS)], src)\
                                .then_inc(S["ot_evac"], 1)
                if qk:
                    dve.wait_ge(S["sc_evac"], (b + 1) * CH)
                    v.tensor_reduce(smx[:, NCH:CH], scores[0:NS, PAST:PAST + NS], AX.X, ALU.max)\
                        .then_inc(S["max_step"], 1)
                    dve.wait_ge(S["max_step"], b * 2 + 1)
                    v.tensor_reduce(snm[:, 0:1], smx[:, :], AX.X, ALU.max).then_inc(S["max_step"], 1)
                    dve.wait_ge(S["max_step"], b * 2 + 2)
                    v.tensor_scalar(snm[:, 1:2], snm[:, 0:1], -1.0, None, ALU.mult).then_inc(S["mx_ready"], 1)
                if pv:
                    low_probs(b - 1, NCH)
                    dve.wait_ge(S["p_ready"], b * CH)
                    v.tensor_reduce(sri[0:NS, 0:1], ssum[:, :], AX.X, ALU.add).then_inc(S["sum_read"], 1)
                    dve.wait_ge(S["sum_read"], b)
                    v.reciprocal(sri[0:NS, 1:2], sri[0:NS, 0:1])
                    v.reciprocal(sri[NS:2 * NS, 1:2], sri[0:NS, 0:1]).then_inc(S["sum_ready"], 1)
                    dve.wait_ge(S["sum_ready"], b)
                    dve.wait_ge(S["pv_done"], b * CH)
                    if ot:
                        dve.wait_ge(S["ot_done"], b - 1)
                    v.tensor_scalar(osb[:, :], PS[:, 6, :], sri[:, 1:2], None, ALU.mult)\
                        .then_inc(S["o_ready"], 1)

            sample(0, 0, True, False, False)
            sample(1, 1, True, True, False)
            with dve.Fori(1, DB // 2) as i:
                sample(2 * i, 0, True, True, True)
                sample(2 * i + 1, 1, True, True, True)
            sample(DB, 0, False, True, True)

            def mixed_lows(tiles):
                for kt in tiles:
                    dve.wait_ge(S["nhi_ready"], KT + kt + 1)
                    v.tensor_tensor(h_lo[:, kt, :], mixT[:, kt, :], h_hi[:, kt, :].bitcast(F32), ALU.subtract)\
                        .then_inc(S["mixed"], 1)

            mixed_lows(range(HM))
            sample(DB + 1, 0, False, False, True)
            dve.wait_ge(S["ot_evac"], 2 * DB)

            mixed_lows(range(HM, KT))

            def residual(u0, evacuated, squares=None):
                with dve.Fori(0, KT // 2) as i:
                    for t in range(2):
                        dve.wait_ge(S["unit_done"], i * 2 + (u0 + t + 1))
                        dst = xT[:, bass.ds(i * 2 + t, 1), :].rearrange("p a (g t) -> p (a g) t", g=2)
                        v.tensor_tensor(dst, pair(2 * t), dst, ALU.add).then_inc(S["tile_evac"], 1)
                        if squares is not None:
                            dve.wait_ge(S["tile_evac"], i * 2 + (evacuated + t + 1))
                            square(i * 2 + t, i * 2 + (squares * KT + t), t)

            dve.wait_ge(S["x_again"], 16)
            residual(U0_OUT, U0_OUT, squares=1)
            dve.wait_ge(S["tile_evac"], U0_FF)
            norm(1, 2 * KT)
            u0, f0 = U0_FF, 0
            for r, n in enumerate(ROUNDS):
                with dve.Fori(0, n // 2) as i:
                    for t in range(2):
                        m = i * 2 + t
                        dve.wait_ge(S["unit_done"], m + (u0 + 1))
                        dve.wait_ge(S["silu_done"], m + (f0 + 1))
                        v.tensor_tensor(halves(stage[:, t, :]), pair(4 * t + 2), halves(stage[:, t, :]), ALU.mult)\
                            .then_inc(S["act_ready"], 1)
                        dve.wait_ge(S["act_hi_done"], m + (f0 + 1))
                        v.tensor_tensor(act_lo[:, bass.ds(m, 1), :].rearrange("p a t -> p (a t)"), stage[:, t, :],
                                        act_hi[:, bass.ds(m, 1), :].rearrange("p a t -> p (a t)").bitcast(F32),
                                        ALU.subtract).then_inc(S["act_done"], 1)
                residual(u0 + n, U0_FF + r * KT, squares=2 if n == ROUNDS[-1] else None)
                u0 += n + KT
                f0 += n
            dve.wait_ge(S["tile_evac"], U0_FF + 2 * KT)
            norm(2, 3 * KT)

        @blk.tensor
        def _(pe):
            mm = nc.tensor.matmul

            def ssq(n, kt, t):
                pe.wait_ge(S["sq_ready"], kt + (n * KT + 1))
                for g in range(2):
                    last = mm(PS[:, 4 + g, 0:TH], ones, stage[:, t, g * TH:(g + 1) * TH],
                              start=(isinstance(kt, int) and kt == 0), stop=(isinstance(kt, int) and kt == KT - 1))
                last.then_inc(S["sq_used"], 1)

            def product_step(bk, hi, lo, x_hi, x_lo, kt, kts):
                for n, (w, x) in enumerate(((hi, x_hi), (hi, x_lo), (lo, x_hi))):
                    for g in range(2):
                        last = mm(PS[:, bk + g, 0:TH], w(kt), x[:, kt, g * TH:(g + 1) * TH],
                                  start=(kt == 0 and n == 0), stop=(kt == kts - 1 and n == 2))
                return last

            def product(bk, hi, lo, x_hi, x_lo, kts):
                for kt in range(kts):
                    last = product_step(bk, hi, lo, x_hi, x_lo, kt, kts)
                return last

            def weight_tile(ring, s, n, kts):
                w = ring[s][:, n * kts * P:(n + 1) * kts * P].rearrange("p (k c) -> p k c", k=kts)
                return lambda kt: w[:, kt, :]

            pe.wait_ge(S["wide_in"], 16)
            for kt in range(KT):
                ssq(0, kt, kt % 2)
            pe.wait_ge(S["const_in"], 2 * 16)
            pe.wait_ge(S["small_in"], 5 * 16)
            for kt in range(KT + 2):
                if kt < KT:
                    pe.wait_ge(S["nh_ready"], kt + 1)
                    for g in range(2):
                        last = mm(PS[0:GR, 6 + g, 0:TH], wg[:, kt, :], sq[:, kt % 2, g * TH:(g + 1) * TH],
                                  start=(kt == 0), stop=(kt == KT - 1))
                    last.then_inc(S["wg_used"], 1)
                if kt >= 2:
                    if kt == 2:
                        pe.wait_ge(S["wl_ready"], 2)
                    pe.wait_ge(S["h_ready"], kt - 1)
                    for t in range(2):
                        last = product_step(2 * t, weight_tile(w_hi_in, t, 0, KT), weight_tile(w_lo_in, t, 0, KT),
                                            h_hi, h_lo, kt - 2, KT)
                        if kt - 2 == KT - 1:
                            last.then_inc(S["unit_done"], 1)

            def projected(i, first=False):
                for t in range(2 if first else 0, 4):
                    u = i * 4 + t
                    pe.wait_ge(S["wl_ready"], u + 1)
                    if not first:
                        pe.wait_ge(S["tile_evac"], u - 3)
                    elif t == 3:
                        pe.wait_ge(S["gate_evac"], 1)
                    product(2 * t, weight_tile(w_hi_in, t % 2, 0, KT), weight_tile(w_lo_in, t % 2, 0, KT),
                            h_hi, h_lo, KT).then_inc(S["unit_done"], 1)

            projected(0, True)
            with pe.Fori(1, NT_IN // 4) as i:
                projected(i)

            pe.wait_ge(S["tile_evac"], NT_IN)
            pe.wait_ge(S["page_step"], 2)
            mm(PS[:, 5, 0:2 * HF], suffix, pgs[:, :, :].rearrange("p a h -> p (a h)"), start=True, stop=True)\
                .then_inc(S["page_sum"], 1)
            pe.wait_ge(S["qk_scaled"], 2)
            for n in range(3 * (ST + 1)):
                t0, i = (KM, VM, VF)[n // (ST + 1)], n % (ST + 1)
                w = P if i < ST else NS
                if n >= 4:
                    pe.wait_ge(S[("nat_out_v", "nat_out_s")[n % 2]], n // 2 - 1)
                for c in range(4):
                    last = nc.tensor.transpose(PS[0:w, n % 4, c * P:(c + 1) * P], PT[:, t0 + c, i * P:i * P + w],
                                               ident)
                last.then_inc(S["nat_done"], 1)
            R = ROWS_F + HM
            pe.wait_ge(S["rows_act"], 1)
            pe.wait_ge(S["rows_ready"], 1)
            for i in range(ST + 1):
                w = P if i < ST else NS
                nc.tensor.transpose(PS[0:w, 4, i * R:(i + 1) * R], ca[:, i * P:i * P + w], ident[0:R, 0:R])
            pe.wait_ge(S["page_done"], 1)
            for h in range(HM):
                mm(PS[:, 5, 32 + h * DB:32 + (h + 1) * DB], sel4[:, h * P:(h + 1) * P], dec[:, :],
                   start=True, stop=True)
            mm(PS[0:NS, 5, 64:64 + NS], selq, ncf[:, SEQ:T], start=True, stop=True).then_inc(S["cat_done"], 1)

            pe.wait_ge(S["cat_evac"], 2)
            pe.wait_ge(S["nat_out_v"], 8)
            pe.wait_ge(S["nat_out_s"], 7)
            pe.wait_ge(S["state_in"], 16)
            def head_rows(h):
                hc = slice(h * P, (h + 1) * P)
                for g in range(2):
                    mm(PS[:, g, 0:TH], sel4[:, hc], m_top[:, g * TH:(g + 1) * TH], start=True, stop=True)
                mm(PS[:, 1, TH:TH + NS], sel4[:, hc], winter[:, :], start=True, stop=True)\
                    .then_inc(S["mb_done"], 1)

            def logits(h, i):
                n = h * (ST + 1) + i
                if n >= 2:
                    pe.wait_ge(S["mst_ready"], n - 1)
                if h and i == 0:
                    pe.wait_ge(S["ctp_out"], h)
                rows = P if i < ST else NS
                end = SEQ if i < ST else T
                mm(PS[0:rows, 4 + n % 2, 0:end - i * P], PT[:, KM + h, i * P:i * P + rows],
                   PT[:, QM + h, i * P:end], start=True, stop=True).then_inc(S["ms_done"], 1)

            def outputs(h, i):
                n, hc, row = h * (ST + 1) + i, slice(h * P, (h + 1) * P), one_at[:, HM - 1 - h:2 * HM - 1 - h]
                pe.wait_ge(S["mst_ready"], n + 1)
                if h and i == 0:
                    pe.wait_ge(S["num_out"], h)
                    pe.wait_ge(S["hn_ready"], h)
                if i < ST:
                    mm(PS[:, 6, i * P:SEQ], vnat[:, i, hc], mstt[:, n % 2, 0:SEQ - i * P],
                       start=(i == 0), stop=(i == ST - 1))
                    mm(PS[0:HM, 7, i * P:SEQ], row, mstt[:, n % 2, 0:SEQ - i * P],
                       start=(h == 0 and i == 0), stop=(h == HM - 1 and i == ST - 1)).then_inc(S["mnd_done"], 1)
                else:
                    mm(PS[:, 0, TH:TH + NS], vnat[0:NS, ST, hc], mstt[0:NS, n % 2, 0:NS], start=True, stop=True)
                    mm(PS[0:HM, 1, TH + NS:TH + 2 * NS], row[0:NS, :], mstt[0:NS, n % 2, 0:NS],
                       start=True, stop=True).then_inc(S["mnd_done"], 1)

            head_rows(0)
            for h in range(HM):
                hc = slice(h * P, (h + 1) * P)
                logits(h, 0)
                logits(h, 1)
                for i in range(ST + 1):
                    if i >= 2:
                        logits(h, i)
                    if i >= 1:
                        outputs(h, i - 1)
                pe.wait_ge(S["mb_evac"], 2 * h + 2)
                outputs(h, ST)
                if h + 1 < HM:
                    head_rows(h + 1)
                    pe.wait_ge(S["mb_evac"], 2 * h + 4)
                pe.wait_ge(S["nq_ready"], h + 1)
                for b in range(DB):
                    mm(PS[:, 0, TH + NS + b * DS:TH + NS + (b + 1) * DS], ctm[:, h, b, :],
                       PT[:, QM + h, SEQ + b * DS:SEQ + (b + 1) * DS], start=True, stop=True)
                mm(PS[0:HM, 1, TH + 2 * NS:TH + 3 * NS], one_at[:, HM - 1 - h:2 * HM - 1 - h], nq,
                   start=True, stop=True).then_inc(S["mint_done"], 1)
                pe.wait_ge(S["vw_ready"], h + 1)
                for i in range(ST):
                    mm(PS[:, 4, 0:P + 1], knat[:, i, hc], vw[:, i, :], start=(i == 0), stop=(i == ST - 1))
                mm(PS[:, 4, P + 1:P + 1 + DB], knat[0:NS, ST, hc], wm[0:NS, :], start=True, stop=True)\
                    .then_inc(S["ct_done"], 1)
                if h:
                    pe.wait_ge(S["ct_out"], h)
                for g in range(2):
                    last = mm(PS[:, 2 + g, :], knat[0:NS, ST, hc],
                              vmk[0:NS, 4 * g:4 * g + 4, :].rearrange("p b v -> p (b v)"), start=True, stop=True)
                last.then_inc(S["ct_done"], 1)
            pe.wait_ge(S["num_out"], HM)
            for h in range(HM):
                pe.wait_ge(S["squared"], h + 1)
                for g in range(2):
                    last = mm(PS[0:HM, 5 + g, 0:TH], one_at[:, HM - 1 - h:2 * HM - 1 - h],
                              hs[:, h, g * TH:(g + 1) * TH], start=(h == 0), stop=(h == HM - 1))
            last.then_inc(S["mss_done"], 1)
            pe.wait_ge(S["mf_ready"], 1)
            pe.wait_ge(S["ct_out"], HM)
            for h in range(HM):
                if h >= 2:
                    pe.wait_ge(S["mmix"], h - 1)
                for g in range(2):
                    last = mm(PS[:, (5, 2)[h % 2] + g, 0:TH], sel4[:, h * P:(h + 1) * P],
                              rnorm[:, g * TH:(g + 1) * TH], start=True, stop=True)
                last.then_inc(S["mf_done"], 1)

            pe.wait_ge(S["mmix"], HM)

            def fox_scores(h):
                rows = slice((h % 2) * DF, (h % 2) * DF + DF)
                if h:
                    pe.wait_ge(S["fb_evac"], h)
                mm(PS[:, 0, :], sel8[:, h * P:(h + 1) * P], ncf[:, 0:SEQ], start=True, stop=True)\
                    .then_inc(S["fb_done"], 1)
                for i in range(ST):
                    if h:
                        pe.wait_ge(S["f_max"], (h - 1) * ST + i + 1)
                    mm(PS[:, 1 + i, 0:(i + 1) * P], PT[rows, QF + h // 2, i * P:(i + 1) * P],
                       PT[rows, KF + h // 2, 0:(i + 1) * P], start=True, stop=True).then_inc(S["fs_done"], 1)

            def fox_outputs(h):
                def turn(j):
                    n = h * ST + j
                    if n >= 2:
                        pe.wait_ge(S["ft_evac"], n - 1)
                    for t in range(j, ST):
                        last = nc.tensor.transpose(PS[:, 5 + j % 2, t * P:(t + 1) * P], pp[:, t, j * P:(j + 1) * P],
                                                   ident)
                    last.then_inc(S["ft_done"], 1)

                def weigh_values(j):
                    pe.wait_ge(S["ft_evac"], h * ST + j + 1)
                    mm(PS[0:DF, 7, j * P:SEQ], fnat[:, j, h * DF:(h + 1) * DF], pts[:, j % 2, j * P:SEQ],
                       start=(j == 0), stop=(j == ST - 1)).then_inc(S["fo_done"], 1)

                pe.wait_ge(S["f_pn"], (h + 1) * ST)
                turn(0)
                turn(1)
                if h:
                    pe.wait_ge(S["fo_evac"], h)
                weigh_values(0)
                turn(2)
                weigh_values(1)
                turn(3)
                weigh_values(2)
                weigh_values(3)

            fox_scores(0)
            for h in range(HF):
                if h + 1 < HF:
                    fox_scores(h + 1)
                fox_outputs(h)

            pe.wait_ge(S["f_max"], HF * ST)
            pe.wait_ge(S["new_copied"], 3)

            def keys_by_queries(b, par, c):
                if c == 0:
                    pe.wait_ge(S["q_ready"], 2 * b + 2)
                if c < NCH:
                    if isinstance(b, int) and b == 0:
                        pe.wait_ge(k_first[c % 4], 8 * PC * (c // 4 + 1))
                        pe.wait_ge(k_in[c % 4], 8 * PC * (c // 4 + 1))
                    else:
                        pe.wait_ge(k_in[c % 4], 16 * PC * (2 * b + c // 4))
                if not (isinstance(b, int) and b == 0 and c < 3):
                    pe.wait_ge(S["sc_evac"], b * CH + c - 2)
                w = PC * PAGE if c < NCH else NS
                for j in range(NJ):
                    keys = kring[c % 4][:, :, j, :] if c < NCH else kf_new[:, j, :]
                    last = mm(PS[0:NS, c % 3, 0:w], qbd[:, par, j, :], keys, start=(j == 0), stop=(j == NJ - 1))
                last.then_inc(S["sc_done"], 1)

            def turn_probs(b, c):
                pe.wait_ge(S["p_ready"], b * CH + c + 1)
                if not (isinstance(b, int) and b == 0 and c < 3):
                    pe.wait_ge(S["pl_ready"], b * CH + c - 2)
                hold_here(pe)
                for g in range(PC if c < NCH else 1):
                    w = P if c < NCH else NS
                    last = nc.tensor.transpose(PS[0:w, 3 + c % 3, g * NS:(g + 1) * NS],
                                               probs[0:NS, c % 3, g * P:g * P + w], ident[0:NS, 0:NS])
                last.then_inc(S["pt_done"], 1)

            def values(b, c):
                pe.wait_ge(S["pl_ready"], b * CH + c + 1)
                if c == 0 and not (isinstance(b, int) and b == 0):
                    pe.wait_ge(S["o_ready"], b)
                if c < NCH:
                    for g in range(PC):
                        if g % 2 == 0:
                            pe.wait_ge(S["vl_ready"], b * (2 * NCH) + (2 * c + g // 2 + 1))
                        mm(PS[:, 6, :], p_t[c % 3][:, g, :], v_hi[c % 2][:, g, :],
                           start=(c == 0 and g == 0), stop=False)
                        last = mm(PS[:, 6, :], p_t[c % 3][:, g, :], v_lo[c % 4][:, g, :], start=False, stop=False)
                else:
                    mm(PS[:, 6, :], p_t[c % 3][0:NS, 0, :], vn_hi[0:NS, :], start=False, stop=False)
                    last = mm(PS[:, 6, :], p_t[c % 3][0:NS, 0, :], vn_lo[0:NS, :], start=False, stop=True)
                last.then_inc(S["pv_done"], 1)

            def turn_out(b):
                pe.wait_ge(S["o_ready"], b + 1)
                if not (isinstance(b, int) and b == 0):
                    pe.wait_ge(S["ot_evac"], 2 * b)
                for j in range(NJ):
                    last = mm(PS[:, 7, j * NS:(j + 1) * NS], osb[:, j * P:(j + 1) * P], fold, start=True, stop=True)
                last.then_inc(S["ot_done"], 1)

            def sample(b, par, qk, pv, ot):
                for c in range(CH + 2):
                    if qk and c < CH:
                        keys_by_queries(b, par, c)
                    if ot and c == 1:
                        turn_out(b - 2)
                    if pv and 1 <= c <= CH:
                        turn_probs(b - 1, c - 1)
                    if pv and c >= 2:
                        values(b - 1, c - 2)

            sample(0, 0, True, False, False)
            pe.wait_ge(S["vn_ready"], 1)
            pe.wait_ge(S["fo_evac"], HF)
            sample(1, 1, True, True, False)
            with pe.Fori(1, DB // 2) as i:
                sample(2 * i, 0, True, True, True)
                sample(2 * i + 1, 1, True, True, True)
            sample(DB, 0, False, True, True)
            turn_out(DB - 1)

            pe.wait_ge(S["ot_evac"], 2 * DB)

            def model_tiles(u0, evacuated, x_hi, x_lo, kts, x_ready, x_before, squares=None):
                def two(i):
                    for s in range(2):
                        pe.wait_ge(S["wl_ready"], i * 2 + (u0 + s + 1))
                        pe.wait_ge(S["tile_evac"], i * 2 + (evacuated + s - 1))
                        for kt in range(kts):
                            if isinstance(i, int) and s == 0:
                                pe.wait_ge(S[x_ready], x_before + kt + 1)
                            last = product_step(2 * s, weight_tile(w_hi, s, 0, kts), weight_tile(w_lo, s, 0, kts),
                                                x_hi, x_lo, kt, kts)
                        last.then_inc(S["unit_done"], 1)
                        if squares is not None and not (isinstance(i, int) and s == 0):
                            ssq(squares, i * 2 + (s - 1), 1 - s)

                two(0)
                with pe.Fori(1, KT // 2) as i:
                    two(i)
                if squares is not None:
                    ssq(squares, KT - 1, 1)

            model_tiles(U0_OUT, U0_OUT, h_hi, h_lo, KT, "mixed", 0, squares=1)
            u0, f0, down0 = U0_FF, 0, U0_FF
            for n in ROUNDS:
                def hidden(i, u0=u0, f0=f0):
                    for s in range(2):
                        first = f0 == 0 and isinstance(i, int)
                        pe.wait_ge(S["wl_ready"], i * 2 + (u0 + s + 1))
                        if not first:
                            pe.wait_ge(S["act_ready"], i * 2 + (f0 + s - 1))
                        for kt in range(KT):
                            if first and s == 0:
                                pe.wait_ge(S["h_ready"], KT + kt + 1)
                            for t in range(2):
                                last = product_step(4 * s + 2 * t, weight_tile(w_hi, s, t, KT),
                                                    weight_tile(w_lo, s, t, KT), h_hi, h_lo, kt, KT)
                                if kt == KT - 1:
                                    last.then_inc(S[("gate_done", "unit_done")[t]], 1)

                pe.wait_ge(S["tile_evac"], down0)
                hidden(0)
                with pe.Fori(1, n // 2) as i:
                    hidden(i)
                pe.wait_ge(S["act_ready"], f0 + n - 1)
                model_tiles(u0 + n, down0, act_hi, act_lo, n, "act_done", f0, squares=2 if n == ROUNDS[-1] else None)
                f0 += n
                u0 += n + KT
                down0 += KT


def kernel(**inputs):
    import concourse.bacc as bacc
    from concourse.bass_utils import run_bass_kernel_spmd

    f = {k: np.asarray(v) for k, v in inputs.items()}

    def tiles(w):
        return w.reshape(w.shape[0] // P, P, w.shape[1]).transpose(1, 0, 2)

    def units(w, width):
        k, n = w.shape
        return w.reshape(k // P, P, n // width, width).transpose(2, 1, 0, 3).reshape(n // width, P, -1)

    w_in = f["w_in"][0]
    g0, f0 = 4 * HM * DM, 4 * HM * DM + 2 * HM
    wgate = np.zeros((D, GR), np.float32)
    wgate[:, 0:HM] = w_in[:, g0:g0 + HM]
    wgate[:, ROWS_F:ROWS_F + HM] = w_in[:, g0 + HM:g0 + 2 * HM]
    wgate[:, ROWS_FF:ROWS_FF + HF] = w_in[:, f0 + 3 * HF * DF:]
    gbias = np.zeros((GR, 1), np.float32)
    gbias[0:HM, 0] = f["b_m_igate"][0]
    gbias[ROWS_F:ROWS_F + HM, 0] = f["b_m_fgate"][0]
    gbias[ROWS_FF:, 0] = f["b_f_fgate"][0]
    cols = np.concatenate([w_in[:, :g0], w_in[:, f0:f0 + 3 * HF * DF]], axis=1)
    wide, rows = constants()
    gate_up = np.concatenate([units(f["w_gate"][0], P), units(f["w_up"][0], P)], axis=2)
    x = np.concatenate([f["x_prompt"].reshape(SEQ, D), f["x_sample"].reshape(NS, D)], axis=0)
    pool_k, pool_v, pool_f = f["cache_fox_k"][0], f["cache_fox_v"][0], f["cache_fox_logf"][0]
    npool = pool_k.shape[0]
    table = f["page_table"].reshape(-1)
    arrays = {
        "x": x.T.reshape(KT, P, T).transpose(1, 0, 2),
        "wide": wide,
        "rows": rows,
        "gains": np.concatenate([f["norm_mix_g"].reshape(KT, P), f["norm_ffn_g"].reshape(KT, P),
                                 f["norm_final_g"].reshape(KT, P), f["mlstm_head_g"].reshape(HM, P)]).T,
        "wgate": tiles(wgate),
        "gbias": gbias,
        "win": units(cols, P),
        "wout": units(f["w_out"][0], P),
        "ptab": table.reshape(1, -1),
        "pidx": table.reshape(2, P).T,
        "m": f["state_mlstm_m"][0].T,
        "n": f["state_mlstm_n"][0].transpose(2, 1, 0),
        "C": f["state_mlstm_C"][0].transpose(3, 1, 0, 2),
        "K": pool_k.reshape(npool, PAGE, NJ, 2 * DF).transpose(0, 3, 2, 1).reshape(npool, P, NJ * PAGE),
        "V": pool_v.reshape(npool, PAGE, HF * DF),
        "logf": pool_f.transpose(0, 2, 1).reshape(npool, HF * PAGE),
    }
    first = 0
    for r, n in enumerate(ROUNDS):
        arrays[f"wgu{r}"] = gate_up[first:first + n]
        arrays[f"wdown{r}"] = units(f["w_down"][0][first * P:(first + n) * P], P)
        first += n
    outs = {
        "o_y": (P, KT, T), "o_kf": (P, NJ, T), "o_vf": (P, NJ, T), "o_logf": (HF, T), "o_m": (HM, 1 + DB),
        "o_C": (P, HM, DB, DM), "o_n": (P, HM, DB), "o_Cp": (P, HM, DM + 1),
    }
    nc = bacc.Bacc("TRN2", target_bir_lowering=False, num_devices=1)
    arrays = {k: np.ascontiguousarray(a) for k, a in arrays.items()}
    A = {k: nc.dram_tensor("in_" + k, a.shape, mybir.dt.from_np(a.dtype), kind="ExternalInput").ap()
         for k, a in arrays.items()}
    for k, s in outs.items():
        A[k] = nc.dram_tensor(k, s, F32, kind="ExternalOutput").ap()
    A["npool"] = npool
    build(nc, A)
    got = run_bass_kernel_spmd(nc, [{"in_" + k: a for k, a in arrays.items()}], core_ids=[0]).results[0]

    def tokens(a):
        a = a.transpose(2, 1, 0).reshape(T, -1)
        return a[:SEQ], a[SEQ:].reshape(DB, DS, -1)

    y, kf, vf = tokens(got["o_y"]), tokens(got["o_kf"]), tokens(got["o_vf"])
    lf = got["o_logf"].T
    m, n, c, cp = got["o_m"], got["o_n"], got["o_C"], got["o_Cp"]
    return (y[0].reshape(1, SEQ, D), y[1],
            kf[0].reshape(1, 1, SEQ, HF, DF), vf[0].reshape(1, 1, SEQ, HF, DF), lf[:SEQ].reshape(1, 1, SEQ, HF),
            cp[:, :, :DM].transpose(1, 2, 0).reshape(1, 1, HM, DM, DM), cp[:, :, DM].T.reshape(1, 1, HM, DM),
            m[:, 0].reshape(1, 1, HM),
            kf[1].reshape(1, DB, DS, HF, DF), vf[1].reshape(1, DB, DS, HF, DF),
            lf[SEQ:].reshape(1, DB, DS, HF),
            c.transpose(2, 1, 3, 0).reshape(1, DB, HM, DM, DM), n.transpose(2, 1, 0).reshape(1, DB, HM, DM),
            m[:, 1:].T.reshape(1, DB, HM))
```
